# Optimizing a Trainium2 kernel written in Bass

```python
import functools
import jax, jax.numpy as jnp
from jax import lax
import numpy as np

D_MODEL = 1024
BATCH = 1
SEQ = 256
DEPTH = 2

GRID_W = 64
CTX_LEN = 256
HEAD_DIM = 64
A_Q_HEADS = 8
A_KV_HEADS = 2
B_Q_HEADS = 8
B_KV_HEADS = 2
C_HEADS = 16
Q_BLOCK = 128
WINDOW = 128
NA_ROWS = 8
NA_COLS = 16
ROPE_THETA = 10000.0
D_FF = 2816
N_EXPERTS = 8
TOP_K = 2
D_FF_EXPERT = 3584
N_MOD = 6
EPS = 1e-6
NEG_INF = -1e30
ATTN_SCALE = HEAD_DIM ** -0.5

kernel_name = 'hybrid_dit_prefix_block'

def rms_norm(x, g):
    xf = x.astype(jnp.float32)
    y = xf * lax.rsqrt(jnp.mean(xf * xf, axis=-1, keepdims=True) + EPS)
    return (y * g.astype(jnp.float32)).astype(x.dtype)

def modulate(x, g, shift, scale):
    return rms_norm(x, g) * (1 + scale) + shift

def heads(t, n):
    return t.reshape(t.shape[:-1] + (n, HEAD_DIM))

def group(q, n_kv):
    b, n, hq, dh = q.shape
    return q.reshape(b, n, n_kv, hq // n_kv, dh)

def axial_rope(n_tokens):
    t = jnp.arange(n_tokens, dtype=jnp.int32)
    row = (t // GRID_W).astype(jnp.float32)
    col = (t % GRID_W).astype(jnp.float32)
    half = HEAD_DIM // 2
    freqs = ROPE_THETA ** (-jnp.arange(0, half, 2, dtype=jnp.float32) / half)
    ang = jnp.concatenate([row[:, None] * freqs, col[:, None] * freqs], axis=-1)
    return jnp.cos(ang), jnp.sin(ang)

def apply_rope(x, cos, sin):
    xf = x.astype(jnp.float32).reshape(x.shape[:-1] + (HEAD_DIM // 2, 2))
    x1, x2 = xf[..., 0], xf[..., 1]
    c, s = cos[:, None, :], sin[:, None, :]
    out = jnp.stack([x1 * c - x2 * s, x1 * s + x2 * c], axis=-1)
    return out.reshape(x.shape).astype(x.dtype)

def softmax_with_sink(s, sink):
    m = jnp.maximum(jnp.max(s, axis=-1, keepdims=True), sink)
    e = jnp.exp(s - m)
    return e / (jnp.sum(e, axis=-1, keepdims=True) + jnp.exp(sink - m))

def context_attend(q, k, v, sink):
    b, n, hkv, g, dh = q.shape
    s = jnp.einsum('bqhgd,bkhd->bhgqk', q * ATTN_SCALE, k).astype(jnp.float32)
    p = jax.nn.softmax(s, axis=-1) if sink is None else softmax_with_sink(s, sink)
    o = jnp.einsum('bhgqk,bkhd->bqhgd', p.astype(v.dtype), v)
    return o.reshape(b, n, hkv * g * dh)

def global_gqa_latent(q, k_all, v_all):
    b, s, hkv, g, dh = q.shape
    nb = s // Q_BLOCK
    qb = jnp.moveaxis(q.reshape(b, nb, Q_BLOCK, hkv, g, dh), 1, 0) * ATTN_SCALE

    def one_block(q_blk):
        sc = jnp.einsum('bqhgd,bkhd->bhgqk', q_blk, k_all).astype(jnp.float32)
        p = jax.nn.softmax(sc, axis=-1).astype(v_all.dtype)
        return jnp.einsum('bhgqk,bkhd->bqhgd', p, v_all)

    o = lax.map(one_block, qb)
    return jnp.moveaxis(o, 0, 1).reshape(b, s, hkv * g * dh)

def window_gqa_latent(q, k, v, k_ctx, v_ctx, sink):
    b, s, hkv, g, dh = q.shape
    nb = s // Q_BLOCK
    nw = 3 * Q_BLOCK

    def band(t):
        tp = jnp.pad(t, ((0, 0), (Q_BLOCK, Q_BLOCK), (0, 0), (0, 0))).reshape(b, nb + 2, Q_BLOCK, hkv, dh)
        tw = jnp.concatenate([tp[:, :-2], tp[:, 1:-1], tp[:, 2:]], axis=2)
        return jnp.moveaxis(tw, 1, 0)

    kw, vw = band(k), band(v)
    qb = jnp.moveaxis(q.reshape(b, nb, Q_BLOCK, hkv, g, dh), 1, 0) * ATTN_SCALE
    blk = jnp.arange(nb, dtype=jnp.int32)[:, None, None]
    qi = jnp.arange(Q_BLOCK, dtype=jnp.int32)[None, :, None]
    kj = jnp.arange(nw, dtype=jnp.int32)[None, None, :]
    key_pos = (blk - 1) * Q_BLOCK + kj
    allowed = (jnp.abs(kj - Q_BLOCK - qi) <= WINDOW) & (key_pos >= 0) & (key_pos < s)

    def one_block(args):
        q_blk, k_blk, v_blk, ok = args
        s_win = jnp.einsum('bqhgd,bkhd->bhgqk', q_blk, k_blk).astype(jnp.float32)
        s_win = jnp.where(ok[None, None, None], s_win, NEG_INF)
        s_ctx = jnp.einsum('bqhgd,bchd->bhgqc', q_blk, k_ctx).astype(jnp.float32)
        p = softmax_with_sink(jnp.concatenate([s_win, s_ctx], axis=-1), sink).astype(v.dtype)
        return (jnp.einsum('bhgqk,bkhd->bqhgd', p[..., :nw], v_blk)
                + jnp.einsum('bhgqc,bchd->bqhgd', p[..., nw:], v_ctx))

    o = lax.map(one_block, (qb, kw, vw, allowed))
    return jnp.moveaxis(o, 0, 1).reshape(b, s, hkv * g * dh)

def neighbourhood_latent(q, k, v, k_ctx, v_ctx, rpb, rows):
    b, s, h, dh = q.shape
    kh = min(NA_ROWS, rows)
    kg = k.reshape(b, rows, GRID_W, h, dh)
    vg = v.reshape(b, rows, GRID_W, h, dh)
    qg = jnp.moveaxis(q.reshape(b, rows, GRID_W, h, dh), 1, 0) * ATTN_SCALE
    r_idx = jnp.arange(rows, dtype=jnp.int32)
    row_start = jnp.clip(r_idx - kh // 2, 0, rows - kh)
    cols = jnp.arange(GRID_W, dtype=jnp.int32)
    col_start = jnp.clip(cols - NA_COLS // 2, 0, GRID_W - NA_COLS)
    col_in = (cols[None, :] >= col_start[:, None]) & (cols[None, :] < col_start[:, None] + NA_COLS)
    col_bias_idx = jnp.clip(cols[None, :] - cols[:, None] + NA_COLS - 1, 0, 2 * NA_COLS - 2)
    rpb32 = rpb.astype(jnp.float32)
    n_loc = kh * GRID_W

    def one_row(args):
        q_row, r, rs = args
        k_band = lax.dynamic_slice_in_dim(kg, rs, kh, axis=1)
        v_band = lax.dynamic_slice_in_dim(vg, rs, kh, axis=1)
        s_loc = jnp.einsum('bqhd,brkhd->bhqrk', q_row, k_band).astype(jnp.float32)
        row_bias_idx = rs + jnp.arange(kh, dtype=jnp.int32) - r + NA_ROWS - 1
        bias = rpb32[:, row_bias_idx[None, :, None], col_bias_idx[:, None, :]]
        s_loc = jnp.where(col_in[:, None, :], s_loc + bias[None], NEG_INF).reshape(b, h, GRID_W, n_loc)
        s_ctx = jnp.einsum('bqhd,bchd->bhqc', q_row, k_ctx).astype(jnp.float32)
        p = jax.nn.softmax(jnp.concatenate([s_loc, s_ctx], axis=-1), axis=-1).astype(v.dtype)
        return (jnp.einsum('bhqn,bnhd->bqhd', p[..., :n_loc], v_band.reshape(b, n_loc, h, dh))
                + jnp.einsum('bhqc,bchd->bqhd', p[..., n_loc:], v_ctx))

    o = lax.map(one_row, (qg, r_idx, row_start))
    return jnp.moveaxis(o, 0, 1).reshape(b, s, h * dh)

def even_mixer(h_lat, h_ctx, last, *, w_in, w_out, g_q, g_k, sink, cos, sin):
    sizes = [A_Q_HEADS * HEAD_DIM, A_KV_HEADS * HEAD_DIM, A_KV_HEADS * HEAD_DIM,
             B_Q_HEADS * HEAD_DIM, B_KV_HEADS * HEAD_DIM, B_KV_HEADS * HEAD_DIM]
    splits = np.cumsum(sizes)[:-1].tolist()

    def project(h):
        qa, ka, va, qb, kb, vb = jnp.split(h @ w_in, splits, axis=-1)
        return (rms_norm(heads(qa, A_Q_HEADS), g_q), rms_norm(heads(ka, A_KV_HEADS), g_k), heads(va, A_KV_HEADS),
                heads(qb, B_Q_HEADS), heads(kb, B_KV_HEADS), heads(vb, B_KV_HEADS))

    qa, ka, va, qb, kb, vb = project(h_lat)
    cqa, cka, cva, cqb, ckb, cvb = project(h_ctx)
    qa, ka, qb, kb = (apply_rope(t, cos, sin) for t in (qa, ka, qb, kb))
    sink4 = sink.astype(jnp.float32).reshape(B_KV_HEADS, B_Q_HEADS // B_KV_HEADS, 1, 1)
    o_a = global_gqa_latent(group(qa, A_KV_HEADS), jnp.concatenate([ka, cka], axis=1),
                            jnp.concatenate([va, cva], axis=1))
    o_b = window_gqa_latent(group(qb, B_KV_HEADS), kb, vb, ckb, cvb, sink4)
    y_lat = jnp.concatenate([o_a, o_b], axis=-1) @ w_out
    if last:
        return y_lat, None
    c_a = context_attend(group(cqa, A_KV_HEADS), cka, cva, None)
    c_b = context_attend(group(cqb, B_KV_HEADS), ckb, cvb, sink4)
    return y_lat, jnp.concatenate([c_a, c_b], axis=-1) @ w_out

def odd_mixer(h_lat, h_ctx, last, *, w_in, w_out, rpb, rows):
    def project(h):
        q, k, v = jnp.split(h @ w_in, 3, axis=-1)
        return heads(q, C_HEADS), heads(k, C_HEADS), heads(v, C_HEADS)

    q, k, v = project(h_lat)
    cq, ck, cv = project(h_ctx)
    y_lat = neighbourhood_latent(q, k, v, ck, cv, rpb, rows) @ w_out
    if last:
        return y_lat, None
    return y_lat, context_attend(cq[:, :, :, None, :], ck, cv, None) @ w_out

def swiglu(h, w_gate, w_up, w_down):
    return (jax.nn.silu(h @ w_gate) * (h @ w_up)) @ w_down

def moe_swiglu(h, w_router, w_gate, w_up, w_down):
    logits = (h @ w_router).astype(jnp.float32)
    top_val, top_idx = lax.top_k(logits, TOP_K)
    weights = jax.nn.softmax(top_val, axis=-1)
    gates = jnp.sum(jax.nn.one_hot(top_idx, N_EXPERTS, dtype=jnp.float32) * weights[..., None], axis=-2)
    gates = gates.astype(h.dtype)
    out = jnp.zeros_like(h)
    for e in range(N_EXPERTS):
        out = out + gates[..., e:e + 1] * swiglu(h, w_gate[e], w_up[e], w_down[e])
    return out

def sandwich_layer(x, ctx, c, c_ctx, mixer, ffn, last, w_mod, b_mod, g_pre_mix, g_post_mix, g_pre_ffn, g_post_ffn):
    m_lat = jnp.split(jax.nn.silu(c)[:, None, :] @ w_mod + b_mod, N_MOD, axis=-1)
    m_ctx = jnp.split(jax.nn.silu(c_ctx) @ w_mod + b_mod, N_MOD, axis=-1)
    y_lat, y_ctx = mixer(modulate(x, g_pre_mix, m_lat[0], m_lat[1]),
                         modulate(ctx, g_pre_mix, m_ctx[0], m_ctx[1]), last)
    x = x + m_lat[2] * rms_norm(y_lat, g_post_mix)
    x = x + m_lat[5] * rms_norm(ffn(modulate(x, g_pre_ffn, m_lat[3], m_lat[4])), g_post_ffn)
    if not last:
        ctx = ctx + m_ctx[2] * rms_norm(y_ctx, g_post_mix)
        ctx = ctx + m_ctx[5] * rms_norm(ffn(modulate(ctx, g_pre_ffn, m_ctx[3], m_ctx[4])), g_post_ffn)
    return x, ctx

def setup_inputs(seed: int = 0) -> dict:
    key = jax.random.key(seed)
    keys = iter(jax.random.split(key, 64))
    ne, no = (DEPTH + 1) // 2, DEPTH // 2
    in_even = (A_Q_HEADS + 2 * A_KV_HEADS + B_Q_HEADS + 2 * B_KV_HEADS) * HEAD_DIM
    mix_even = (A_Q_HEADS + B_Q_HEADS) * HEAD_DIM
    mix_odd = C_HEADS * HEAD_DIM

    def normal(shape, scale):
        return scale * jax.random.normal(next(keys), shape, jnp.float32)

    def gain(shape):
        return 1.0 + normal(shape, 0.05)

    return {
        'x': normal((BATCH, SEQ, D_MODEL), 1.0),
        'c': normal((BATCH, D_MODEL), 1.0),
        'ctx': normal((BATCH, CTX_LEN, D_MODEL), 1.0),
        'c_ctx': normal((D_MODEL,), 1.0),
        'e_w_mod': normal((ne, D_MODEL, N_MOD * D_MODEL), D_MODEL ** -0.5),
        'e_b_mod': normal((ne, N_MOD * D_MODEL), 0.02),
        'e_g_pre_mix': gain((ne, D_MODEL)),
        'e_g_post_mix': gain((ne, D_MODEL)),
        'e_g_pre_ffn': gain((ne, D_MODEL)),
        'e_g_post_ffn': gain((ne, D_MODEL)),
        'e_w_in': normal((ne, D_MODEL, in_even), D_MODEL ** -0.5),
        'e_w_out': normal((ne, mix_even, D_MODEL), mix_even ** -0.5),
        'e_g_q': gain((ne, HEAD_DIM)),
        'e_g_k': gain((ne, HEAD_DIM)),
        'e_sink': normal((ne, B_Q_HEADS), 0.5),
        'e_w_gate': normal((ne, D_MODEL, D_FF), D_MODEL ** -0.5),
        'e_w_up': normal((ne, D_MODEL, D_FF), D_MODEL ** -0.5),
        'e_w_down': normal((ne, D_FF, D_MODEL), D_FF ** -0.5),
        'o_w_mod': normal((no, D_MODEL, N_MOD * D_MODEL), D_MODEL ** -0.5),
        'o_b_mod': normal((no, N_MOD * D_MODEL), 0.02),
        'o_g_pre_mix': gain((no, D_MODEL)),
        'o_g_post_mix': gain((no, D_MODEL)),
        'o_g_pre_ffn': gain((no, D_MODEL)),
        'o_g_post_ffn': gain((no, D_MODEL)),
        'o_w_in': normal((no, D_MODEL, 3 * mix_odd), D_MODEL ** -0.5),
        'o_w_out': normal((no, mix_odd, D_MODEL), mix_odd ** -0.5),
        'o_rpb': normal((no, C_HEADS, 2 * NA_ROWS - 1, 2 * NA_COLS - 1), 0.1),
        'o_w_router': normal((no, D_MODEL, N_EXPERTS), D_MODEL ** -0.5),
        'o_w_gate': normal((no, N_EXPERTS, D_MODEL, D_FF_EXPERT), D_MODEL ** -0.5),
        'o_w_up': normal((no, N_EXPERTS, D_MODEL, D_FF_EXPERT), D_MODEL ** -0.5),
        'o_w_down': normal((no, N_EXPERTS, D_FF_EXPERT, D_MODEL), D_FF_EXPERT ** -0.5),
    }

def reference(x, c, ctx, c_ctx,
              e_w_mod, e_b_mod, e_g_pre_mix, e_g_post_mix, e_g_pre_ffn, e_g_post_ffn,
              e_w_in, e_w_out, e_g_q, e_g_k, e_sink, e_w_gate, e_w_up, e_w_down,
              o_w_mod, o_b_mod, o_g_pre_mix, o_g_post_mix, o_g_pre_ffn, o_g_post_ffn,
              o_w_in, o_w_out, o_rpb, o_w_router, o_w_gate, o_w_up, o_w_down):
    rows = x.shape[1] // GRID_W
    cos, sin = axial_rope(x.shape[1])
    for i in range(DEPTH):
        j = i // 2
        last = i == DEPTH - 1
        if i % 2 == 0:
            mixer = functools.partial(even_mixer, w_in=e_w_in[j], w_out=e_w_out[j], g_q=e_g_q[j], g_k=e_g_k[j],
                                      sink=e_sink[j], cos=cos, sin=sin)
            ffn = functools.partial(swiglu, w_gate=e_w_gate[j], w_up=e_w_up[j], w_down=e_w_down[j])
            x, ctx = sandwich_layer(x, ctx, c, c_ctx, mixer, ffn, last, e_w_mod[j], e_b_mod[j],
                                    e_g_pre_mix[j], e_g_post_mix[j], e_g_pre_ffn[j], e_g_post_ffn[j])
        else:
            mixer = functools.partial(odd_mixer, w_in=o_w_in[j], w_out=o_w_out[j], rpb=o_rpb[j], rows=rows)
            ffn = functools.partial(moe_swiglu, w_router=o_w_router[j], w_gate=o_w_gate[j], w_up=o_w_up[j],
                                    w_down=o_w_down[j])
            x, ctx = sandwich_layer(x, ctx, c, c_ctx, mixer, ffn, last, o_w_mod[j], o_b_mod[j],
                                    o_g_pre_mix[j], o_g_post_mix[j], o_g_pre_ffn[j], o_g_post_ffn[j])
    return x


_drawn_inputs = setup_inputs


def setup_inputs(seed=0):
    import zlib

    import numpy as np

    out = dict(_drawn_inputs(seed))
    spreads = {}
    factors = {'e_g_q': 8.0, 'e_g_k': 4.078, 'e_sink': 8.0, 'o_g_post_ffn': 2.94, 'o_rpb': 3.788}
    for name, (base, spread) in spreads.items():
        noise = np.random.default_rng([zlib.crc32(name.encode()), seed]).standard_normal(out[name].shape)
        drawn = base * np.exp(spread * noise) if base else spread * noise
        out[name] = __import__('jax').numpy.asarray(drawn.astype(out[name].dtype))
    for name, factor in factors.items():
        out[name] = (out[name] * factor).astype(out[name].dtype)
    return out
```

```python
from contextlib import ExitStack

import concourse.bass as bass
from concourse import mybir
import numpy as np

P = 128
D = 1024
KD = D // P
SEQ = 256
CTX = 256
TILES = (SEQ + CTX) // P
LAT_TILES = SEQ // P
GRID_W = 64
ROWS = SEQ // GRID_W
DH = 64
N_MOD = 6
D_FF = 2816
D_FFE = 3584
EXPERTS = 8
QKV_E = 1536
GROUP_E = QKV_E // 2
QK_E = 10 * DH
HEADS_O = 16
NA_ROWS = 8
NA_COLS = 16
RPB_W = 2 * NA_COLS - 1
RPB_R = 2 * NA_ROWS - 1
ROW_SHIFTS = 2 * ROWS - 1
EPS = 1e-6
SCALE = DH ** -0.5
NEG = -1e30
WINDOW = 128

N = 512
SLOT = 4 * N
RAW = 6
SPLIT = 3
FFC = 256
CHUNKS_E = D_FF // FFC
CHUNKS_O = D_FFE // FFC
ITEM_SLOTS = 3 * CHUNKS_O
ITEM_COLS = 12
PER_MOD = 2 * (N_MOD * D // N)

M0_S = 0
WIN0_S = M0_S + PER_MOD
M1_S = WIN0_S + 6
WOUT0_S = M1_S + PER_MOD
FFA_S = WOUT0_S + 4
FFB_S = FFA_S + 3 * CHUNKS_E
WIN1_S = FFB_S + 3 * CHUNKS_E
WOUT1_S = WIN1_S + 12
MOE_S = WOUT1_S + 4


def split_number(s):
    return s - (PER_MOD if s < M1_S else 2 * PER_MOD)


ALU = mybir.AluOpType
ACT = mybir.ActivationFunctionType
F32 = mybir.dt.float32
F32R = mybir.dt.float32r
I32 = mybir.dt.int32
U32 = mybir.dt.uint32
AX_X = mybir.AxisListType.X

C_IDENT = 0
C_WIN = C_IDENT + P
C_ROPE = C_WIN + 2 * P
C_COL = C_ROPE + 4 * 32
C_IOTA = C_COL + GRID_W
C_TRI = C_IOTA + P
C_E8 = C_TRI + P
C_ALL = C_E8 + EXPERTS


def shape_constants():
    out = np.zeros((P, C_ALL), np.float32)
    i = np.arange(P)
    out[:, C_IDENT:C_WIN] = np.eye(P)
    for t in range(2):
        dist = np.abs((t * P + i)[:, None] - ((1 - t) * P + i)[None, :])
        out[:, C_WIN + t * P:C_WIN + (t + 1) * P] = np.where(dist <= WINDOW, 0.0, NEG)
    half = DH // 2
    freqs = (np.float32(10000.0) ** (-np.arange(0, half, 2, dtype=np.float32) / np.float32(half))).astype(np.float32)
    for t in range(2):
        token = t * P + i
        row, col = (token // GRID_W).astype(np.float32), (token % GRID_W).astype(np.float32)
        ang = np.concatenate([row[:, None] * freqs, col[:, None] * freqs], axis=-1).astype(np.float32)
        out[:, C_ROPE + t * 64:C_ROPE + t * 64 + 32] = np.cos(ang)
        out[:, C_ROPE + t * 64 + 32:C_ROPE + t * 64 + 64] = np.sin(ang)
    qc, kc = (i % GRID_W)[:, None], np.arange(GRID_W)[None, :]
    first = np.clip(qc - NA_COLS // 2, 0, GRID_W - NA_COLS)
    out[:, C_COL:C_IOTA] = np.where((kc >= first) & (kc < first + NA_COLS), 0.0, NEG)
    out[:, C_IOTA:C_TRI] = i[None, :]
    out[:, C_TRI:C_E8] = i[:, None] < i[None, :]
    out[:, C_E8:] = np.arange(EXPERTS)[None, :]
    return out


class Chain:

    def __init__(self, eng, sem):
        self.eng, self.sem, self.n = eng, sem, 0

    def add(self, ins):
        ins.then_inc(self.sem, 1)
        self.n = self.n + 1

    def wait(self):
        self.eng.wait_ge(self.sem, self.n)


def build(nc, a):
    with ExitStack() as ctx:
        def sem(name):
            return ctx.enter_context(nc.semaphore(name))

        def sems(prefix, names):
            return {n: sem(f"{prefix}_{n}") for n in names.split()}

        def sb(name, shape, dt=F32, scope=ctx):
            return scope.enter_context(nc.sbuf_tensor(name, shape, dt))

        raw = sb("raw", [P, RAW, SLOT])
        whi = sb("whi", [P, SPLIT, SLOT], F32R)
        wlo = sb("wlo", [P, SPLIT, SLOT], F32R)
        rpb_sb = sb("rpb_sb", [HEADS_O * ROW_SHIFTS, P])
        x_lat = sb("x_lat", [P, LAT_TILES, D])
        hh = sb("hh", [P, KD, N], F32R)
        hl = sb("hl", [P, KD, N], F32R)
        o_sb = sb("o_sb", [P, D])
        const = sb("const", [P, C_ALL])
        vt = sb("vt", [P, 2, 80])
        silu_c = sb("silu_c", [P, KD, 2])
        mod = sb("mod", [P, 2, N_MOD * KD, 2])
        coef_a = sb("coef_a", [P, 2, 2, KD, 2])
        coef_g = sb("coef_g", [P, 2, 2, KD, 2])
        qk_gain = sb("qk_gain", [P, 2, DH])
        sink = sb("sink", [P, 8])
        neg_sink = sb("neg_sink", [P, 8])
        ones = sb("ones", [P, P])
        eps = sb("eps", [P, 1])
        ssq = sb("ssq", [P, 8])
        root = sb("root", [P, 8])
        rstd = sb("rstd", [P, 8])
        w_router = sb("w_router", [P, KD, EXPERTS])
        neg_max = sb("neg_max", [P, 2, 8])
        sink_arg = sb("sink_arg", [P, 2, 8])
        sink_exp = sb("sink_exp", [P, 2, 8])
        exp_sum = sb("exp_sum", [P, 2, 8])
        exp_inv = sb("exp_inv", [P, 2, 8])

        with ExitStack() as even:
            x_ctx = sb("x_ctx", [P, 2, D], F32, even)
            with ExitStack() as s:
                vrow0 = sb("vrow0", [96, P], F32, s)
                vrow1 = sb("vrow1", [80, P], F32, s)
            with ExitStack() as s:
                qkv = sb("qkv", [P, TILES, QKV_E], F32, s)
                qk_t = sb("qk_t", [P, 10, N], F32, s)
            with ExitStack() as s:
                f_gate = sb("f_gate", [P, 2, D], F32, s)
                f_tmp = sb("f_tmp", [P, 2, D], F32, s)
                f_mod = sb("f_mod", [P, 2, KD, P], F32, s)
                f_silu = sb("f_silu", [P, 2, FFC], F32, s)
                f_h = sb("f_h", [P, 2, FFC], F32, s)
                f_hth = sb("f_hth", [P, 2, 2, 2 * P], F32R, s)
                f_htl = sb("f_htl", [P, 2, 2, 2 * P], F32R, s)
        with ExitStack() as s:
            o_q = sb("o_q", [P, 8, SEQ], F32, s)
            o_k = sb("o_k", [P, 8, N], F32, s)
            o_v = sb("o_v", [P, TILES, D], F32, s)
            o_bias = sb("o_bias", [P, 4, SEQ], F32, s)
            o_p = sb("o_p", [P, 2, 2, N], F32, s)
            o_pt = sb("o_pt", [P, 2, 2, N], F32, s)
        with ExitStack() as s:
            m_gate = sb("m_gate", [P, 1, D], F32, s)
            m_tmp = sb("m_tmp", [P, 2, D], F32, s)
            m_mod = sb("m_mod", [P, 2, KD, P], F32, s)
            m_acc = sb("m_acc", [P, 2, D], F32, s)
            h_hi = sb("h_hi", [P, 2, D], F32R, s)
            h_lo = sb("h_lo", [P, 2, D], F32R, s)
            m_silu = sb("m_silu", [P, 1, FFC], F32, s)
            m_h = sb("m_h", [P, 1, FFC], F32, s)
            m_hth = sb("m_hth", [P, 2, 2, P], F32R, s)
            m_htl = sb("m_htl", [P, 2, 2, P], F32R, s)
            m_y = m_tmp[:, 0, :]
            pick = sb("pick", [P, 2, P], F32R, s)
            put = sb("put", [P, 2, P], F32, s)
            put_t = sb("put_t", [P, 2, P], F32, s)
            logits = sb("logits", [P, 2, EXPERTS], F32, s)
            top = sb("top", [P, 2, 8], F32, s)
            top_i = sb("top_i", [P, 2, 8], U32, s)
            top_f = sb("top_f", [P, 2, 8], F32, s)
            gw = sb("gw", [P, 2, 4], F32, s)
            hot = sb("hot", [P, 2, 2, EXPERTS], F32, s)
            items = sb("items", [P, 7, ITEM_COLS], F32, s)
            over = sb("over", [P, 4, 12], F32, s)
            over_hot = sb("over_hot", [P, 4, EXPERTS], F32, s)
            over_tmp = sb("over_tmp", [P, 7, EXPERTS], F32, s)
            table = sb("table", [1, 16], I32, s)

        ps = ctx.enter_context(nc.psum_tensor("ps", [P, 8, N], F32))
        bias_dram = nc.dram_tensor("bias_scratch", [HEADS_O * ROW_SHIFTS, GRID_W, P], F32, kind="Internal").ap()

        ident = const[:, C_IDENT:C_WIN]

        def x_tile(t):
            return x_lat[:, t, :] if t < LAT_TILES else x_ctx[:, t - LAT_TILES, :]

        x_loaded, const_loaded, vec_loaded, misc_loaded = (sem(n) for n in
                                                           ("x_loaded", "const_loaded", "vec_loaded", "misc_loaded"))
        raw_landed = [sem(f"raw_landed{i}") for i in range(RAW)]
        hi_ready, lo_ready, slot_used, mod_used = (sem(n) for n in ("hi_ready", "lo_ready", "slot_used", "mod_used"))
        act_chain, dve_chain = sem("act_chain"), sem("dve_chain")
        st = sems("set", "vt silu_c vec coef0 coef1 pool")
        norms = [sems(f"norm{i}", "ssq root xn xt t1 hi lo") for i in range(5)]
        router = sems("router", "logits back exp ex sel rank")
        gates = [sems(f"gate{i}", "bc sb") for i in range(5)]
        resids = [sems(f"resid{i}", "root x") for i in range(5)]
        gemms = [sems(f"gemm{i}", "act dve") for i in range(4)]
        ffns = [sems(f"ffn{i}", "silu h t hi lo") for i in range(3)]
        attns = [sems(f"attn{i}", "s nm p t pta ptd o osb ot oth otl") for i in range(2)]
        qk = sems("qk", "ssq root ready t act dve")
        bias = sems("bias", "rows wrote pool")
        bias_landed = [sem(f"bias_landed{i}") for i in range(4)]
        route_ready, pick_ready, gathered, ht_hi, ht_lo = (sem(n) for n in
                                                           ("route_ready", "pick_ready", "gathered", "ht_hi", "ht_lo"))
        put_ready, put_turned, put_t_ready, y_copied, scattered = (
            sem(n) for n in ("put_ready", "put_turned", "put_t_ready", "y_copied", "scattered"))
        acc_added = [sem(f"acc_added{t}") for t in range(2)]
        out_stored = sem("out_stored")

        def used(s, turns=0):
            return slot_used, turns * RAW + split_number(s) + 1

        even_plan = {"groups": 2 * TILES, "even": True}
        odd_plan = {"groups": 4, "even": False}
        qkv_p = [[qkv[:, b, i * GROUP_E:i * GROUP_E + N] for i in range(2)] for b in range(2)]
        qkv_pt = [[qkv[:, 2 + b, i * GROUP_E:i * GROUP_E + N] for i in range(2)] for b in range(2)]

        def qkv_parts(n, t):
            src = ps[:, (n % 2) * 4 + t, :]
            queries = [qkv[:, t, GROUP_E * g:GROUP_E * g + 8 * DH].rearrange("p (c a d) -> p a c d", a=2, d=DH)
                       for g in range(2)]
            if n == 0:
                return [(queries[0], src.rearrange("p (a c d) -> p a c d", a=2, d=DH))]
            if n == 1:
                return [(qkv[:, t, N:GROUP_E], src[:, 0:256]),
                        (queries[1][:, 0], src[:, 256:512].rearrange("p (c d) -> p c d", d=DH))]
            return [(queries[1][:, 1], src[:, 0:256].rearrange("p (c d) -> p c d", d=DH)),
                    (qkv[:, t, GROUP_E + 8 * DH:QKV_E], src[:, 256:512])]

        def nkeys(plan, g):
            return N if not plan["even"] or g // 2 < LAT_TILES else CTX

        def has_sink(plan, g):
            return plan["even"] and g % 2 == 1

        def buf(p, b, i):
            return p[b][i] if isinstance(p, list) else p[:, b, i, :]

        def qk_ssq():
            return qk_t[:, 9, 0:40]

        def qk_root():
            return qk_t[:, 9, 64:104]

        def attention_act(act, s, plan, p, pt):
            pairs = 4 * plan["groups"]
            for at in range(pairs + 6):
                if at < pairs:
                    g, n = at // 4, nkeys(plan, at // 4)
                    act.wait_ge(s["nm"], at + 1)
                    if at >= 2:
                        act.wait_ge(s["t"], at - 1)
                    for i in range(2):
                        h = 2 * (at % 4) + i
                        ins = act.activation(buf(p, at % 2, i)[:, 0:n], ps[:, 2 * (at % 2) + i, 0:n], ACT.Exp,
                                             bias=neg_max[:, g % 2, h:h + 1], accum_out=exp_sum[:, g % 2, h:h + 1])
                    if has_sink(plan, g):
                        h = 2 * (at % 4)
                        ins = act.activation(sink_exp[:, g % 2, h:h + 2], sink_arg[:, g % 2, h:h + 2], ACT.Exp)
                    ins.then_inc(s["p"], 1)
                if 1 <= at <= pairs:
                    n = nkeys(plan, (at - 1) // 4)
                    act.wait_ge(s["t"], at)
                    act.activation(buf(pt, (at - 1) % 2, 0)[:, 0:n], ps[:, 4, 0:n], ACT.Copy).then_inc(s["pta"], 1)
                for half in range(2):
                    last = at - 4 - half
                    if last >= 0 and last % 8 == 7 and last < pairs:
                        t = last // 8
                        act.wait_ge(s["ot"], 2 * t + half + 1)
                        act.activation(hh[:, 4 * half:4 * half + 4, t * P:(t + 1) * P],
                                       ps[:, 7, :].rearrange("p (k n) -> p k n", n=P), ACT.Copy).then_inc(s["oth"], 1)

        block = ctx.enter_context(nc.Block())

        @block.sync
        def _(sp):
            sp.dma_start(const[:], a["constants"]).then_inc(const_loaded, 16)
            for layer, rows in (("e", vrow0), ("o", vrow1)):
                sp.dma_start(rows[0:48, :], a[f"{layer}_b_mod"].rearrange("o (r p) -> (o r) p", p=P)).then_inc(vec_loaded, 16)
                for i, g in enumerate(("pre_mix", "post_mix", "pre_ffn", "post_ffn")):
                    sp.dma_start(rows[48 + 8 * i:56 + 8 * i, :],
                                 a[f"{layer}_g_{g}"].rearrange("o (r p) -> (o r) p", p=P)).then_inc(vec_loaded, 16)
            sp.dma_start(vrow0[80:88, :], a["c"].rearrange("o (r p) -> (o r) p", p=P)).then_inc(vec_loaded, 16)
            sp.dma_start(vrow0[88:96, :], a["c_ctx"].rearrange("(r p) -> r p", p=P)).then_inc(vec_loaded, 16)
            sp.dma_start(x_lat[:], a["x"].rearrange("o (t p) d -> p (o t) d", p=P)).then_inc(x_loaded, 16)
            sp.dma_start(x_ctx[:], a["ctx"].rearrange("o (t p) d -> p (o t) d", p=P)).then_inc(x_loaded, 16)

            def fill(s, pairs, turns=0):
                before = s - RAW
                if before >= 0:
                    if before < WIN0_S:
                        sp.wait_ge(mod_used, before // 2 + 1)
                    elif M1_S <= before < WOUT0_S:
                        sp.wait_ge(mod_used, PER_MOD // 2 + (before - M1_S) // 2 + 1)
                    else:
                        sp.wait_ge(lo_ready, turns * RAW + split_number(before) + 1)
                for dst, src in pairs:
                    sp.dma_start(dst, src).then_inc(raw_landed[s % RAW], 16)

            def fill_projection(s, w, n, half):
                dst = raw[:, s % RAW, :].rearrange("p (k n) -> p k n", n=N)
                src = w.rearrange("o (k p) n -> p (o k) n", p=P)[:, 4 * half:4 * half + 4, n * N:(n + 1) * N]
                fill(s, [(dst[:, 0:2], src[:, 0:2]), (dst[:, 2:4], src[:, 2:4])])

            def fill_all(first, w, chunks):
                for n in range(chunks):
                    for half in range(2):
                        fill_projection(first + 2 * n + half, w, n, half)

            def swiglu_stream(first, chunks, wg, wu, wd, expert_k, expert_b, item_turns):
                def gu(s, kk, turns, j):
                    for half in range(2):
                        dst = raw[:, (s + half) % RAW, :].rearrange("p (k n) -> p k n", n=N)
                        k0 = bass.ds(expert_k + 4 * half, 4)
                        c0 = bass.ds(j * 2 * FFC + kk * FFC, FFC)
                        fill(s + half, [(dst[:, :, 0:FFC], wg[:, k0, c0]), (dst[:, :, FFC:N], wu[:, k0, c0])], turns)

                def down(s, kk, turns, j):
                    dst = raw[:, s % RAW, :].rearrange("p (b n) -> p b n", n=D)
                    b0 = expert_b + j * 4 + 2 * kk
                    fill(s, [(dst[:, b:b + 1], wd[:, bass.ds(b0 + b, 1)]) for b in range(2)], turns)

                gu(first, 0, item_turns, 0)

                def body(kk, turns, j):
                    gu(first + 3 * kk - 1, kk, turns, j)
                    down(first + 3 * kk + 1, kk - 1, turns, j)

                body(1, item_turns, 0)
                with sp.Fori(0, (chunks - 2) // 2) as j:
                    body(2, item_turns + j, j)
                    body(3, item_turns + j, j)
                if chunks % 2:
                    body(chunks - 1, item_turns, 0)
                down(first + 3 * chunks - 1, chunks - 1, item_turns, 0)

            fill_all(M0_S, a["e_w_mod"], PER_MOD // 2)
            fill_all(WIN0_S, a["e_w_in"], 3)
            fill_all(M1_S, a["o_w_mod"], PER_MOD // 2)
            fill_all(WOUT0_S, a["e_w_out"], 2)
            eg, eu = (a[n].rearrange("o (k p) f -> p (o k) f", p=P) for n in ("e_w_gate", "e_w_up"))
            ed = a["e_w_down"].rearrange("o (b p) n -> p (o b) n", p=P)
            for first in (FFA_S, FFB_S):
                swiglu_stream(first, CHUNKS_E, eg, eu, ed, 0, 0, 0)
            fill_all(WIN1_S, a["o_w_in"], 6)
            fill_all(WOUT1_S, a["o_w_out"], 2)

            og, ou = (a[n].rearrange("o e (k p) f -> p (o e k) f", p=P) for n in ("o_w_gate", "o_w_up"))
            od = a["o_w_down"].rearrange("o e (b p) n -> p (o e b) n", p=P)
            turns_per_item = ITEM_SLOTS // RAW
            with sp.Fori(0, EXPERTS - 1) as i:
                swiglu_stream(MOE_S, CHUNKS_O, og, ou, od, i * KD, i * (D_FFE // P), i * turns_per_item)
            sp.wait_ge(route_ready, 1)
            n_items = sp.value_load(table[0:1, ITEM_COLS:ITEM_COLS + 1], min_val=EXPERTS, max_val=EXPERTS + 3)
            with sp.Fori(EXPERTS - 1, n_items) as i:
                e = sp.value_load(table[0:1, bass.ds(i, 1)], min_val=0, max_val=EXPERTS - 1)
                swiglu_stream(MOE_S, CHUNKS_O, og, ou, od, e * KD, e * (D_FFE // P), i * turns_per_item)
            sp.wait_ge(resids[4]["x"], 2)
            sp.dma_start(a["out"].rearrange("o (t p) d -> p (o t) d", p=P), x_lat[:]).then_inc(out_stored, 16)
            sp.wait_ge(out_stored, 16)

        @block.gpsimd
        def _(pool):
            pool.memset(ones[:], 1.0).then_inc(st["pool"], 1)
            pool.memset(eps[:], EPS).then_inc(st["pool"], 1)
            pool.memset(rpb_sb[:], 0.0).then_inc(st["pool"], 1)
            for i, name in enumerate(("e_g_q", "e_g_k")):
                pool.dma_start(qk_gain[:, i, :], bass.AP(a[name].tensor, 0, [[0, P], [1, DH]])).then_inc(misc_loaded, 16)
            pool.dma_start(sink[:], bass.AP(a["e_sink"].tensor, 0, [[0, P], [1, 8]])).then_inc(misc_loaded, 16)
            pool.dma_start(w_router[:], a["o_w_router"].rearrange("o (k p) e -> p (o k) e", p=P)).then_inc(misc_loaded, 16)
            pool.wait_ge(st["pool"], 3)
            for h in range(HEADS_O):
                r0 = NA_ROWS - ROWS
                pool.dma_start(rpb_sb[h * ROW_SHIFTS:(h + 1) * ROW_SHIFTS, GRID_W - NA_COLS:GRID_W - NA_COLS + RPB_W],
                               a["o_rpb"][0, h, r0:r0 + ROW_SHIFTS, :]).then_inc(bias["rows"], 16)
            pool.wait_ge(bias["rows"], 16 * HEADS_O)
            n_rows = HEADS_O * ROW_SHIFTS
            pool.dma_start(bass.AP(bias_dram.tensor, 0, [[GRID_W * P, n_rows], [P, GRID_W], [1, P]]),
                           bass.AP(rpb_sb, 0, [[P, n_rows], [0, GRID_W], [1, P]])).then_inc(bias["wrote"], 16)
            pool.wait_ge(bias["wrote"], 16)
            def mask_unit(u):
                pool.wait_ge(bias_landed[u % 4], 32 * (u // 4 + 1))
                v = o_bias[:, u % 4, :].rearrange("p (k c) -> p k c", c=GRID_W)
                m = bass.AP(const, C_COL, [[C_ALL, P], [0, ROWS], [1, GRID_W]])
                pool.tensor_tensor(v, v, m, ALU.add).then_inc(bias["pool"], 1)

            pool.wait_ge(const_loaded, 16)
            pool.wait_ge(norms[3]["lo"], TILES)
            for u in range(2 * HEADS_O):
                t, h = u // HEADS_O, u % HEADS_O
                if u >= 4:
                    pool.wait_ge(attns[1]["s"], (u - 4) // 2 + 1)
                for r2 in range(2):
                    row = 2 * t + r2
                    src = bass.AP(bias_dram.tensor, (h * ROW_SHIFTS + ROWS - 1 - row) * GRID_W * P + GRID_W - 1,
                                  [[P - 1, GRID_W], [GRID_W * P, ROWS], [1, GRID_W]])
                    pool.dma_start(o_bias[r2 * GRID_W:(r2 + 1) * GRID_W, u % 4, :].rearrange("p (k c) -> p k c", c=GRID_W),
                                   src).then_inc(bias_landed[u % 4], 16)
                if u >= 1:
                    mask_unit(u - 1)
            mask_unit(2 * HEADS_O - 1)

        @block.scalar
        def _(act):
            chain = Chain(act, act_chain)

            def hi(s, turns=0):
                q = split_number(s)
                act.wait_ge(raw_landed[s % RAW], turns * 32 + 32 * (s // RAW + 1))
                if q >= SPLIT:
                    act.wait_ge(slot_used, turns * RAW + q - SPLIT + 1)
                act.activation(whi[:, q % SPLIT, :], raw[:, s % RAW, :], ACT.Copy).then_inc(hi_ready, 1)

            def norm(m, tiles, junk, mod_tile, dst=None):
                for i, t in enumerate(tiles):
                    if i:
                        chain.wait()
                    chain.add(act.activation(junk, x_tile(t), ACT.Square, accum_out=ssq[:, i:i + 1]))
                chain.wait()
                act.activation(root[:, 0:len(tiles)], ssq[:, 0:len(tiles)], ACT.Sqrt, scale=1.0 / D,
                               bias=eps[:, 0:1]).then_inc(m["root"], 1)
                for i, t in enumerate(tiles):
                    if dst is None:
                        act.wait_ge(m["t1"], i + 1)
                        act.activation(hh[:, :, i * P:(i + 1) * P], mod_tile[:, i % 2], ACT.Copy).then_inc(m["hi"], 1)
                    else:
                        act.wait_ge(router["back"], i + 1)
                        act.activation(dst[:, i, :], ps[:, 2 + 2 * i:4 + 2 * i, :].rearrange("p b n -> p (b n)"),
                                       ACT.Copy).then_inc(m["hi"], 1)

            def gate(g, dst, n, bank=6):
                for j in range(n):
                    act.wait_ge(g["bc"], j + 1)
                    act.activation(dst[:, j, :], ps[:, bank - 2 * j:bank + 2 - 2 * j, :].rearrange("p b n -> p (b n)"),
                                   ACT.Copy).then_inc(g["sb"], 1)

            def resid(r, tiles, y_ready, y_of, junk):
                for i, t in enumerate(tiles):
                    act.wait_ge(*y_ready(i))
                    if i >= 1:
                        act.wait_ge(r["x"], i)
                    chain.add(act.activation(junk[:, i % 2, :], y_of(i), ACT.Square, accum_out=ssq[:, i:i + 1]))
                    chain.wait()
                    act.activation(root[:, i:i + 1], ssq[:, i:i + 1], ACT.Sqrt, scale=1.0 / D,
                                   bias=eps[:, 0:1]).then_inc(r["root"], 1)

            def swiglu(f, first, m_tiles, silu, hth):
                def silu_chunk(kk, turns):
                    act.wait_ge(*used(first + (3 * kk if kk else 1), turns))
                    act.activation(silu[:], ps[:, 0:m_tiles, 0:FFC], ACT.Silu).then_inc(f["silu"], 1)

                def turned(kk, turns):
                    act.wait_ge(f["t"], turns * 2 + kk + 1)
                    cols = 2 * m_tiles * P
                    act.activation(hth[:, kk % 2].rearrange("p b n -> p (b n)"), ps[:, m_tiles, 0:cols],
                                   ACT.Copy).then_inc(f["hi"], 1)

                def body(kk, turns, last=False):
                    hi(first + 3 * kk + 1, turns)
                    hi(first + 3 * kk + 2, turns)
                    silu_chunk(kk, turns)
                    if not last:
                        hi(first + 3 * kk + 3, turns)
                    turned(kk, turns)
                return body

            def swiglu_all(f, first, m_tiles, chunks, silu, hth, item_turns, in_head=None):
                body = swiglu(f, first, m_tiles, silu, hth)
                hi(first, item_turns)
                body(0, item_turns)
                if in_head is not None:
                    in_head()
                body(1, item_turns)
                pairs = (chunks - 2) // 2
                if chunks % 2:
                    with act.Fori(0, pairs) as j:
                        body(2, item_turns + j)
                        body(3, item_turns + j)
                    body(chunks - 1, item_turns, last=True)
                else:
                    with act.Fori(0, pairs - 1) as j:
                        body(2, item_turns + j)
                        body(3, item_turns + j)
                    body(chunks - 2, item_turns)
                    body(chunks - 1, item_turns, last=True)

            act.wait_ge(st["vt"], 2)
            act.activation(silu_c[:], ps[:, 0, 80:96].rearrange("p (j k) -> p k j", j=2), ACT.Silu).then_inc(st["silu_c"], 1)
            act.wait_ge(x_loaded, 32)
            act.wait_ge(st["pool"], 3)
            norm(norms[0], range(TILES), o_sb[:], f_mod)
            for q in range(3):
                hi(WIN0_S + q)
            for n in range(3):
                if n < 2:
                    hi(WIN0_S + 2 * n + 3)
                for t in range(2):
                    act.wait_ge(*used(WIN0_S + 2 * n + 1))
                    for dst, src in qkv_parts(n, t):
                        ins = act.activation(dst, src, ACT.Copy)
                    ins.then_inc(gemms[0]["act"], 1)
                if n < 1:
                    hi(WIN0_S + 2 * n + 4)
            act.wait_ge(qk["ssq"], 1)
            act.activation(qk_root(), qk_ssq(), ACT.Sqrt, scale=1.0 / DH, bias=eps[:, 0:1]).then_inc(qk["root"], 1)
            for i in range(0, 10, 2):
                act.wait_ge(qk["t"], i + 1)
                act.activation(qk_t[:, i, :], ps[:, 1 + i % 6, :], ACT.Copy,
                               scale=SCALE if i % 5 < 4 else 1.0).then_inc(qk["act"], 1)
            attention_act(act, attns[0], even_plan, qkv_p, qkv_pt)
            gate(gates[0], f_gate, 2)
            for q in range(4):
                hi(WOUT0_S + q)
            resid(resids[0], range(TILES), lambda i: used(WOUT0_S + 3), lambda i: ps[:, 2 * i:2 * i + 2, :].rearrange("p b n -> p (b n)"), f_tmp)
            for n, (first, tiles) in enumerate(((FFA_S, (0, 1)), (FFB_S, (2, 3)))):
                act.wait_ge(resids[n]["x"], 4 if n == 0 else 2)
                norm(norms[1 + n], tiles, f_tmp[:, 0, :], f_mod)
                gate(gates[1 + n], f_gate, 1)
                swiglu_all(ffns[n], first, 2, CHUNKS_E, f_silu, f_hth, 0)
                resid(resids[1 + n], tiles, lambda i, first=first: used(first + 3 * CHUNKS_E - 1),
                      lambda i: ps[:, 3 + 2 * i:5 + 2 * i, :].rearrange("p b n -> p (b n)"), f_tmp)
            act.wait_ge(resids[2]["x"], 2)
            norm(norms[3], range(TILES), f_tmp[:, 0, :], f_mod)
            for q in range(3):
                hi(WIN1_S + q)
            for n in range(6):
                if 2 * n + 3 < 12:
                    hi(WIN1_S + 2 * n + 3)
                for b in range(2):
                    act.wait_ge(*used(WIN1_S + 2 * n + 1))
                    src = ps[:, (n % 2) * 4 + b, :]
                    if n < 2:
                        ins = act.activation(o_q[:, 4 * n + b, :], src[:, 0:SEQ], ACT.Copy, scale=SCALE)
                    elif n < 4:
                        ins = act.activation(o_k[:, 4 * (n - 2) + b, :], src, ACT.Copy)
                    else:
                        ins = act.activation(o_v[:, b, (n - 4) * N:(n - 3) * N], src, ACT.Copy)
                    ins.then_inc(gemms[2]["act"], 1)
                if 2 * n + 4 < 12:
                    hi(WIN1_S + 2 * n + 4)
            attention_act(act, attns[1], odd_plan, o_p, o_pt)
            gate(gates[3], m_gate, 1)
            for q in range(4):
                hi(WOUT1_S + q)
            resid(resids[3], (0, 1), lambda i: used(WOUT1_S + 3), lambda i: ps[:, 2 * i:2 * i + 2, :].rearrange("p b n -> p (b n)"), m_tmp)
            act.wait_ge(resids[3]["x"], 2)
            norm(norms[4], (0, 1), m_tmp[:, 0, :], m_mod, h_hi)
            gate(gates[4], m_gate, 1, 0)
            act.wait_ge(router["exp"], 1)
            act.activation(gw[:, :, 1:2], gw[:, :, 0:1], ACT.Exp).then_inc(router["ex"], 1)

            def ht(i):
                act.wait_ge(gathered, i + 1)
                act.activation(hh[:, :, 0:P], ps[:, 4:6, :].rearrange("p b (k n) -> p (b k) n", n=P), ACT.Copy).then_inc(ht_hi, 1)

            ht(0)
            act.wait_ge(route_ready, 1)
            n_items = act.value_load(table[0:1, ITEM_COLS:ITEM_COLS + 1], min_val=EXPERTS, max_val=EXPERTS + 3)
            with act.Fori(0, n_items) as i:
                def put_turn():
                    act.wait_ge(put_turned, i + 1)
                    act.activation(put_t[:].rearrange("p t n -> p (t n)"), ps[:, 4, 0:2 * P], ACT.Copy).then_inc(put_t_ready, 1)
                swiglu_all(ffns[2], MOE_S, 1, CHUNKS_O, m_silu, m_hth, i * (ITEM_SLOTS // RAW), put_turn)
                act.wait_ge(*used(MOE_S + ITEM_SLOTS - 1, i * (ITEM_SLOTS // RAW)))
                act.activation(m_y, ps[:, 2:4, :].rearrange("p b n -> p (b n)"), ACT.Copy).then_inc(y_copied, 1)
                ht(i + 1)
            resid(resids[4], (0, 1), lambda i: (acc_added[1], n_items + 1), lambda i: m_acc[:, i, :], m_tmp)

        @block.vector
        def _(dve):
            chain = Chain(dve, dve_chain)

            def lo(s, turns=0):
                q = split_number(s)
                dve.wait_ge(hi_ready, turns * RAW + q + 1)
                dve.tensor_tensor(wlo[:, q % SPLIT, :], raw[:, s % RAW, :], whi[:, q % SPLIT, :].bitcast(F32),
                                  ALU.subtract).then_inc(lo_ready, 1)

            def coefficients(layer, mod_bank, ready):
                b = vt[:, layer, 0:48].unsqueeze(2).to_broadcast([P, 48, 2])
                chain.add(dve.tensor_tensor(mod[:, layer], ps[:, mod_bank, 0:96].rearrange("p (c j) -> p c j", j=2), b, ALU.add))
                chain.wait()
                for i in range(2):
                    pre = vt[:, layer, 48 + 16 * i:56 + 16 * i].unsqueeze(2).to_broadcast([P, KD, 2])
                    post = vt[:, layer, 56 + 16 * i:64 + 16 * i].unsqueeze(2).to_broadcast([P, KD, 2])
                    dve.scalar_tensor_tensor(coef_a[:, layer, i], mod[:, layer, 8 * (1 + 3 * i):8 * (2 + 3 * i)], 1.0, pre,
                                             ALU.add, ALU.mult).then_inc(ready, 1)
                    dve.tensor_tensor(coef_g[:, layer, i], mod[:, layer, 8 * (2 + 3 * i):8 * (3 + 3 * i)], post,
                                      ALU.mult).then_inc(ready, 1)

            def norm(m, tiles, layer, which, xn, mod_tile, coef, banks, dst=None):
                dve.wait_ge(m["root"], 1)
                chain.add(dve.reciprocal(rstd[:, 0:len(tiles)], root[:, 0:len(tiles)]))
                chain.wait()
                dve.wait_ge(coef, 4)

                def scale(i, t):
                    if i >= 2:
                        dve.wait_ge(m["xt"], i - 1)
                    dve.tensor_scalar(xn[:, i % 2, :], x_tile(t), rstd[:, i:i + 1], None, ALU.mult).then_inc(m["xn"], 1)

                def modulate(i, t):
                    j = 0 if t < LAT_TILES else 1
                    dve.wait_ge(m["xt"], i + 1)
                    if i >= 2:
                        if dst is None:
                            dve.wait_ge(m["hi"], i - 1)
                            dve.wait_ge(m["lo"], i - 1)
                    for k in range(KD):
                        ins = dve.tensor_scalar(mod_tile[:, i % 2, k, :],
                                          ps[:, banks[i % 2] + k // 4, (k % 4) * P:(k % 4 + 1) * P],
                                          coef_a[:, layer, which, k, j:j + 1], mod[:, layer, 24 * which + k, j:j + 1],
                                          ALU.mult, ALU.add)
                    ins.then_inc(m["t1"], 1)

                def split(i):
                    dve.wait_ge(m["hi"], i + 1)
                    if dst is None:
                        dve.tensor_tensor(hl[:, :, i * P:(i + 1) * P], mod_tile[:, i % 2],
                                          hh[:, :, i * P:(i + 1) * P].bitcast(F32), ALU.subtract).then_inc(m["lo"], 1)
                    else:
                        dve.tensor_tensor(dst[1][:, i, :], ps[:, 2 + 2 * i:4 + 2 * i, :].rearrange("p b n -> p (b n)"),
                                          dst[0][:, i, :].bitcast(F32), ALU.subtract).then_inc(m["lo"], 1)

                n = len(tiles)
                scale(0, tiles[0])
                for i, t in enumerate(tiles):
                    if i + 1 < n:
                        scale(i + 1, tiles[i + 1])
                    modulate(i, t)
                    if dst is None:
                        split(i)
                if dst is not None:
                    for i in range(n):
                        split(i)

            def resid(r, tiles, g, y_of, gate_tile, tmp):
                for i, t in enumerate(tiles):
                    dve.wait_ge(r["root"], i + 1)
                    chain.add(dve.reciprocal(rstd[:, i:i + 1], root[:, i:i + 1]))
                    chain.wait()
                    j = 0 if len(tiles) == 2 or t < LAT_TILES else 1
                    dve.wait_ge(g["sb"], j + 1)
                    chain.add(dve.scalar_tensor_tensor(tmp[:, i % 2, :], y_of(i), rstd[:, i:i + 1], gate_tile[:, j, :],
                                                       ALU.mult, ALU.mult))
                    chain.wait()
                    dve.tensor_tensor(x_tile(t), x_tile(t), tmp[:, i % 2, :], ALU.add).then_inc(r["x"], 1)

            def swiglu_body(f, first, m_tiles, silu, h, hth, htl):
                def body(kk, turns, last=False):
                    lo(first + 3 * kk + 1, turns)
                    lo(first + 3 * kk + 2, turns)
                    dve.wait_ge(f["silu"], turns * 2 + kk + 1)
                    dve.tensor_tensor(h[:], silu[:], ps[:, 0:m_tiles, FFC:N], ALU.mult).then_inc(f["h"], 1)
                    if not last:
                        lo(first + 3 * kk + 3, turns)
                    dve.wait_ge(f["hi"], turns * 2 + kk + 1)
                    cols = 2 * m_tiles * P
                    dve.tensor_tensor(htl[:, kk % 2].rearrange("p b n -> p (b n)"), ps[:, m_tiles, 0:cols],
                                      hth[:, kk % 2].rearrange("p b n -> p (b n)").bitcast(F32),
                                      ALU.subtract).then_inc(f["lo"], 1)
                return body

            def swiglu_all(f, first, m_tiles, chunks, silu, h, hth, htl, item_turns, in_head=None):
                body = swiglu_body(f, first, m_tiles, silu, h, hth, htl)
                lo(first, item_turns)
                body(0, item_turns)
                if in_head is not None:
                    in_head()
                body(1, item_turns)
                pairs = (chunks - 2) // 2
                if chunks % 2:
                    with dve.Fori(0, pairs) as j:
                        body(2, item_turns + j)
                        body(3, item_turns + j)
                    body(chunks - 1, item_turns, last=True)
                else:
                    with dve.Fori(0, pairs - 1) as j:
                        body(2, item_turns + j)
                        body(3, item_turns + j)
                    body(chunks - 2, item_turns)
                    body(chunks - 1, item_turns, last=True)

            def attention(s, plan, p, pt):
                pairs = 4 * plan["groups"]
                for at in range(pairs + 6):
                    if at < pairs:
                        g, n = at // 4, nkeys(plan, at // 4)
                        h = 2 * (at % 4)
                        nm = neg_max[:, g % 2, h:h + 2]
                        dve.wait_ge(s["s"], at + 1)
                        ins = dve.tensor_reduce(nm, ps[:, 2 * (at % 2):2 * (at % 2) + 2, 0:n], AX_X, ALU.max, negate=True)
                        if has_sink(plan, g):
                            chain.add(ins)
                            chain.wait()
                            chain.add(dve.tensor_tensor(nm, nm, neg_sink[:, h:h + 2], ALU.min))
                            chain.wait()
                            ins = dve.tensor_tensor(sink_arg[:, g % 2, h:h + 2], nm, sink[:, h:h + 2], ALU.add)
                        ins.then_inc(s["nm"], 1)
                    if 1 <= at <= pairs:
                        n = nkeys(plan, (at - 1) // 4)
                        dve.wait_ge(s["t"], at)
                        dve.tensor_copy(buf(pt, (at - 1) % 2, 1)[:, 0:n], ps[:, 5, 0:n]).then_inc(s["ptd"], 1)
                    last = at - 2
                    if last >= 0 and last % 4 == 3 and last < pairs:
                        g = last // 4
                        dve.wait_ge(s["p"], last + 1)
                        total = exp_sum[:, g % 2, :]
                        if has_sink(plan, g):
                            chain.add(dve.tensor_tensor(total, total, sink_exp[:, g % 2, :], ALU.add))
                            chain.wait()
                        chain.add(dve.reciprocal(exp_inv[:, g % 2, :], total))
                        dve.wait_ge(s["o"], g + 1)
                        if g % 2 == 0 and g >= 2:
                            dve.wait_ge(s["ot"], g)
                        chain.wait()
                        dve.tensor_tensor(o_sb[:, (g % 2) * N:(g % 2 + 1) * N].rearrange("p (h d) -> p h d", d=DH),
                                          ps[:, 6, :].rearrange("p (h d) -> p h d", d=DH),
                                          exp_inv[:, g % 2, :].unsqueeze(2).to_broadcast([P, 8, DH]),
                                          ALU.mult).then_inc(s["osb"], 1)
                    for half in range(2):
                        last = at - 4 - half
                        if last >= 0 and last % 8 == 7 and last < pairs:
                            t = last // 8
                            dve.wait_ge(s["oth"], 2 * t + half + 1)
                            dve.tensor_tensor(hl[:, 4 * half:4 * half + 4, t * P:(t + 1) * P],
                                              ps[:, 7, :].rearrange("p (k n) -> p k n", n=P),
                                              hh[:, 4 * half:4 * half + 4, t * P:(t + 1) * P].bitcast(F32),
                                              ALU.subtract).then_inc(s["otl"], 1)

            dve.wait_ge(st["silu_c"], 1)
            dve.tensor_copy(vt[:, 0, :], ps[:, 0, 0:80]).then_inc(st["vec"], 1)
            dve.tensor_copy(vt[:, 1, :], ps[:, 0, 96:176]).then_inc(st["vec"], 1)
            dve.wait_ge(misc_loaded, 64)
            chain.add(dve.tensor_scalar(neg_sink[:], sink[:], -1.0, None, ALU.mult))
            dve.wait_ge(st["vec"], 2)
            dve.wait_ge(mod_used, PER_MOD // 2)
            coefficients(0, 1, st["coef0"])
            dve.wait_ge(const_loaded, 16)
            norm(norms[0], range(TILES), 0, 0, f_tmp, f_mod, st["coef0"], (2, 4))
            for q in range(3):
                lo(WIN0_S + q)
            for n in range(3):
                if n < 2:
                    lo(WIN0_S + 2 * n + 3)
                for t in range(2, 4):
                    dve.wait_ge(*used(WIN0_S + 2 * n + 1))
                    for dst, src in qkv_parts(n, t):
                        ins = dve.tensor_copy(dst, src)
                    ins.then_inc(gemms[0]["dve"], 1)
                if n < 1:
                    lo(WIN0_S + 2 * n + 4)
            dve.wait_ge(gemms[0]["act"], 6)
            dve.wait_ge(gemms[0]["dve"], 6)
            for t in range(TILES):
                sq = qk_t[:, 2 * t:2 * t + 2, :].rearrange("p a b -> p (a b)")[:, 0:QK_E]
                chain.add(dve.tensor_tensor(sq, qkv[:, t, 0:QK_E], qkv[:, t, 0:QK_E], ALU.mult))
            chain.wait()
            for t in range(TILES):
                sq = qk_t[:, 2 * t:2 * t + 2, :].rearrange("p a b -> p (a b)")[:, 0:QK_E]
                ins = dve.tensor_reduce(qk_ssq()[:, 10 * t:10 * t + 10], sq.rearrange("p (h d) -> p h d", d=DH), AX_X, ALU.add)
            ins.then_inc(qk["ssq"], 1)
            dve.wait_ge(qk["root"], 1)
            qk_inv = qk_t[:, 9, 128:168]
            chain.add(dve.reciprocal(qk_inv, qk_root()))
            for t in range(TILES):
                v = qkv[:, t, 0:QK_E].rearrange("p (h d) -> p h d", d=DH)
                chain.wait()
                chain.add(dve.tensor_tensor(v, v, qk_inv[:, 10 * t:10 * t + 10].unsqueeze(2).to_broadcast([P, 10, DH]), ALU.mult))
                chain.wait()
                for i, (h0, h1) in enumerate(((0, 8), (8, 10))):
                    gain = qk_gain[:, i, :].unsqueeze(1).to_broadcast([P, h1 - h0, DH])
                    ins = dve.tensor_tensor(v[:, h0:h1], v[:, h0:h1], gain, ALU.mult)
                    if i == 0 or t < LAT_TILES:
                        chain.add(ins)
                    else:
                        ins.then_inc(qk["ready"], 1)
                if t >= LAT_TILES:
                    continue
                chain.wait()
                for g in range(2):
                    v = qkv[:, t, g * GROUP_E:g * GROUP_E + QK_E].rearrange("p (h c e) -> p h c e", h=10, e=2)
                    rot = qk_t[:, 4 * g:4 * g + 4, :].rearrange("p a b -> p (a b)")[:, 0:4 * 320].rearrange(
                        "p (m h c) -> p m h c", m=4, c=32)
                    cs = [const[:, C_ROPE + t * 64 + 32 * m:C_ROPE + t * 64 + 32 * (m + 1)].unsqueeze(1).to_broadcast([P, 10, 32])
                          for m in range(2)]
                    for m, (e, w) in enumerate(((0, 0), (1, 1), (0, 1), (1, 0))):
                        chain.add(dve.tensor_tensor(rot[:, m], v[:, :, :, e], cs[w], ALU.mult))
                    chain.wait()
                    chain.add(dve.tensor_tensor(v[:, :, :, 0], rot[:, 0], rot[:, 1], ALU.subtract))
                    ins = dve.tensor_tensor(v[:, :, :, 1], rot[:, 2], rot[:, 3], ALU.add)
                    if g == 0:
                        chain.add(ins)
                    else:
                        ins.then_inc(qk["ready"], 1)
            for i in range(1, 10, 2):
                dve.wait_ge(qk["t"], i + 1)
                dve.tensor_scalar(qk_t[:, i, :], ps[:, 1 + i % 6, :], SCALE if i % 5 < 4 else 1.0, None,
                                  ALU.mult).then_inc(qk["dve"], 1)
            dve.wait_ge(mod_used, PER_MOD)
            coefficients(1, 0, st["coef1"])
            chain.wait()
            attention(attns[0], even_plan, qkv_p, qkv_pt)
            for q in range(4):
                lo(WOUT0_S + q)
            resid(resids[0], range(TILES), gates[0], lambda i: ps[:, 2 * i:2 * i + 2, :].rearrange("p b n -> p (b n)"),
                  f_gate, f_tmp)
            for n, (first, tiles) in enumerate(((FFA_S, (0, 1)), (FFB_S, (2, 3)))):
                norm(norms[1 + n], tiles, 0, 1, f_tmp, f_mod, st["coef0"], (0, 2))
                swiglu_all(ffns[n], first, 2, CHUNKS_E, f_silu, f_h, f_hth, f_htl, 0)
                resid(resids[1 + n], tiles, gates[1 + n], lambda i: ps[:, 3 + 2 * i:5 + 2 * i, :].rearrange("p b n -> p (b n)"),
                      f_gate, f_tmp)
            norm(norms[3], range(TILES), 1, 0, f_tmp, f_mod, st["coef1"], (0, 2))
            for q in range(3):
                lo(WIN1_S + q)
            for n in range(6):
                if 2 * n + 3 < 12:
                    lo(WIN1_S + 2 * n + 3)
                for b in range(2, 4):
                    dve.wait_ge(*used(WIN1_S + 2 * n + 1))
                    src = ps[:, (n % 2) * 4 + b, :]
                    if n < 2:
                        ins = dve.tensor_scalar(o_q[:, 4 * n + b, :], src[:, 0:SEQ], SCALE, None, ALU.mult)
                    elif n < 4:
                        ins = dve.tensor_copy(o_k[:, 4 * (n - 2) + b, :], src)
                    else:
                        ins = dve.tensor_copy(o_v[:, b, (n - 4) * N:(n - 3) * N], src)
                    ins.then_inc(gemms[2]["dve"], 1)
                if 2 * n + 4 < 12:
                    lo(WIN1_S + 2 * n + 4)
            attention(attns[1], odd_plan, o_p, o_pt)
            for q in range(4):
                lo(WOUT1_S + q)
            resid(resids[3], (0, 1), gates[3], lambda i: ps[:, 2 * i:2 * i + 2, :].rearrange("p b n -> p (b n)"),
                  m_gate, m_tmp)
            norm(norms[4], (0, 1), 1, 1, m_tmp, m_mod, st["coef1"], (0, 0), (h_hi, h_lo))

            e8 = const[:, C_E8:C_ALL]
            dve.wait_ge(router["logits"], 2)
            chain.add(dve.tensor_copy(logits[:], ps[:, 6, 0:16].rearrange("p (t e) -> p t e", e=EXPERTS)))
            chain.wait()
            for t in range(2):
                chain.add(dve.max(top[:, t, :], logits[:, t, :]))
            chain.wait()
            for t in range(2):
                chain.add(dve.max_index(top_i[:, t, :], top[:, t, :], logits[:, t, :]))
            dve.tensor_tensor(gw[:, :, 0:1], top[:, :, 1:2], top[:, :, 0:1], ALU.subtract).then_inc(router["exp"], 1)
            chain.wait()
            chain.add(dve.tensor_copy(top_f[:], top_i[:]))
            dve.wait_ge(router["ex"], 1)
            chain.add(dve.tensor_scalar(gw[:, :, 2:3], gw[:, :, 1:2], 1.0, None, ALU.add))
            chain.wait()
            chain.add(dve.reciprocal(gw[:, :, 2:3], gw[:, :, 2:3]))
            chain.wait()
            chain.add(dve.tensor_tensor(gw[:, :, 3:4], gw[:, :, 1:2], gw[:, :, 2:3], ALU.mult))
            for t in range(2):
                chain.add(dve.tensor_scalar(hot[:, t, 0, :], e8, top_f[:, t, 0:1], None, ALU.is_equal))
                chain.wait()
                dve.scalar_tensor_tensor(items[:, 2 + t, 0:EXPERTS], e8, top_f[:, t, 1:2], hot[:, t, 0, :], ALU.is_equal,
                                         ALU.add).then_inc(router["sel"], 1)
                chain.add(dve.tensor_scalar(hot[:, t, 1, :], e8, top_f[:, t, 1:2], gw[:, t, 3:4], ALU.is_equal, ALU.mult))
                chain.wait()
                chain.add(dve.scalar_tensor_tensor(items[:, 4 + t, 0:EXPERTS], hot[:, t, 0, :], gw[:, t, 2:3], hot[:, t, 1, :],
                                                   ALU.mult, ALU.add))
            chain.add(dve.tensor_copy(items[:, 6, 0:EXPERTS], e8))
            chain.add(dve.memset(over[:], 0.0))
            dve.wait_ge(router["rank"], 1)
            chain.add(dve.tensor_copy(items[:, 0:2, 0:EXPERTS], ps[:, 6, 16:32].rearrange("p (t e) -> p t e", e=EXPERTS)))
            chain.wait()
            chain.add(dve.tensor_scalar(over[:, 0, 4:12], ps[:, 6, 32:40], float(P), None, ALU.is_gt))
            for step in range(3):
                chain.wait()
                d = 1 << step
                chain.add(dve.tensor_tensor(over[:, step + 1, 4:12], over[:, step, 4:12], over[:, step, 4 - d:12 - d], ALU.add))
            for j in range(4):
                chain.wait()
                chain.add(dve.scalar_tensor_tensor(over_hot[:, j, :], over[:, 3, 4:12], float(j + 1), over[:, 0, 4:12],
                                                   ALU.is_equal, ALU.mult))
                chain.wait()
                chain.add(dve.tensor_tensor(over_tmp[:], items[:, :, 0:EXPERTS],
                                            over_hot[:, j, :].unsqueeze(1).to_broadcast([P, 7, EXPERTS]), ALU.mult))
                chain.wait()
                chain.add(dve.tensor_reduce(items[:, :, EXPERTS + j], over_tmp[:], AX_X, ALU.add))
            chain.wait()
            chain.add(dve.tensor_scalar(items[:, 0:2, EXPERTS:ITEM_COLS], items[:, 0:2, EXPERTS:ITEM_COLS], float(P), None,
                                        ALU.subtract))
            chain.add(dve.tensor_copy(table[0:1, 0:ITEM_COLS], items[0:1, 6, :]))
            dve.tensor_scalar(table[0:1, ITEM_COLS:ITEM_COLS + 1], over[0:1, 3, 11:12], float(EXPERTS), None,
                              ALU.add).then_inc(route_ready, 1)

            iota = const[:, C_IOTA:C_TRI]

            def make_pick(i):
                for t in range(2):
                    ins = dve.tensor_scalar(pick[:, t, :], iota, items[:, t, bass.ds(i, 1)], items[:, 2 + t, bass.ds(i, 1)],
                                            ALU.is_equal, ALU.mult)
                    ins.then_inc(pick_ready, 1)

            def ht(i):
                dve.wait_ge(ht_hi, i + 1)
                dve.tensor_copy(hl[:, :, 0:P], ps[:, 6:8, :].rearrange("p b (k n) -> p (b k) n", n=P)).then_inc(ht_lo, 1)

            make_pick(0)
            dve.wait_ge(gathered, 1)
            ht(0)
            for t in range(2):
                dve.memset(m_acc[:, t, :], 0.0).then_inc(acc_added[t], 1)
            n_items = dve.value_load(table[0:1, ITEM_COLS:ITEM_COLS + 1], min_val=EXPERTS, max_val=EXPERTS + 3)
            with dve.Fori(0, n_items) as i:
                def make_put():
                    for t in range(2):
                        dve.tensor_scalar(put[:, t, :], iota, items[:, t, bass.ds(i, 1)], items[:, 4 + t, bass.ds(i, 1)],
                                          ALU.is_equal, ALU.mult).then_inc(put_ready, 1)
                    make_pick(i + 1)
                swiglu_all(ffns[2], MOE_S, 1, CHUNKS_O, m_silu, m_h, m_hth, m_htl, i * (ITEM_SLOTS // RAW), make_put)
                ht(i + 1)
                for t in range(2):
                    dve.wait_ge(scattered, i * 2 + t + 1)
                    dve.wait_ge(acc_added[t], i + 1)
                    dve.tensor_tensor(m_acc[:, t, :], m_acc[:, t, :], ps[:, 2 * t:2 * t + 2, :].rearrange("p b n -> p (b n)"),
                                      ALU.add).then_inc(acc_added[t], 1)
            resid(resids[4], (0, 1), gates[4], lambda i: m_acc[:, i, :], m_gate, m_tmp)

        @block.tensor
        def _(pe):
            def use(s, turns=0):
                pe.wait_ge(lo_ready, turns * RAW + split_number(s) + 1)

            def product(out, lhs, rhs, start, stop):
                (lh, ll), (rh, rl) = lhs, rhs
                pe.matmul(out, lh, rh, start=start, stop=False)
                pe.matmul(out, ll, rh, start=False, stop=False)
                return pe.matmul(out, lh, rl, start=False, stop=stop)

            def both(s, a0, a1):
                q = split_number(s) % SPLIT
                return whi[:, q, a0:a1], wlo[:, q, a0:a1]

            def tokens(k, a0, a1):
                return hh[:, k, a0:a1], hl[:, k, a0:a1]

            def modulation(first, bank):
                for n in range(PER_MOD // 2):
                    for half in range(2):
                        s = first + 2 * n + half
                        pe.wait_ge(raw_landed[s % RAW], 32 * (s // RAW + 1))
                    for j in range(4):
                        for k in range(KD):
                            s = first + 2 * n + k // 4
                            c0 = (k % 4) * N + j * P
                            ins = pe.matmul(ps[:, bank, 2 * (4 * n + j):2 * (4 * n + j) + 2], raw[:, s % RAW, c0:c0 + P],
                                            silu_c[:, k, :], start=(k == 0), stop=(k == KD - 1))
                    ins.then_inc(mod_used, 1)

            def norm(m, n, banks, xn, after=None):
                for i in range(n):
                    pe.wait_ge(m["xn"], i + 1)
                    if banks[0] == banks[1]:
                        if i >= 1:
                            pe.wait_ge(m["t1"], i)
                    elif i >= 2:
                        pe.wait_ge(m["t1"], i - 1)
                    for k in range(KD):
                        ins = pe.transpose(ps[:, banks[i % 2] + k // 4, (k % 4) * P:(k % 4 + 1) * P],
                                           xn[:, i % 2, k * P:(k + 1) * P], ident)
                    ins.then_inc(m["xt"], 1)

            def broadcast_gate(g, layer, which, streams, bank=6):
                for n, j in enumerate(streams):
                    for k in range(KD):
                        ins = pe.matmul(ps[:, bank - 2 * n + k // 4, (k % 4) * P:(k % 4 + 1) * P],
                                        coef_g[:, layer, which, k, j:j + 1].to_broadcast([P, P]), ident,
                                        start=True, stop=True)
                    ins.then_inc(g["bc"], 1)

            def project(first, chunks, tiles, bank_of, before=None):
                for n in range(chunks):
                    if before is not None:
                        before(n)
                    for half in range(2):
                        s = first + 2 * n + half
                        use(s)
                        for t in tiles:
                            for kk in range(4):
                                k = 4 * half + kk
                                ins = product(ps[:, bank_of(n, t), :], tokens(k, t * P, (t + 1) * P),
                                              both(s, kk * N, (kk + 1) * N), k == 0, k == KD - 1)
                        ins.then_inc(slot_used, 1)

            def swiglu(f, first, m_tiles, chunks, h, hth, htl, y_bank, item_turns=0, in_head=None, y_free=None):
                def gate_up(kk, turns):
                    for half in range(2):
                        s = first + (3 * kk - 1 if kk else 0) + half
                        use(s, turns)
                        for m in range(m_tiles):
                            for k4 in range(4):
                                k = 4 * half + k4
                                ins = product(ps[:, m, :], tokens(k, m * P, (m + 1) * P), both(s, k4 * N, (k4 + 1) * N),
                                              k == 0, k == KD - 1)
                        ins.then_inc(slot_used, 1)

                def turn(kk, turns):
                    pe.wait_ge(f["h"], turns * 2 + kk + 1)
                    for b in range(2):
                        for m in range(m_tiles):
                            c0 = (b * m_tiles + m) * P
                            ins = pe.transpose(ps[:, m_tiles, c0:c0 + P], h[:, m, b * P:(b + 1) * P], ident)
                    ins.then_inc(f["t"], 1)

                def down(kk, s, turns, start=False, stop=False):
                    use(s, turns)
                    pe.wait_ge(f["hi"], turns * 2 + kk + 1)
                    pe.wait_ge(f["lo"], turns * 2 + kk + 1)
                    for m in range(m_tiles):
                        for nh in range(2):
                            for b in range(2):
                                ins = product(ps[:, y_bank + 2 * m + nh, :],
                                              (hth[:, kk % 2, b, m * P:(m + 1) * P], htl[:, kk % 2, b, m * P:(m + 1) * P]),
                                              both(s, b * D + nh * N, b * D + (nh + 1) * N),
                                              start and b == 0, stop and b == 1)
                    ins.then_inc(slot_used, 1)

                def body(kk, turns):
                    gate_up(kk, turns)
                    down(kk - 1, first + 3 * kk + 1, turns, start=(kk == 1))
                    turn(kk, turns)

                gate_up(0, item_turns)
                turn(0, item_turns)
                if in_head is not None:
                    in_head()
                body(1, item_turns)
                with pe.Fori(0, (chunks - 2) // 2) as j:
                    body(2, item_turns + j)
                    body(3, item_turns + j)
                if chunks % 2:
                    body(chunks - 1, item_turns)
                down(chunks - 1, first + 3 * chunks - 1, item_turns, stop=True)

            def attention(s, plan, p, pt):
                pairs = 4 * plan["groups"]

                def scores(at):
                    g = at // 4
                    if at >= 2:
                        pe.wait_ge(s["p"], at - 1)
                    for i in range(2):
                        h = 2 * (at % 4) + i
                        out = ps[:, 2 * (at % 2) + i, 0:nkeys(plan, g)]
                        t = g // 2
                        if plan["even"]:
                            half, col, key0 = h // 4, 5 * (g % 2), 0 if t < LAT_TILES else SEQ
                            rows = slice(DH * half, DH * (half + 1))
                            masked = g % 2 == 1 and t < LAT_TILES
                            ins = pe.matmul(out, qk_t[rows, col + h % 4, t * P:(t + 1) * P], qk_t[rows, col + 4, key0:N],
                                            start=True, stop=not masked)
                            if masked:
                                c0 = (1 - t) * P
                                ins = pe.matmul(out[:, c0:c0 + P], ident, const[:, C_WIN + t * P:C_WIN + (t + 1) * P],
                                                start=False, stop=True)
                        else:
                            h += 8 * (g % 2)
                            rows = slice(DH * (h % 2), DH * (h % 2 + 1))
                            pe.matmul(out, o_q[rows, h // 2, t * P:(t + 1) * P], o_k[rows, h // 2, :], start=True, stop=False)
                            pe.wait_ge(bias["pool"], 2 * at + i + 1)
                            ins = pe.matmul(out[:, 0:SEQ], ident, o_bias[:, (2 * at + i) % 4, :], start=False, stop=True)
                    ins.then_inc(s["s"], 1)

                def turn(at):
                    pe.wait_ge(s["p"], at + 1)
                    if at >= 1:
                        pe.wait_ge(s["pta"], at)
                        pe.wait_ge(s["ptd"], at)
                    for i in range(2):
                        for b in range(nkeys(plan, at // 4) // P):
                            ins = pe.transpose(ps[:, 4 + i, b * P:(b + 1) * P], buf(p, at % 2, i)[:, b * P:(b + 1) * P], ident)
                    ins.then_inc(s["t"], 1)

                def values(at):
                    g = at // 4
                    pe.wait_ge(s["pta"], at + 1)
                    pe.wait_ge(s["ptd"], at + 1)
                    if at % 4 == 0 and g >= 1:
                        pe.wait_ge(s["osb"], g)
                    blocks = nkeys(plan, g) // P
                    for i in range(2):
                        h = 2 * (at % 4) + i
                        for b in range(blocks):
                            tile = TILES - blocks + b
                            if plan["even"]:
                                c0 = GROUP_E * (g % 2) + QK_E + DH * (h // 4)
                                v = qkv[:, tile, c0:c0 + DH]
                            else:
                                v = o_v[:, tile, DH * (h + 8 * (g % 2)):DH * (h + 1 + 8 * (g % 2))]
                            ins = pe.matmul(ps[:, 6, DH * h:DH * (h + 1)], buf(pt, at % 2, i)[:, b * P:(b + 1) * P], v,
                                            start=(b == 0), stop=(b == blocks - 1))
                    if at % 4 == 3:
                        ins.then_inc(s["o"], 1)

                def turn_out(t, half):
                    pe.wait_ge(s["osb"], 2 * t + 2)
                    if 2 * t + half >= 1:
                        pe.wait_ge(s["otl"], 2 * t + half)
                    for k in range(4):
                        c0 = (4 * half + k) * P
                        ins = pe.transpose(ps[:, 7, k * P:(k + 1) * P], o_sb[:, c0:c0 + P], ident)
                    ins.then_inc(s["ot"], 1)

                scores(0)
                for at in range(pairs + 6):
                    if at + 1 < pairs:
                        scores(at + 1)
                    if at < pairs:
                        turn(at)
                    if 1 <= at <= pairs:
                        values(at - 1)
                    for half in range(2):
                        last = at - 3 - half
                        if last >= 0 and last % 8 == 7 and last < pairs:
                            turn_out(last // 8, half)
                pe.wait_ge(s["otl"], plan["groups"])

            pe.wait_ge(vec_loaded, 16 * 12)
            pe.wait_ge(const_loaded, 16)
            pe.transpose(ps[:, 0, 0:96], vrow0[:], ident[0:96, 0:96]).then_inc(st["vt"], 1)
            pe.transpose(ps[:, 0, 96:176], vrow1[:], ident[0:80, 0:80]).then_inc(st["vt"], 1)
            pe.wait_ge(st["silu_c"], 1)
            modulation(M0_S, 1)
            norm(norms[0], TILES, (2, 4), f_tmp)
            pe.wait_ge(norms[0]["lo"], TILES)

            def banks_free0(n):
                if n >= 2:
                    pe.wait_ge(gemms[0]["act"], 2 * (n - 1))
                    pe.wait_ge(gemms[0]["dve"], 2 * (n - 1))

            project(WIN0_S, 3, range(TILES), lambda n, t: (n % 2) * 4 + t, banks_free0)
            pe.wait_ge(gemms[0]["act"], 6)
            modulation(M1_S, 0)
            pe.wait_ge(qk["ready"], TILES)
            for i in range(10):
                g, c = i // 5, i % 5
                if i >= 6:
                    pe.wait_ge(qk["dve"] if i % 2 else qk["act"], (i - 6) // 2 + 1)
                for t in range(TILES):
                    src = qkv[:, t, GROUP_E * g + P * c:GROUP_E * g + P * (c + 1)]
                    ins = pe.transpose(ps[:, 1 + i % 6, t * P:(t + 1) * P], src, ident)
                ins.then_inc(qk["t"], 1)
            pe.wait_ge(qk["act"], 5)
            pe.wait_ge(qk["dve"], 5)
            pe.wait_ge(st["coef1"], 4)
            attention(attns[0], even_plan, qkv_p, qkv_pt)
            broadcast_gate(gates[0], 0, 0, (0, 1))
            pe.wait_ge(gates[0]["sb"], 2)
            project(WOUT0_S, 2, range(TILES), lambda n, t: 2 * t + n)
            for n, (first, stream) in enumerate(((FFA_S, 0), (FFB_S, 1))):
                norm(norms[1 + n], 2, (0, 2), f_tmp)
                broadcast_gate(gates[1 + n], 0, 1, (stream,))
                pe.wait_ge(gates[1 + n]["sb"], 1)
                pe.wait_ge(norms[1 + n]["lo"], 2)
                swiglu(ffns[n], first, 2, CHUNKS_E, f_h, f_hth, f_htl, 3)
            norm(norms[3], TILES, (0, 2), f_tmp)
            pe.wait_ge(norms[3]["lo"], TILES)
            for n in range(6):
                if n >= 2:
                    pe.wait_ge(gemms[2]["act"], 2 * (n - 1))
                    pe.wait_ge(gemms[2]["dve"], 2 * (n - 1))
                for half in range(2):
                    s = WIN1_S + 2 * n + half
                    use(s)
                    for b in range(4):
                        for kk in range(4):
                            k = 4 * half + kk
                            out = ps[:, (n % 2) * 4 + b, :]
                            if n < 4:
                                width = SEQ if n < 2 else N
                                ins = product(out[:, 0:width], both(s, kk * N + b * P, kk * N + (b + 1) * P),
                                              tokens(k, 0, width), k == 0, k == KD - 1)
                            else:
                                ins = product(out, tokens(k, b * P, (b + 1) * P), both(s, kk * N, (kk + 1) * N),
                                              k == 0, k == KD - 1)
                    ins.then_inc(slot_used, 1)
            pe.wait_ge(gemms[2]["act"], 12)
            pe.wait_ge(gemms[2]["dve"], 12)
            attention(attns[1], odd_plan, o_p, o_pt)
            broadcast_gate(gates[3], 1, 0, (0,))
            project(WOUT1_S, 2, range(LAT_TILES), lambda n, t: 2 * t + n)
            m = norms[4]
            norm(m, 2, (0, 0), m_tmp)
            pe.wait_ge(misc_loaded, 64)
            for i in range(2):
                pe.wait_ge(m["t1"], i + 1)
                for k in range(KD):
                    ins = pe.matmul(ps[:, 6, 8 * i:8 * i + 8], m_mod[:, i, k, :], w_router[:, k, :],
                                    start=(k == 0), stop=(k == KD - 1))
                ins.then_inc(router["logits"], 1)
                for k in range(KD):
                    ins = pe.transpose(ps[:, 2 + 2 * i + k // 4, (k % 4) * P:(k % 4 + 1) * P], m_mod[:, i, k, :], ident)
                ins.then_inc(router["back"], 1)
            broadcast_gate(gates[4], 1, 1, (0,), 0)
            pe.wait_ge(router["sel"], 2)
            tri = const[:, C_TRI:C_E8]
            sel = [items[:, 2 + t, 0:EXPERTS] for t in range(2)]
            pe.matmul(ps[:, 6, 16:24], tri, sel[0], start=True, stop=True)
            pe.matmul(ps[:, 6, 24:32], ones[:], sel[0], start=True, stop=False)
            pe.matmul(ps[:, 6, 24:32], tri, sel[1], start=False, stop=True)
            pe.matmul(ps[:, 6, 32:40], ones[:], sel[0], start=True, stop=False)
            pe.matmul(ps[:, 6, 32:40], ones[:], sel[1], start=False, stop=True).then_inc(router["rank"], 1)

            def gather(i):
                pe.wait_ge(pick_ready, i * 2 + 2)
                for part, src in enumerate((h_hi, h_lo)):
                    for k in range(KD):
                        for t in range(2):
                            ins = pe.matmul(ps[:, 4 + 2 * part + k // 4, (k % 4) * P:(k % 4 + 1) * P],
                                            src[:, t, k * P:(k + 1) * P], pick[:, t, :], start=(t == 0), stop=(t == 1))
                ins.then_inc(gathered, 1)

            pe.wait_ge(m["lo"], 2)
            gather(0)
            pe.wait_ge(gates[4]["sb"], 1)
            pe.wait_ge(route_ready, 1)
            n_items = pe.value_load(table[0:1, ITEM_COLS:ITEM_COLS + 1], min_val=EXPERTS, max_val=EXPERTS + 3)
            with pe.Fori(0, n_items) as i:
                pe.wait_ge(ht_hi, i + 1)
                pe.wait_ge(ht_lo, i + 1)
                pe.wait_ge(acc_added[0], i + 1)

                def turn_put():
                    pe.wait_ge(put_ready, i * 2 + 2)
                    for t in range(2):
                        ins = pe.transpose(ps[:, 4, t * P:(t + 1) * P], put[:, t, :], ident)
                    ins.then_inc(put_turned, 1)
                    pe.wait_ge(acc_added[1], i + 1)

                swiglu(ffns[2], MOE_S, 1, CHUNKS_O, m_h, m_hth, m_htl, 2, i * (ITEM_SLOTS // RAW), turn_put)
                pe.wait_ge(put_t_ready, i + 1)
                gather(i + 1)
                pe.wait_ge(y_copied, i + 1)
                for t in range(2):
                    for nh in range(2):
                        ins = pe.matmul(ps[:, 2 * t + nh, :], put_t[:, t, :], m_y[:, nh * N:(nh + 1) * N], start=True, stop=True)
                    ins.then_inc(scattered, 1)


_INS = ["x", "c", "ctx", "c_ctx", "e_w_mod", "e_b_mod", "e_g_pre_mix", "e_g_post_mix", "e_g_pre_ffn", "e_g_post_ffn",
        "e_w_in", "e_w_out", "e_g_q", "e_g_k", "e_sink", "e_w_gate", "e_w_up", "e_w_down", "o_w_mod", "o_b_mod",
        "o_g_pre_mix", "o_g_post_mix", "o_g_pre_ffn", "o_g_post_ffn", "o_w_in", "o_w_out", "o_rpb", "o_w_router",
        "o_w_gate", "o_w_up", "o_w_down"]


def kernel(**inputs):
    import concourse.bacc as _bacc
    from concourse.bass_utils import run_bass_kernel_spmd as _run

    nc = _bacc.Bacc("TRN2", target_bir_lowering=False, num_devices=1)
    arrays, args = {}, {}
    given = {name: np.ascontiguousarray(inputs[name]) for name in _INS}
    given["constants"] = shape_constants()
    for name, x in given.items():
        arrays[f"in_{name}"] = x
        args[name] = nc.dram_tensor(f"in_{name}", x.shape, mybir.dt.from_np(x.dtype), kind="ExternalInput").ap()
    args["out"] = nc.dram_tensor("out_0", (1, SEQ, D), F32, kind="ExternalOutput").ap()
    build(nc, args)
    r = _run(nc, [arrays], core_ids=[0])
    return r.results[0]["out_0"]
```

```python
from contextlib import ExitStack

import concourse.bass as bass
from concourse import mybir
import numpy as np

P = 128
D = 1024
KD = D // P
SEQ = 256
CTX = 256
TILES = (SEQ + CTX) // P
LAT_TILES = SEQ // P
GRID_W = 64
ROWS = SEQ // GRID_W
DH = 64
N_MOD = 6
D_FF = 2816
D_FFE = 3584
EXPERTS = 8
QKV_E = 1536
GROUP_E = QKV_E // 2
QK_E = 10 * DH
HEADS_O = 16
NA_ROWS = 8
NA_COLS = 16
RPB_W = 2 * NA_COLS - 1
RPB_R = 2 * NA_ROWS - 1
ROW_SHIFTS = 2 * ROWS - 1
EPS = 1e-6
SCALE = DH ** -0.5
NEG = -1e30
WINDOW = 128

EARLY_MOD = 4
N = 512
SLOT = 4 * N
RAW = 6
SPLIT = 3
FFC = 256
CHUNKS_E = D_FF // FFC
CHUNKS_O = D_FFE // FFC
ITEM_SLOTS = 3 * CHUNKS_O
ITEM_COLS = 12
PER_MOD = 2 * (N_MOD * D // N)

M0_S = 0
WIN0_S = M0_S + PER_MOD
M1_S = WIN0_S + 6
WOUT0_S = M1_S + PER_MOD
FFA_S = WOUT0_S + 4
FFB_S = FFA_S + 3 * CHUNKS_E
WIN1_S = FFB_S + 3 * CHUNKS_E
WOUT1_S = WIN1_S + 12
MOE_S = WOUT1_S + 4


ALU = mybir.AluOpType
ACT = mybir.ActivationFunctionType
F32 = mybir.dt.float32
F32R = mybir.dt.float32r
I32 = mybir.dt.int32
U32 = mybir.dt.uint32
AX_X = mybir.AxisListType.X

C_IDENT = 0
C_WIN = C_IDENT + P
C_ROPE = C_WIN + 2 * P
C_COL = C_ROPE + 4 * 32
C_IOTA = C_COL + GRID_W
C_TRI = C_IOTA + P
C_E8 = C_TRI + P
C_ALL = C_E8 + EXPERTS


def shape_constants():
    out = np.zeros((P, C_ALL), np.float32)
    i = np.arange(P)
    out[:, C_IDENT:C_WIN] = np.eye(P)
    for t in range(2):
        dist = np.abs((t * P + i)[:, None] - ((1 - t) * P + i)[None, :])
        out[:, C_WIN + t * P:C_WIN + (t + 1) * P] = np.where(dist <= WINDOW, 0.0, NEG)
    half = DH // 2
    freqs = (np.float32(10000.0) ** (-np.arange(0, half, 2, dtype=np.float32) / np.float32(half))).astype(np.float32)
    for t in range(2):
        token = t * P + i
        row, col = (token // GRID_W).astype(np.float32), (token % GRID_W).astype(np.float32)
        ang = np.concatenate([row[:, None] * freqs, col[:, None] * freqs], axis=-1).astype(np.float32)
        out[:, C_ROPE + t * 64:C_ROPE + t * 64 + 32] = np.cos(ang)
        out[:, C_ROPE + t * 64 + 32:C_ROPE + t * 64 + 64] = np.sin(ang)
    qc, kc = (i % GRID_W)[:, None], np.arange(GRID_W)[None, :]
    first = np.clip(qc - NA_COLS // 2, 0, GRID_W - NA_COLS)
    out[:, C_COL:C_IOTA] = np.where((kc >= first) & (kc < first + NA_COLS), 0.0, NEG)
    out[:, C_IOTA:C_TRI] = i[None, :]
    out[:, C_TRI:C_E8] = i[:, None] < i[None, :]
    out[:, C_E8:] = np.arange(EXPERTS)[None, :]
    return out


class Chain:

    def __init__(self, eng, sem):
        self.eng, self.sem, self.n = eng, sem, 0

    def add(self, ins):
        ins.then_inc(self.sem, 1)
        self.n = self.n + 1

    def wait(self):
        self.eng.wait_ge(self.sem, self.n)


def build(nc, a):
    with ExitStack() as ctx:
        def sem(name):
            return ctx.enter_context(nc.semaphore(name))

        def sems(prefix, names):
            return {n: sem(f"{prefix}_{n}") for n in names.split()}

        def sb(name, shape, dt=F32, scope=ctx):
            return scope.enter_context(nc.sbuf_tensor(name, shape, dt))

        raw = sb("raw", [P, RAW, SLOT])
        whi = sb("whi", [P, SPLIT, SLOT], F32R)
        wlo = sb("wlo", [P, SPLIT, SLOT], F32R)
        rpb_sb = sb("rpb_sb", [HEADS_O * ROW_SHIFTS, P])
        x_lat = sb("x_lat", [P, LAT_TILES, D])
        hh = sb("hh", [P, KD, N], F32R)
        hl = sb("hl", [P, KD, N], F32R)
        o_sb = sb("o_sb", [P, D])
        const = sb("const", [P, C_ALL])
        vt = sb("vt", [P, 2, 80])
        silu_c = sb("silu_c", [P, KD, 2])
        mod = sb("mod", [P, 2, N_MOD * KD, 2])
        coef_a = sb("coef_a", [P, 2, 2, KD, 2])
        coef_g = sb("coef_g", [P, 2, 2, KD, 2])
        qk_gain = sb("qk_gain", [P, 2, DH])
        sink = sb("sink", [P, 8])
        neg_sink = sb("neg_sink", [P, 8])
        ones = sb("ones", [P, P])
        eps = sb("eps", [P, 1])
        ssq = sb("ssq", [P, 8])
        root = sb("root", [P, 8])
        rstd = sb("rstd", [P, 8])
        w_router = sb("w_router", [P, KD, EXPERTS])
        neg_max = sb("neg_max", [P, 2, 8])
        sink_arg = sb("sink_arg", [P, 2, 8])
        sink_exp = sb("sink_exp", [P, 2, 8])
        exp_sum = sb("exp_sum", [P, 2, 8])
        exp_inv = sb("exp_inv", [P, 2, 8])

        with ExitStack() as even:
            x_ctx = sb("x_ctx", [P, 2, D], F32, even)
            with ExitStack() as s:
                vrow0 = sb("vrow0", [96, P], F32, s)
                vrow1 = sb("vrow1", [80, P], F32, s)
            with ExitStack() as s:
                qkv = sb("qkv", [P, TILES, QKV_E], F32, s)
                qk_t = sb("qk_t", [P, 10, N], F32, s)
                mod_row = sb("mod_row", [P, 2, N], F32, s)
            with ExitStack() as s:
                f_gate = sb("f_gate", [P, 2, D], F32, s)
                f_tmp = sb("f_tmp", [P, 2, D], F32, s)
                f_mod = sb("f_mod", [P, 2, KD, P], F32, s)
                f_silu = sb("f_silu", [P, 2, FFC], F32, s)
                f_h = sb("f_h", [P, 2, FFC], F32, s)
                f_hth = sb("f_hth", [P, 2, 2, 2 * P], F32R, s)
                f_htl = sb("f_htl", [P, 2, 2, 2 * P], F32R, s)
        with ExitStack() as s:
            o_q = sb("o_q", [P, 8, SEQ], F32, s)
            o_k = sb("o_k", [P, 8, N], F32, s)
            o_v = sb("o_v", [P, TILES, D], F32, s)
            o_bias = sb("o_bias", [P, 4, SEQ], F32, s)
            o_p = sb("o_p", [P, 2, 2, N], F32, s)
            o_pt = sb("o_pt", [P, 2, 2, N], F32, s)
        with ExitStack() as s:
            m_gate = sb("m_gate", [P, 1, D], F32, s)
            m_tmp = sb("m_tmp", [P, 2, D], F32, s)
            m_mod = sb("m_mod", [P, 2, KD, P], F32, s)
            m_acc = sb("m_acc", [P, 2, D], F32, s)
            h_hi = sb("h_hi", [P, 2, D], F32R, s)
            h_lo = sb("h_lo", [P, 2, D], F32R, s)
            m_silu = sb("m_silu", [P, 1, FFC], F32, s)
            m_h = sb("m_h", [P, 1, FFC], F32, s)
            m_hth = sb("m_hth", [P, 2, 2, P], F32R, s)
            m_htl = sb("m_htl", [P, 2, 2, P], F32R, s)
            m_y = m_tmp[:, 0, :]
            pick = sb("pick", [P, 2, P], F32R, s)
            put = sb("put", [P, 2, P], F32, s)
            put_t = sb("put_t", [P, 2, P], F32, s)
            logits = sb("logits", [P, 2, EXPERTS], F32, s)
            top = sb("top", [P, 2, 8], F32, s)
            top_i = sb("top_i", [P, 2, 8], U32, s)
            top_f = sb("top_f", [P, 2, 8], F32, s)
            gw = sb("gw", [P, 2, 4], F32, s)
            hot = sb("hot", [P, 2, 2, EXPERTS], F32, s)
            items = sb("items", [P, 7, ITEM_COLS], F32, s)
            over = sb("over", [P, 4, 12], F32, s)
            over_hot = sb("over_hot", [P, 4, EXPERTS], F32, s)
            over_tmp = sb("over_tmp", [P, 7, EXPERTS], F32, s)
            table = sb("table", [1, 16], I32, s)

        ps = ctx.enter_context(nc.psum_tensor("ps", [P, 8, N], F32))
        bias_dram = nc.dram_tensor("bias_scratch", [HEADS_O * ROW_SHIFTS, GRID_W, P], F32, kind="Internal").ap()

        ident = const[:, C_IDENT:C_WIN]

        def x_tile(t):
            return x_lat[:, t, :] if t < LAT_TILES else x_ctx[:, t - LAT_TILES, :]

        x_loaded, const_loaded, vec_loaded, misc_loaded = (sem(n) for n in
                                                           ("x_loaded", "const_loaded", "vec_loaded", "misc_loaded"))
        raw_landed = [sem(f"raw_landed{i}") for i in range(RAW)]
        hi_ready, lo_ready, slot_used = (sem(n) for n in ("hi_ready", "lo_ready", "slot_used"))
        mods = [sems(f"mod{i}", "bc_hi bc_lo row turned taken") for i in range(2)]
        act_chain, dve_chain = sem("act_chain"), sem("dve_chain")
        st = sems("set", "vt silu_c vec coef0 coef1 pool")
        norms = [sems(f"norm{i}", "root xn xt t1 hi lo") for i in range(5)]
        router = sems("router", "logits back exp ex sel rank")
        gates = [sems(f"gate{i}", "bc sb") for i in range(5)]
        resids = [sems(f"resid{i}", "root x") for i in range(5)]
        gemms = [sems(f"gemm{i}", "act dve") for i in range(2)]
        ffns = [sems(f"ffn{i}", "silu h t hi lo") for i in range(3)]
        attns = [sems(f"attn{i}", "s nm p t pta ptd o osb ot oth otl") for i in range(2)]
        qk = sems("qk", "ssq root ready t act dve")
        bias = sems("bias", "rows wrote pool")
        bias_landed = [sem(f"bias_landed{i}") for i in range(4)]
        route_ready, pick_ready, gathered, ht_hi, ht_lo = (sem(n) for n in
                                                           ("route_ready", "pick_ready", "gathered", "ht_hi", "ht_lo"))
        put_ready, put_turned, put_t_ready, y_copied, scattered = (
            sem(n) for n in ("put_ready", "put_turned", "put_t_ready", "y_copied", "scattered"))
        acc_added = [sem(f"acc_added{t}") for t in range(2)]
        out_stored = sem("out_stored")

        def used(s, turns=0):
            return slot_used, turns * RAW + s + 1

        even_plan = {"groups": 2 * TILES, "even": True}
        odd_plan = {"groups": 4, "even": False}
        qkv_p = [[qkv[:, b, i * GROUP_E:i * GROUP_E + N] for i in range(2)] for b in range(2)]
        qkv_pt = [[qkv[:, 2 + b, i * GROUP_E:i * GROUP_E + N] for i in range(2)] for b in range(2)]

        def qkv_parts(n, t):
            src = ps[:, (n % 2) * 4 + t, :]
            queries = [qkv[:, t, GROUP_E * g:GROUP_E * g + 8 * DH].rearrange("p (c a d) -> p a c d", a=2, d=DH)
                       for g in range(2)]
            if n == 0:
                return [(queries[0], src.rearrange("p (a c d) -> p a c d", a=2, d=DH))]
            if n == 1:
                return [(qkv[:, t, N:GROUP_E], src[:, 0:256]),
                        (queries[1][:, 0], src[:, 256:512].rearrange("p (c d) -> p c d", d=DH))]
            return [(queries[1][:, 1], src[:, 0:256].rearrange("p (c d) -> p c d", d=DH)),
                    (qkv[:, t, GROUP_E + 8 * DH:QKV_E], src[:, 256:512])]

        def nkeys(plan, g):
            return N if not plan["even"] or g // 2 < LAT_TILES else CTX

        def has_sink(plan, g):
            return plan["even"] and g % 2 == 1

        def buf(p, b, i):
            return p[b][i] if isinstance(p, list) else p[:, b, i, :]

        def qk_ssq():
            return qk_t[:, 9, 0:40]

        def qk_root():
            return qk_t[:, 9, 64:104]

        def attention_act(act, s, plan, p, pt, mod_copy, split_to):
            pairs = 4 * plan["groups"]
            for at in range(pairs + 6):
                if at < pairs:
                    g, n = at // 4, nkeys(plan, at // 4)
                    act.wait_ge(s["nm"], at + 1)
                    if at >= 2:
                        act.wait_ge(s["t"], at - 1)
                    for i in range(2):
                        h = 2 * (at % 4) + i
                        ins = act.activation(buf(p, at % 2, i)[:, 0:n], ps[:, 2 * (at % 2) + i, 0:n], ACT.Exp,
                                             bias=neg_max[:, g % 2, h:h + 1], accum_out=exp_sum[:, g % 2, h:h + 1])
                    if has_sink(plan, g):
                        h = 2 * (at % 4)
                        ins = act.activation(sink_exp[:, g % 2, h:h + 2], sink_arg[:, g % 2, h:h + 2], ACT.Exp)
                    ins.then_inc(s["p"], 1)
                if 1 <= at <= pairs:
                    n = nkeys(plan, (at - 1) // 4)
                    act.wait_ge(s["t"], at)
                    act.activation(buf(pt, (at - 1) % 2, 0)[:, 0:n], ps[:, 4, 0:n], ACT.Copy).then_inc(s["pta"], 1)
                if plan["even"] and at < pairs and at % 4 == 1:
                    mod_copy(mods[1], 1, EARLY_MOD + at // 4, 7)
                    split_to(M1_S + 2 * (EARLY_MOD + at // 4) + 3)
                if plan["even"] and at < pairs and at % 4 == 2:
                    split_to(M1_S + 2 * (EARLY_MOD + at // 4) + 4)
                for half in range(2):
                    last = at - 4 - half
                    if last >= 0 and last % 8 == 7 and last < pairs:
                        t = last // 8
                        act.wait_ge(s["ot"], 2 * t + half + 1)
                        act.activation(hh[:, 4 * half:4 * half + 4, t * P:(t + 1) * P],
                                       ps[:, 7, :].rearrange("p (k n) -> p k n", n=P), ACT.Copy).then_inc(s["oth"], 1)

        block = ctx.enter_context(nc.Block())

        @block.sync
        def _(sp):
            sp.dma_start(const[:], a["constants"]).then_inc(const_loaded, 16)
            for layer, rows in (("e", vrow0), ("o", vrow1)):
                sp.dma_start(rows[0:48, :], a[f"{layer}_b_mod"].rearrange("o (r p) -> (o r) p", p=P)).then_inc(vec_loaded, 16)
                for i, g in enumerate(("pre_mix", "post_mix", "pre_ffn", "post_ffn")):
                    sp.dma_start(rows[48 + 8 * i:56 + 8 * i, :],
                                 a[f"{layer}_g_{g}"].rearrange("o (r p) -> (o r) p", p=P)).then_inc(vec_loaded, 16)
            sp.dma_start(vrow0[80:88, :], a["c"].rearrange("o (r p) -> (o r) p", p=P)).then_inc(vec_loaded, 16)
            sp.dma_start(vrow0[88:96, :], a["c_ctx"].rearrange("(r p) -> r p", p=P)).then_inc(vec_loaded, 16)
            sp.dma_start(x_lat[:], a["x"].rearrange("o (t p) d -> p (o t) d", p=P)).then_inc(x_loaded, 16)
            sp.dma_start(x_ctx[:], a["ctx"].rearrange("o (t p) d -> p (o t) d", p=P)).then_inc(x_loaded, 16)

            def fill(s, pairs, turns=0):
                before = s - RAW
                if before >= 0:
                    sp.wait_ge(lo_ready, turns * RAW + before + 1)
                for dst, src in pairs:
                    sp.dma_start(dst, src).then_inc(raw_landed[s % RAW], 16)

            def fill_projection(s, w, n, half):
                dst = raw[:, s % RAW, :].rearrange("p (k n) -> p k n", n=N)
                src = w.rearrange("o (k p) n -> p (o k) n", p=P)[:, 4 * half:4 * half + 4, n * N:(n + 1) * N]
                fill(s, [(dst[:, 0:2], src[:, 0:2]), (dst[:, 2:4], src[:, 2:4])])

            def fill_all(first, w, chunks):
                for n in range(chunks):
                    for half in range(2):
                        fill_projection(first + 2 * n + half, w, n, half)

            def swiglu_stream(first, chunks, wg, wu, wd, expert_k, expert_b, item_turns):
                def gu(s, kk, turns, j):
                    for half in range(2):
                        dst = raw[:, (s + half) % RAW, :].rearrange("p (k n) -> p k n", n=N)
                        k0 = bass.ds(expert_k + 4 * half, 4)
                        c0 = bass.ds(j * 2 * FFC + kk * FFC, FFC)
                        fill(s + half, [(dst[:, :, 0:FFC], wg[:, k0, c0]), (dst[:, :, FFC:N], wu[:, k0, c0])], turns)

                def down(s, kk, turns, j):
                    dst = raw[:, s % RAW, :].rearrange("p (b n) -> p b n", n=D)
                    b0 = expert_b + j * 4 + 2 * kk
                    fill(s, [(dst[:, b:b + 1], wd[:, bass.ds(b0 + b, 1)]) for b in range(2)], turns)

                gu(first, 0, item_turns, 0)

                def body(kk, turns, j):
                    gu(first + 3 * kk - 1, kk, turns, j)
                    down(first + 3 * kk + 1, kk - 1, turns, j)

                body(1, item_turns, 0)
                with sp.Fori(0, (chunks - 2) // 2) as j:
                    body(2, item_turns + j, j)
                    body(3, item_turns + j, j)
                if chunks % 2:
                    body(chunks - 1, item_turns, 0)
                down(first + 3 * chunks - 1, chunks - 1, item_turns, 0)

            fill_all(M0_S, a["e_w_mod"], PER_MOD // 2)
            fill_all(WIN0_S, a["e_w_in"], 3)
            fill_all(M1_S, a["o_w_mod"], PER_MOD // 2)
            fill_all(WOUT0_S, a["e_w_out"], 2)
            eg, eu = (a[n].rearrange("o (k p) f -> p (o k) f", p=P) for n in ("e_w_gate", "e_w_up"))
            ed = a["e_w_down"].rearrange("o (b p) n -> p (o b) n", p=P)
            for first in (FFA_S, FFB_S):
                swiglu_stream(first, CHUNKS_E, eg, eu, ed, 0, 0, 0)
            fill_all(WIN1_S, a["o_w_in"], 6)
            fill_all(WOUT1_S, a["o_w_out"], 2)

            og, ou = (a[n].rearrange("o e (k p) f -> p (o e k) f", p=P) for n in ("o_w_gate", "o_w_up"))
            od = a["o_w_down"].rearrange("o e (b p) n -> p (o e b) n", p=P)
            turns_per_item = ITEM_SLOTS // RAW
            with sp.Fori(0, EXPERTS - 1) as i:
                swiglu_stream(MOE_S, CHUNKS_O, og, ou, od, i * KD, i * (D_FFE // P), i * turns_per_item)
            sp.wait_ge(route_ready, 1)
            n_items = sp.value_load(table[0:1, ITEM_COLS:ITEM_COLS + 1], min_val=EXPERTS, max_val=EXPERTS + 3)
            with sp.Fori(EXPERTS - 1, n_items) as i:
                e = sp.value_load(table[0:1, bass.ds(i, 1)], min_val=0, max_val=EXPERTS - 1)
                swiglu_stream(MOE_S, CHUNKS_O, og, ou, od, e * KD, e * (D_FFE // P), i * turns_per_item)
            for ahead in range(2):
                dst = raw[:, (MOE_S + ahead) % RAW, :].rearrange("p (k n) -> p k n", n=N)
                fill(MOE_S + ahead, [(dst[:, 0:2], og[:, 0:2, 0:N]), (dst[:, 2:4], og[:, 2:4, 0:N])], n_items * turns_per_item)
            sp.wait_ge(resids[4]["x"], 2)
            sp.dma_start(a["out"].rearrange("o (t p) d -> p (o t) d", p=P), x_lat[:]).then_inc(out_stored, 16)
            sp.wait_ge(out_stored, 16)

        @block.gpsimd
        def _(pool):
            pool.memset(ones[:], 1.0).then_inc(st["pool"], 1)
            pool.memset(eps[:], EPS).then_inc(st["pool"], 1)
            pool.memset(rpb_sb[:], 0.0).then_inc(st["pool"], 1)
            for i, name in enumerate(("e_g_q", "e_g_k")):
                pool.dma_start(qk_gain[:, i, :], bass.AP(a[name].tensor, 0, [[0, P], [1, DH]])).then_inc(misc_loaded, 16)
            pool.dma_start(sink[:], bass.AP(a["e_sink"].tensor, 0, [[0, P], [1, 8]])).then_inc(misc_loaded, 16)
            pool.dma_start(w_router[:], a["o_w_router"].rearrange("o (k p) e -> p (o k) e", p=P)).then_inc(misc_loaded, 16)
            pool.wait_ge(st["pool"], 3)
            for h in range(HEADS_O):
                r0 = NA_ROWS - ROWS
                pool.dma_start(rpb_sb[h * ROW_SHIFTS:(h + 1) * ROW_SHIFTS, GRID_W - NA_COLS:GRID_W - NA_COLS + RPB_W],
                               a["o_rpb"][0, h, r0:r0 + ROW_SHIFTS, :]).then_inc(bias["rows"], 16)
            pool.wait_ge(bias["rows"], 16 * HEADS_O)
            n_rows = HEADS_O * ROW_SHIFTS
            pool.dma_start(bass.AP(bias_dram.tensor, 0, [[GRID_W * P, n_rows], [P, GRID_W], [1, P]]),
                           bass.AP(rpb_sb, 0, [[P, n_rows], [0, GRID_W], [1, P]])).then_inc(bias["wrote"], 16)
            pool.wait_ge(bias["wrote"], 16)
            def mask_unit(u):
                pool.wait_ge(bias_landed[u % 4], 32 * (u // 4 + 1))
                v = o_bias[:, u % 4, :].rearrange("p (k c) -> p k c", c=GRID_W)
                m = bass.AP(const, C_COL, [[C_ALL, P], [0, ROWS], [1, GRID_W]])
                pool.tensor_tensor(v, v, m, ALU.add).then_inc(bias["pool"], 1)

            pool.wait_ge(const_loaded, 16)
            pool.wait_ge(norms[3]["lo"], TILES)
            for u in range(2 * HEADS_O):
                t, h = u // HEADS_O, u % HEADS_O
                if u >= 4:
                    pool.wait_ge(attns[1]["s"], (u - 4) // 2 + 1)
                for r2 in range(2):
                    row = 2 * t + r2
                    src = bass.AP(bias_dram.tensor, (h * ROW_SHIFTS + ROWS - 1 - row) * GRID_W * P + GRID_W - 1,
                                  [[P - 1, GRID_W], [GRID_W * P, ROWS], [1, GRID_W]])
                    pool.dma_start(o_bias[r2 * GRID_W:(r2 + 1) * GRID_W, u % 4, :].rearrange("p (k c) -> p k c", c=GRID_W),
                                   src).then_inc(bias_landed[u % 4], 16)
                if u >= 1:
                    mask_unit(u - 1)
            mask_unit(2 * HEADS_O - 1)

        @block.scalar
        def _(act):
            chain = Chain(act, act_chain)
            ahead = [0]

            def hi(s, turns=0):
                act.wait_ge(raw_landed[s % RAW], turns * 32 + 32 * (s // RAW + 1))
                if s >= SPLIT:
                    act.wait_ge(*used(s - SPLIT, turns))
                act.activation(whi[:, s % SPLIT, :], raw[:, s % RAW, :], ACT.Copy).then_inc(hi_ready, 1)

            def split_to(s):
                while ahead[0] <= s:
                    hi(ahead[0])
                    ahead[0] += 1

            def spread_conditioning(m):
                act.activation(hh[:, :, 3 * P:4 * P].rearrange("p k (j n) -> p k j n", j=2),
                               silu_c[:].unsqueeze(3).to_broadcast([P, KD, 2, P // 2]), ACT.Copy).then_inc(m["bc_hi"], 1)

            def mod_copy(m, layer, n, bank):
                act.wait_ge(*used((M1_S if layer else M0_S) + 2 * n + 1))
                if n >= 2:
                    act.wait_ge(m["turned"], n - 1)
                act.activation(mod_row[:, n % 2, :], ps[:, bank, :], ACT.Copy).then_inc(m["row"], 1)

            def norm(m, tiles, junk, mod_tile, dst=None):
                for i, t in enumerate(tiles):
                    if i:
                        chain.wait()
                    chain.add(act.activation(junk, x_tile(t), ACT.Square, accum_out=ssq[:, i:i + 1]))
                chain.wait()
                act.activation(root[:, 0:len(tiles)], ssq[:, 0:len(tiles)], ACT.Sqrt, scale=1.0 / D,
                               bias=eps[:, 0:1]).then_inc(m["root"], 1)
                for i, t in enumerate(tiles):
                    if dst is None:
                        act.wait_ge(m["t1"], i + 1)
                        act.activation(hh[:, :, i * P:(i + 1) * P], mod_tile[:, i % 2], ACT.Copy).then_inc(m["hi"], 1)
                    else:
                        act.wait_ge(router["back"], i + 1)
                        act.activation(dst[:, i, :], ps[:, 2 + 2 * i:4 + 2 * i, :].rearrange("p b n -> p (b n)"),
                                       ACT.Copy).then_inc(m["hi"], 1)

            def gate(g, dst, n, bank=6):
                for j in range(n):
                    act.wait_ge(g["bc"], j + 1)
                    act.activation(dst[:, j, :], ps[:, bank - 2 * j:bank + 2 - 2 * j, :].rearrange("p b n -> p (b n)"),
                                   ACT.Copy).then_inc(g["sb"], 1)

            def resid(r, tiles, y_ready, y_of, junk):
                for i, t in enumerate(tiles):
                    act.wait_ge(*y_ready(i))
                    if i >= 1:
                        act.wait_ge(r["x"], i)
                    chain.add(act.activation(junk[:, i % 2, :], y_of(i), ACT.Square, accum_out=ssq[:, i:i + 1]))
                    chain.wait()
                    act.activation(root[:, i:i + 1], ssq[:, i:i + 1], ACT.Sqrt, scale=1.0 / D,
                                   bias=eps[:, 0:1]).then_inc(r["root"], 1)

            def swiglu(f, first, m_tiles, silu, hth):
                def silu_chunk(kk, turns):
                    act.wait_ge(*used(first + (3 * kk if kk else 1), turns))
                    act.activation(silu[:], ps[:, 0:m_tiles, 0:FFC], ACT.Silu).then_inc(f["silu"], 1)

                def turned(kk, turns):
                    act.wait_ge(f["t"], turns * 2 + kk + 1)
                    cols = 2 * m_tiles * P
                    act.activation(hth[:, kk % 2].rearrange("p b n -> p (b n)"), ps[:, m_tiles, 0:cols],
                                   ACT.Copy).then_inc(f["hi"], 1)

                def body(kk, turns):
                    if kk:
                        hi(first + 3 * kk + 1, turns)
                    hi(first + 3 * kk + 2, turns)
                    silu_chunk(kk, turns)
                    hi(first + 3 * kk + 3, turns)
                    turned(kk, turns)
                return body

            def swiglu_all(f, first, m_tiles, chunks, silu, hth, item_turns, in_head=None):
                body = swiglu(f, first, m_tiles, silu, hth)
                body(0, item_turns)
                if in_head is not None:
                    in_head()
                body(1, item_turns)
                with act.Fori(0, (chunks - 2) // 2) as j:
                    body(2, item_turns + j)
                    body(3, item_turns + j)
                if chunks % 2:
                    body(chunks - 1, item_turns)
                hi(first + 3 * chunks + 1, item_turns)

            act.wait_ge(st["vt"], 2)
            act.activation(silu_c[:], ps[:, 0, 80:96].rearrange("p (j k) -> p k j", j=2), ACT.Silu).then_inc(st["silu_c"], 1)
            act.wait_ge(st["silu_c"], 1)
            spread_conditioning(mods[0])
            for n in range(PER_MOD // 2):
                split_to(M0_S + 2 * n + 3)
                mod_copy(mods[0], 0, n, n % 2)
                split_to(M0_S + 2 * n + 4)
            act.wait_ge(x_loaded, 32)
            act.wait_ge(st["pool"], 3)
            norm(norms[0], range(TILES), o_sb[:], f_mod)
            for n in range(3):
                split_to(WIN0_S + 2 * n + 3)
                for t in range(2):
                    act.wait_ge(*used(WIN0_S + 2 * n + 1))
                    for dst, src in qkv_parts(n, t):
                        ins = act.activation(dst, src, ACT.Copy)
                    ins.then_inc(gemms[0]["act"], 1)
                split_to(WIN0_S + 2 * n + 4)
            spread_conditioning(mods[1])
            act.wait_ge(qk["ssq"], 1)
            act.activation(qk_root(), qk_ssq(), ACT.Sqrt, scale=1.0 / DH, bias=eps[:, 0:1]).then_inc(qk["root"], 1)
            for n in range(EARLY_MOD):
                mod_copy(mods[1], 1, n, 0)
                split_to(M1_S + 2 * n + 4)
            for i in range(0, 10, 2):
                act.wait_ge(qk["t"], i + 1)
                act.activation(qk_t[:, i, :], ps[:, 1 + i % 6, :], ACT.Copy,
                               scale=SCALE if i % 5 < 4 else 1.0).then_inc(qk["act"], 1)
            attention_act(act, attns[0], even_plan, qkv_p, qkv_pt, mod_copy, split_to)
            gate(gates[0], f_gate, 2)
            split_to(WOUT0_S + 5)
            resid(resids[0], range(TILES), lambda i: used(WOUT0_S + 3), lambda i: ps[:, 2 * i:2 * i + 2, :].rearrange("p b n -> p (b n)"), f_tmp)
            for n, (first, tiles) in enumerate(((FFA_S, (0, 1)), (FFB_S, (2, 3)))):
                act.wait_ge(resids[n]["x"], 4 if n == 0 else 2)
                norm(norms[1 + n], tiles, f_tmp[:, 0, :], f_mod)
                gate(gates[1 + n], f_gate, 1)
                swiglu_all(ffns[n], first, 2, CHUNKS_E, f_silu, f_hth, 0)
                ahead[0] = first + 3 * CHUNKS_E + 2
                resid(resids[1 + n], tiles, lambda i, first=first: used(first + 3 * CHUNKS_E - 1),
                      lambda i: ps[:, 3 + 2 * i:5 + 2 * i, :].rearrange("p b n -> p (b n)"), f_tmp)
            act.wait_ge(resids[2]["x"], 2)
            norm(norms[3], range(TILES), f_tmp[:, 0, :], f_mod)
            for n in range(6):
                split_to(WIN1_S + 2 * n + 3)
                for b in range(2):
                    act.wait_ge(*used(WIN1_S + 2 * n + 1))
                    src = ps[:, (n % 2) * 4 + b, :]
                    if n < 2:
                        ins = act.activation(o_q[:, 4 * n + b, :], src[:, 0:SEQ], ACT.Copy, scale=SCALE)
                    elif n < 4:
                        ins = act.activation(o_k[:, 4 * (n - 2) + b, :], src, ACT.Copy)
                    else:
                        ins = act.activation(o_v[:, b, (n - 4) * N:(n - 3) * N], src, ACT.Copy)
                    ins.then_inc(gemms[1]["act"], 1)
                split_to(WIN1_S + 2 * n + 4)
            attention_act(act, attns[1], odd_plan, o_p, o_pt, mod_copy, split_to)
            gate(gates[3], m_gate, 1)
            split_to(WOUT1_S + 5)
            resid(resids[3], (0, 1), lambda i: used(WOUT1_S + 3), lambda i: ps[:, 2 * i:2 * i + 2, :].rearrange("p b n -> p (b n)"), m_tmp)
            act.wait_ge(resids[3]["x"], 2)
            norm(norms[4], (0, 1), m_tmp[:, 0, :], m_mod, h_hi)
            gate(gates[4], m_gate, 1, 0)
            act.wait_ge(router["exp"], 1)
            act.activation(gw[:, :, 1:2], gw[:, :, 0:1], ACT.Exp).then_inc(router["ex"], 1)

            def ht(i):
                act.wait_ge(gathered, i + 1)
                act.activation(hh[:, :, 0:P], ps[:, 4:6, :].rearrange("p b (k n) -> p (b k) n", n=P), ACT.Copy).then_inc(ht_hi, 1)

            ht(0)
            act.wait_ge(route_ready, 1)
            n_items = act.value_load(table[0:1, ITEM_COLS:ITEM_COLS + 1], min_val=EXPERTS, max_val=EXPERTS + 3)
            with act.Fori(0, n_items) as i:
                def put_turn():
                    act.wait_ge(put_turned, i + 1)
                    act.activation(put_t[:].rearrange("p t n -> p (t n)"), ps[:, 4, 0:2 * P], ACT.Copy).then_inc(put_t_ready, 1)
                swiglu_all(ffns[2], MOE_S, 1, CHUNKS_O, m_silu, m_hth, i * (ITEM_SLOTS // RAW), put_turn)
                act.wait_ge(*used(MOE_S + ITEM_SLOTS - 1, i * (ITEM_SLOTS // RAW)))
                act.activation(m_y, ps[:, 2:4, :].rearrange("p b n -> p (b n)"), ACT.Copy).then_inc(y_copied, 1)
                ht(i + 1)
            resid(resids[4], (0, 1), lambda i: (acc_added[1], n_items + 1), lambda i: m_acc[:, i, :], m_tmp)

        @block.vector
        def _(dve):
            chain = Chain(dve, dve_chain)
            ahead = [0]

            def lo(s, turns=0):
                dve.wait_ge(hi_ready, turns * RAW + s + 1)
                dve.tensor_tensor(wlo[:, s % SPLIT, :], raw[:, s % RAW, :], whi[:, s % SPLIT, :].bitcast(F32),
                                  ALU.subtract).then_inc(lo_ready, 1)

            def split_to(s):
                while ahead[0] <= s:
                    lo(ahead[0])
                    ahead[0] += 1

            def spread_conditioning(m):
                dve.wait_ge(m["bc_hi"], 1)
                v = [b[:, :, 3 * P:4 * P].rearrange("p k (j n) -> p k j n", j=2) for b in (hl, hh)]
                for j in range(2):
                    ins = dve.tensor_tensor(v[0][:, :, j], silu_c[:, :, j].unsqueeze(2).to_broadcast([P, KD, P // 2]),
                                            v[1][:, :, j].bitcast(F32), ALU.subtract)
                ins.then_inc(m["bc_lo"], 1)

            def mod_take(m, layer, n, bank):
                dve.wait_ge(m["turned"], n + 1)
                src = ps[:, bank, :].rearrange("p (b x) -> p b x", x=P)[:, :, 0:P:P // 2]
                dve.tensor_tensor(mod[:, layer, 4 * n:4 * n + 4, :], src,
                                  vt[:, layer, 4 * n:4 * n + 4].unsqueeze(2).to_broadcast([P, 4, 2]), ALU.add).then_inc(m["taken"], 1)

            def coefficients(layer, ready):
                dve.wait_ge(mods[layer]["taken"], PER_MOD // 2)
                for i in range(2):
                    pre = vt[:, layer, 48 + 16 * i:56 + 16 * i].unsqueeze(2).to_broadcast([P, KD, 2])
                    post = vt[:, layer, 56 + 16 * i:64 + 16 * i].unsqueeze(2).to_broadcast([P, KD, 2])
                    dve.scalar_tensor_tensor(coef_a[:, layer, i], mod[:, layer, 8 * (1 + 3 * i):8 * (2 + 3 * i)], 1.0, pre,
                                             ALU.add, ALU.mult).then_inc(ready, 1)
                    dve.tensor_tensor(coef_g[:, layer, i], mod[:, layer, 8 * (2 + 3 * i):8 * (3 + 3 * i)], post,
                                      ALU.mult).then_inc(ready, 1)

            def norm(m, tiles, layer, which, xn, mod_tile, coef, banks, dst=None):
                dve.wait_ge(m["root"], 1)
                chain.add(dve.reciprocal(rstd[:, 0:len(tiles)], root[:, 0:len(tiles)]))
                chain.wait()
                dve.wait_ge(coef, 4)

                def scale(i, t):
                    if i >= 2:
                        dve.wait_ge(m["xt"], i - 1)
                    dve.tensor_scalar(xn[:, i % 2, :], x_tile(t), rstd[:, i:i + 1], None, ALU.mult).then_inc(m["xn"], 1)

                def modulate(i, t):
                    j = 0 if t < LAT_TILES else 1
                    dve.wait_ge(m["xt"], i + 1)
                    if i >= 2:
                        if dst is None:
                            dve.wait_ge(m["hi"], i - 1)
                            dve.wait_ge(m["lo"], i - 1)
                    for k in range(KD):
                        ins = dve.tensor_scalar(mod_tile[:, i % 2, k, :],
                                          ps[:, banks[i % 2] + k // 4, (k % 4) * P:(k % 4 + 1) * P],
                                          coef_a[:, layer, which, k, j:j + 1], mod[:, layer, 24 * which + k, j:j + 1],
                                          ALU.mult, ALU.add)
                    ins.then_inc(m["t1"], 1)

                def split(i):
                    dve.wait_ge(m["hi"], i + 1)
                    if dst is None:
                        dve.tensor_tensor(hl[:, :, i * P:(i + 1) * P], mod_tile[:, i % 2],
                                          hh[:, :, i * P:(i + 1) * P].bitcast(F32), ALU.subtract).then_inc(m["lo"], 1)
                    else:
                        dve.tensor_tensor(dst[1][:, i, :], ps[:, 2 + 2 * i:4 + 2 * i, :].rearrange("p b n -> p (b n)"),
                                          dst[0][:, i, :].bitcast(F32), ALU.subtract).then_inc(m["lo"], 1)

                n = len(tiles)
                scale(0, tiles[0])
                for i, t in enumerate(tiles):
                    if i + 1 < n:
                        scale(i + 1, tiles[i + 1])
                    modulate(i, t)
                    if dst is None:
                        split(i)
                if dst is not None:
                    for i in range(n):
                        split(i)

            def resid(r, tiles, g, y_of, gate_tile, tmp):
                for i, t in enumerate(tiles):
                    dve.wait_ge(r["root"], i + 1)
                    chain.add(dve.reciprocal(rstd[:, i:i + 1], root[:, i:i + 1]))
                    chain.wait()
                    j = 0 if len(tiles) == 2 or t < LAT_TILES else 1
                    dve.wait_ge(g["sb"], j + 1)
                    chain.add(dve.scalar_tensor_tensor(tmp[:, i % 2, :], y_of(i), rstd[:, i:i + 1], gate_tile[:, j, :],
                                                       ALU.mult, ALU.mult))
                    chain.wait()
                    dve.tensor_tensor(x_tile(t), x_tile(t), tmp[:, i % 2, :], ALU.add).then_inc(r["x"], 1)

            def swiglu_body(f, first, m_tiles, silu, h, hth, htl):
                def body(kk, turns):
                    if kk:
                        lo(first + 3 * kk + 1, turns)
                    lo(first + 3 * kk + 2, turns)
                    dve.wait_ge(f["silu"], turns * 2 + kk + 1)
                    dve.tensor_tensor(h[:], silu[:], ps[:, 0:m_tiles, FFC:N], ALU.mult).then_inc(f["h"], 1)
                    lo(first + 3 * kk + 3, turns)
                    dve.wait_ge(f["hi"], turns * 2 + kk + 1)
                    cols = 2 * m_tiles * P
                    dve.tensor_tensor(htl[:, kk % 2].rearrange("p b n -> p (b n)"), ps[:, m_tiles, 0:cols],
                                      hth[:, kk % 2].rearrange("p b n -> p (b n)").bitcast(F32),
                                      ALU.subtract).then_inc(f["lo"], 1)
                return body

            def swiglu_all(f, first, m_tiles, chunks, silu, h, hth, htl, item_turns, in_head=None):
                body = swiglu_body(f, first, m_tiles, silu, h, hth, htl)
                body(0, item_turns)
                if in_head is not None:
                    in_head()
                body(1, item_turns)
                with dve.Fori(0, (chunks - 2) // 2) as j:
                    body(2, item_turns + j)
                    body(3, item_turns + j)
                if chunks % 2:
                    body(chunks - 1, item_turns)
                lo(first + 3 * chunks + 1, item_turns)

            def attention(s, plan, p, pt):
                pairs = 4 * plan["groups"]
                for at in range(pairs + 6):
                    if at < pairs:
                        g, n = at // 4, nkeys(plan, at // 4)
                        h = 2 * (at % 4)
                        nm = neg_max[:, g % 2, h:h + 2]
                        dve.wait_ge(s["s"], at + 1)
                        ins = dve.tensor_reduce(nm, ps[:, 2 * (at % 2):2 * (at % 2) + 2, 0:n], AX_X, ALU.max, negate=True)
                        if has_sink(plan, g):
                            chain.add(ins)
                            chain.wait()
                            chain.add(dve.tensor_tensor(nm, nm, neg_sink[:, h:h + 2], ALU.min))
                            chain.wait()
                            ins = dve.tensor_tensor(sink_arg[:, g % 2, h:h + 2], nm, sink[:, h:h + 2], ALU.add)
                        ins.then_inc(s["nm"], 1)
                    if 1 <= at <= pairs:
                        n = nkeys(plan, (at - 1) // 4)
                        dve.wait_ge(s["t"], at)
                        dve.tensor_copy(buf(pt, (at - 1) % 2, 1)[:, 0:n], ps[:, 5, 0:n]).then_inc(s["ptd"], 1)
                    last = at - 2
                    if last >= 0 and last % 4 == 3 and last < pairs:
                        g = last // 4
                        dve.wait_ge(s["p"], last + 1)
                        total = exp_sum[:, g % 2, :]
                        if has_sink(plan, g):
                            chain.add(dve.tensor_tensor(total, total, sink_exp[:, g % 2, :], ALU.add))
                            chain.wait()
                        chain.add(dve.reciprocal(exp_inv[:, g % 2, :], total))
                        dve.wait_ge(s["o"], g + 1)
                        if g % 2 == 0 and g >= 2:
                            dve.wait_ge(s["ot"], g)
                        chain.wait()
                        dve.tensor_tensor(o_sb[:, (g % 2) * N:(g % 2 + 1) * N].rearrange("p (h d) -> p h d", d=DH),
                                          ps[:, 6, :].rearrange("p (h d) -> p h d", d=DH),
                                          exp_inv[:, g % 2, :].unsqueeze(2).to_broadcast([P, 8, DH]),
                                          ALU.mult).then_inc(s["osb"], 1)
                    if plan["even"] and at < pairs and at % 4 == 2:
                        mod_take(mods[1], 1, EARLY_MOD + at // 4, 7)
                        split_to(M1_S + 2 * (EARLY_MOD + at // 4) + 3)
                    if plan["even"] and at < pairs and at % 4 == 3:
                        split_to(M1_S + 2 * (EARLY_MOD + at // 4) + 4)
                    for half in range(2):
                        last = at - 4 - half
                        if last >= 0 and last % 8 == 7 and last < pairs:
                            t = last // 8
                            dve.wait_ge(s["oth"], 2 * t + half + 1)
                            dve.tensor_tensor(hl[:, 4 * half:4 * half + 4, t * P:(t + 1) * P],
                                              ps[:, 7, :].rearrange("p (k n) -> p k n", n=P),
                                              hh[:, 4 * half:4 * half + 4, t * P:(t + 1) * P].bitcast(F32),
                                              ALU.subtract).then_inc(s["otl"], 1)

            dve.wait_ge(st["silu_c"], 1)
            dve.tensor_copy(vt[:, 0, :], ps[:, 0, 0:80]).then_inc(st["vec"], 1)
            dve.tensor_copy(vt[:, 1, :], ps[:, 0, 96:176]).then_inc(st["vec"], 1)
            dve.wait_ge(misc_loaded, 64)
            chain.add(dve.tensor_scalar(neg_sink[:], sink[:], -1.0, None, ALU.mult))
            dve.wait_ge(st["vec"], 2)
            spread_conditioning(mods[0])
            for n in range(PER_MOD // 2):
                split_to(M0_S + 2 * n + 3)
                if n:
                    mod_take(mods[0], 0, n - 1, 2 + (n - 1) % 2)
                split_to(M0_S + 2 * n + 4)
            n = PER_MOD // 2 - 1
            mod_take(mods[0], 0, n, 2 + n % 2)
            coefficients(0, st["coef0"])
            dve.wait_ge(const_loaded, 16)
            norm(norms[0], range(TILES), 0, 0, f_tmp, f_mod, st["coef0"], (2, 4))
            for n in range(3):
                split_to(WIN0_S + 2 * n + 3)
                for t in range(2, 4):
                    dve.wait_ge(*used(WIN0_S + 2 * n + 1))
                    for dst, src in qkv_parts(n, t):
                        ins = dve.tensor_copy(dst, src)
                    ins.then_inc(gemms[0]["dve"], 1)
                split_to(WIN0_S + 2 * n + 4)
            spread_conditioning(mods[1])
            dve.wait_ge(gemms[0]["act"], 6)
            dve.wait_ge(gemms[0]["dve"], 6)
            for t in range(TILES):
                sq = qk_t[:, 2 * t:2 * t + 2, :].rearrange("p a b -> p (a b)")[:, 0:QK_E]
                chain.add(dve.tensor_tensor(sq, qkv[:, t, 0:QK_E], qkv[:, t, 0:QK_E], ALU.mult))
            chain.wait()
            for t in range(TILES):
                sq = qk_t[:, 2 * t:2 * t + 2, :].rearrange("p a b -> p (a b)")[:, 0:QK_E]
                ins = dve.tensor_reduce(qk_ssq()[:, 10 * t:10 * t + 10], sq.rearrange("p (h d) -> p h d", d=DH), AX_X, ALU.add)
            ins.then_inc(qk["ssq"], 1)
            dve.wait_ge(qk["root"], 1)
            qk_inv = qk_t[:, 9, 128:168]
            chain.add(dve.reciprocal(qk_inv, qk_root()))
            for t in range(TILES):
                v = qkv[:, t, 0:QK_E].rearrange("p (h d) -> p h d", d=DH)
                chain.wait()
                chain.add(dve.tensor_tensor(v, v, qk_inv[:, 10 * t:10 * t + 10].unsqueeze(2).to_broadcast([P, 10, DH]), ALU.mult))
                chain.wait()
                for i, (h0, h1) in enumerate(((0, 8), (8, 10))):
                    gain = qk_gain[:, i, :].unsqueeze(1).to_broadcast([P, h1 - h0, DH])
                    ins = dve.tensor_tensor(v[:, h0:h1], v[:, h0:h1], gain, ALU.mult)
                    if i == 0 or t < LAT_TILES:
                        chain.add(ins)
                    else:
                        ins.then_inc(qk["ready"], 1)
                chain.wait()
                for g in range(2 if t < LAT_TILES else 0):
                    v = qkv[:, t, g * GROUP_E:g * GROUP_E + QK_E].rearrange("p (h c e) -> p h c e", h=10, e=2)
                    rot = qk_t[:, 4 * g:4 * g + 4, :].rearrange("p a b -> p (a b)")[:, 0:4 * 320].rearrange(
                        "p (m h c) -> p m h c", m=4, c=32)
                    cs = [const[:, C_ROPE + t * 64 + 32 * m:C_ROPE + t * 64 + 32 * (m + 1)].unsqueeze(1).to_broadcast([P, 10, 32])
                          for m in range(2)]
                    for m, (e, w) in enumerate(((0, 0), (1, 1), (0, 1), (1, 0))):
                        chain.add(dve.tensor_tensor(rot[:, m], v[:, :, :, e], cs[w], ALU.mult))
                    chain.wait()
                    chain.add(dve.tensor_tensor(v[:, :, :, 0], rot[:, 0], rot[:, 1], ALU.subtract))
                    ins = dve.tensor_tensor(v[:, :, :, 1], rot[:, 2], rot[:, 3], ALU.add)
                    if g == 0:
                        chain.add(ins)
                    else:
                        ins.then_inc(qk["ready"], 1)
                if t < EARLY_MOD:
                    mod_take(mods[1], 1, t, 7)
                    split_to(M1_S + 2 * t + 4)
            for i in range(1, 10, 2):
                dve.wait_ge(qk["t"], i + 1)
                dve.tensor_scalar(qk_t[:, i, :], ps[:, 1 + i % 6, :], SCALE if i % 5 < 4 else 1.0, None,
                                  ALU.mult).then_inc(qk["dve"], 1)
            attention(attns[0], even_plan, qkv_p, qkv_pt)
            coefficients(1, st["coef1"])
            split_to(WOUT0_S + 5)
            resid(resids[0], range(TILES), gates[0], lambda i: ps[:, 2 * i:2 * i + 2, :].rearrange("p b n -> p (b n)"),
                  f_gate, f_tmp)
            for n, (first, tiles) in enumerate(((FFA_S, (0, 1)), (FFB_S, (2, 3)))):
                norm(norms[1 + n], tiles, 0, 1, f_tmp, f_mod, st["coef0"], (0, 2))
                swiglu_all(ffns[n], first, 2, CHUNKS_E, f_silu, f_h, f_hth, f_htl, 0)
                ahead[0] = first + 3 * CHUNKS_E + 2
                resid(resids[1 + n], tiles, gates[1 + n], lambda i: ps[:, 3 + 2 * i:5 + 2 * i, :].rearrange("p b n -> p (b n)"),
                      f_gate, f_tmp)
            norm(norms[3], range(TILES), 1, 0, f_tmp, f_mod, st["coef1"], (0, 2))
            for n in range(6):
                split_to(WIN1_S + 2 * n + 3)
                for b in range(2, 4):
                    dve.wait_ge(*used(WIN1_S + 2 * n + 1))
                    src = ps[:, (n % 2) * 4 + b, :]
                    if n < 2:
                        ins = dve.tensor_scalar(o_q[:, 4 * n + b, :], src[:, 0:SEQ], SCALE, None, ALU.mult)
                    elif n < 4:
                        ins = dve.tensor_copy(o_k[:, 4 * (n - 2) + b, :], src)
                    else:
                        ins = dve.tensor_copy(o_v[:, b, (n - 4) * N:(n - 3) * N], src)
                    ins.then_inc(gemms[1]["dve"], 1)
                split_to(WIN1_S + 2 * n + 4)
            attention(attns[1], odd_plan, o_p, o_pt)
            split_to(WOUT1_S + 5)
            resid(resids[3], (0, 1), gates[3], lambda i: ps[:, 2 * i:2 * i + 2, :].rearrange("p b n -> p (b n)"),
                  m_gate, m_tmp)
            norm(norms[4], (0, 1), 1, 1, m_tmp, m_mod, st["coef1"], (0, 0), (h_hi, h_lo))

            e8 = const[:, C_E8:C_ALL]
            dve.wait_ge(router["logits"], 2)
            chain.add(dve.tensor_copy(logits[:], ps[:, 6, 0:16].rearrange("p (t e) -> p t e", e=EXPERTS)))
            chain.wait()
            for t in range(2):
                chain.add(dve.max(top[:, t, :], logits[:, t, :]))
            chain.wait()
            for t in range(2):
                chain.add(dve.max_index(top_i[:, t, :], top[:, t, :], logits[:, t, :]))
            dve.tensor_tensor(gw[:, :, 0:1], top[:, :, 1:2], top[:, :, 0:1], ALU.subtract).then_inc(router["exp"], 1)
            chain.wait()
            chain.add(dve.tensor_copy(top_f[:], top_i[:]))
            dve.wait_ge(router["ex"], 1)
            chain.add(dve.tensor_scalar(gw[:, :, 2:3], gw[:, :, 1:2], 1.0, None, ALU.add))
            chain.wait()
            chain.add(dve.reciprocal(gw[:, :, 2:3], gw[:, :, 2:3]))
            chain.wait()
            chain.add(dve.tensor_tensor(gw[:, :, 3:4], gw[:, :, 1:2], gw[:, :, 2:3], ALU.mult))
            for t in range(2):
                chain.add(dve.tensor_scalar(hot[:, t, 0, :], e8, top_f[:, t, 0:1], None, ALU.is_equal))
                chain.wait()
                dve.scalar_tensor_tensor(items[:, 2 + t, 0:EXPERTS], e8, top_f[:, t, 1:2], hot[:, t, 0, :], ALU.is_equal,
                                         ALU.add).then_inc(router["sel"], 1)
                chain.add(dve.tensor_scalar(hot[:, t, 1, :], e8, top_f[:, t, 1:2], gw[:, t, 3:4], ALU.is_equal, ALU.mult))
                chain.wait()
                chain.add(dve.scalar_tensor_tensor(items[:, 4 + t, 0:EXPERTS], hot[:, t, 0, :], gw[:, t, 2:3], hot[:, t, 1, :],
                                                   ALU.mult, ALU.add))
            chain.add(dve.tensor_copy(items[:, 6, 0:EXPERTS], e8))
            chain.add(dve.memset(over[:], 0.0))
            dve.wait_ge(router["rank"], 1)
            chain.add(dve.tensor_copy(items[:, 0:2, 0:EXPERTS], ps[:, 6, 16:32].rearrange("p (t e) -> p t e", e=EXPERTS)))
            chain.wait()
            chain.add(dve.tensor_scalar(over[:, 0, 4:12], ps[:, 6, 32:40], float(P), None, ALU.is_gt))
            for step in range(3):
                chain.wait()
                d = 1 << step
                chain.add(dve.tensor_tensor(over[:, step + 1, 4:12], over[:, step, 4:12], over[:, step, 4 - d:12 - d], ALU.add))
            for j in range(4):
                chain.wait()
                chain.add(dve.scalar_tensor_tensor(over_hot[:, j, :], over[:, 3, 4:12], float(j + 1), over[:, 0, 4:12],
                                                   ALU.is_equal, ALU.mult))
                chain.wait()
                chain.add(dve.tensor_tensor(over_tmp[:], items[:, :, 0:EXPERTS],
                                            over_hot[:, j, :].unsqueeze(1).to_broadcast([P, 7, EXPERTS]), ALU.mult))
                chain.wait()
                chain.add(dve.tensor_reduce(items[:, :, EXPERTS + j], over_tmp[:], AX_X, ALU.add))
            chain.wait()
            chain.add(dve.tensor_scalar(items[:, 0:2, EXPERTS:ITEM_COLS], items[:, 0:2, EXPERTS:ITEM_COLS], float(P), None,
                                        ALU.subtract))
            chain.add(dve.tensor_copy(table[0:1, 0:ITEM_COLS], items[0:1, 6, :]))
            dve.tensor_scalar(table[0:1, ITEM_COLS:ITEM_COLS + 1], over[0:1, 3, 11:12], float(EXPERTS), None,
                              ALU.add).then_inc(route_ready, 1)

            iota = const[:, C_IOTA:C_TRI]

            def make_pick(i):
                for t in range(2):
                    ins = dve.tensor_scalar(pick[:, t, :], iota, items[:, t, bass.ds(i, 1)], items[:, 2 + t, bass.ds(i, 1)],
                                            ALU.is_equal, ALU.mult)
                    ins.then_inc(pick_ready, 1)

            def ht(i):
                dve.wait_ge(ht_hi, i + 1)
                dve.tensor_copy(hl[:, :, 0:P], ps[:, 6:8, :].rearrange("p b (k n) -> p (b k) n", n=P)).then_inc(ht_lo, 1)

            make_pick(0)
            dve.wait_ge(gathered, 1)
            ht(0)
            for t in range(2):
                dve.memset(m_acc[:, t, :], 0.0).then_inc(acc_added[t], 1)
            n_items = dve.value_load(table[0:1, ITEM_COLS:ITEM_COLS + 1], min_val=EXPERTS, max_val=EXPERTS + 3)
            with dve.Fori(0, n_items) as i:
                def make_put():
                    for t in range(2):
                        dve.tensor_scalar(put[:, t, :], iota, items[:, t, bass.ds(i, 1)], items[:, 4 + t, bass.ds(i, 1)],
                                          ALU.is_equal, ALU.mult).then_inc(put_ready, 1)
                    make_pick(i + 1)
                swiglu_all(ffns[2], MOE_S, 1, CHUNKS_O, m_silu, m_h, m_hth, m_htl, i * (ITEM_SLOTS // RAW), make_put)
                ht(i + 1)
                for t in range(2):
                    dve.wait_ge(scattered, i * 2 + t + 1)
                    dve.wait_ge(acc_added[t], i + 1)
                    dve.tensor_tensor(m_acc[:, t, :], m_acc[:, t, :], ps[:, 2 * t:2 * t + 2, :].rearrange("p b n -> p (b n)"),
                                      ALU.add).then_inc(acc_added[t], 1)
            resid(resids[4], (0, 1), gates[4], lambda i: m_acc[:, i, :], m_gate, m_tmp)

        @block.tensor
        def _(pe):
            def use(s, turns=0):
                pe.wait_ge(lo_ready, turns * RAW + s + 1)

            def product(out, lhs, rhs, start, stop):
                (lh, ll), (rh, rl) = lhs, rhs
                pe.matmul(out, lh, rh, start=start, stop=False)
                pe.matmul(out, ll, rh, start=False, stop=False)
                return pe.matmul(out, lh, rl, start=False, stop=stop)

            def both(s, a0, a1):
                q = s % SPLIT
                return whi[:, q, a0:a1], wlo[:, q, a0:a1]

            def tokens(k, a0, a1):
                return hh[:, k, a0:a1], hl[:, k, a0:a1]

            def mod_rows(first, n, bank):
                for half in range(2):
                    s = first + 2 * n + half
                    use(s)
                    for kk in range(4):
                        k = 4 * half + kk
                        ins = product(ps[:, bank, :], tokens(k, 3 * P, 4 * P), both(s, kk * N, (kk + 1) * N),
                                      k == 0, k == KD - 1)
                    ins.then_inc(slot_used, 1)

            def mod_turn(m, n, bank):
                pe.wait_ge(m["row"], n + 1)
                for b in range(4):
                    ins = pe.transpose(ps[:, bank, b * P:(b + 1) * P], mod_row[:, n % 2, b * P:(b + 1) * P], ident)
                ins.then_inc(m["turned"], 1)

            def norm(m, n, banks, xn):
                for i in range(n):
                    pe.wait_ge(m["xn"], i + 1)
                    if banks[0] == banks[1]:
                        if i >= 1:
                            pe.wait_ge(m["t1"], i)
                    elif i >= 2:
                        pe.wait_ge(m["t1"], i - 1)
                    for k in range(KD):
                        ins = pe.transpose(ps[:, banks[i % 2] + k // 4, (k % 4) * P:(k % 4 + 1) * P],
                                           xn[:, i % 2, k * P:(k + 1) * P], ident)
                    ins.then_inc(m["xt"], 1)

            def broadcast_gate(g, layer, which, streams, bank=6):
                for n, j in enumerate(streams):
                    for k in range(KD):
                        ins = pe.matmul(ps[:, bank - 2 * n + k // 4, (k % 4) * P:(k % 4 + 1) * P],
                                        coef_g[:, layer, which, k, j:j + 1].to_broadcast([P, P]), ident,
                                        start=True, stop=True)
                    ins.then_inc(g["bc"], 1)

            def project(first, chunks, tiles, bank_of, before=None, tile_ready=None):
                for n in range(chunks):
                    if before is not None:
                        before(n)
                    for half in range(2):
                        s = first + 2 * n + half
                        use(s)
                        for t in tiles:
                            if tile_ready is not None and n == 0 and half == 0:
                                pe.wait_ge(tile_ready, t + 1)
                            for kk in range(4):
                                k = 4 * half + kk
                                ins = product(ps[:, bank_of(n, t), :], tokens(k, t * P, (t + 1) * P),
                                              both(s, kk * N, (kk + 1) * N), k == 0, k == KD - 1)
                        ins.then_inc(slot_used, 1)

            def swiglu(f, first, m_tiles, chunks, h, hth, htl, y_bank, item_turns=0, in_head=None, y_free=None):
                def gate_up(kk, turns):
                    for half in range(2):
                        s = first + (3 * kk - 1 if kk else 0) + half
                        use(s, turns)
                        for m in range(m_tiles):
                            for k4 in range(4):
                                k = 4 * half + k4
                                ins = product(ps[:, m, :], tokens(k, m * P, (m + 1) * P), both(s, k4 * N, (k4 + 1) * N),
                                              k == 0, k == KD - 1)
                        ins.then_inc(slot_used, 1)

                def turn(kk, turns):
                    pe.wait_ge(f["h"], turns * 2 + kk + 1)
                    for b in range(2):
                        for m in range(m_tiles):
                            c0 = (b * m_tiles + m) * P
                            ins = pe.transpose(ps[:, m_tiles, c0:c0 + P], h[:, m, b * P:(b + 1) * P], ident)
                    ins.then_inc(f["t"], 1)

                def down(kk, s, turns, start=False, stop=False):
                    use(s, turns)
                    pe.wait_ge(f["hi"], turns * 2 + kk + 1)
                    pe.wait_ge(f["lo"], turns * 2 + kk + 1)
                    for m in range(m_tiles):
                        for nh in range(2):
                            for b in range(2):
                                ins = product(ps[:, y_bank + 2 * m + nh, :],
                                              (hth[:, kk % 2, b, m * P:(m + 1) * P], htl[:, kk % 2, b, m * P:(m + 1) * P]),
                                              both(s, b * D + nh * N, b * D + (nh + 1) * N),
                                              start and b == 0, stop and b == 1)
                    ins.then_inc(slot_used, 1)

                def body(kk, turns):
                    gate_up(kk, turns)
                    down(kk - 1, first + 3 * kk + 1, turns, start=(kk == 1))
                    turn(kk, turns)

                gate_up(0, item_turns)
                turn(0, item_turns)
                if in_head is not None:
                    in_head()
                body(1, item_turns)
                with pe.Fori(0, (chunks - 2) // 2) as j:
                    body(2, item_turns + j)
                    body(3, item_turns + j)
                if chunks % 2:
                    body(chunks - 1, item_turns)
                down(chunks - 1, first + 3 * chunks - 1, item_turns, stop=True)

            def attention(s, plan, p, pt):
                pairs = 4 * plan["groups"]

                def scores(at):
                    g = at // 4
                    if at >= 2:
                        pe.wait_ge(s["p"], at - 1)
                    for i in range(2):
                        h = 2 * (at % 4) + i
                        out = ps[:, 2 * (at % 2) + i, 0:nkeys(plan, g)]
                        t = g // 2
                        if plan["even"]:
                            half, col, key0 = h // 4, 5 * (g % 2), 0 if t < LAT_TILES else SEQ
                            rows = slice(DH * half, DH * (half + 1))
                            masked = g % 2 == 1 and t < LAT_TILES
                            ins = pe.matmul(out, qk_t[rows, col + h % 4, t * P:(t + 1) * P], qk_t[rows, col + 4, key0:N],
                                            start=True, stop=not masked)
                            if masked:
                                c0 = (1 - t) * P
                                ins = pe.matmul(out[:, c0:c0 + P], ident, const[:, C_WIN + t * P:C_WIN + (t + 1) * P],
                                                start=False, stop=True)
                        else:
                            h += 8 * (g % 2)
                            rows = slice(DH * (h % 2), DH * (h % 2 + 1))
                            pe.matmul(out, o_q[rows, h // 2, t * P:(t + 1) * P], o_k[rows, h // 2, :], start=True, stop=False)
                            pe.wait_ge(bias["pool"], 2 * at + i + 1)
                            ins = pe.matmul(out[:, 0:SEQ], ident, o_bias[:, (2 * at + i) % 4, :], start=False, stop=True)
                    ins.then_inc(s["s"], 1)

                def turn(at):
                    pe.wait_ge(s["p"], at + 1)
                    if at >= 1:
                        pe.wait_ge(s["pta"], at)
                        pe.wait_ge(s["ptd"], at)
                    for i in range(2):
                        for b in range(nkeys(plan, at // 4) // P):
                            ins = pe.transpose(ps[:, 4 + i, b * P:(b + 1) * P], buf(p, at % 2, i)[:, b * P:(b + 1) * P], ident)
                    ins.then_inc(s["t"], 1)

                def values(at):
                    g = at // 4
                    pe.wait_ge(s["pta"], at + 1)
                    pe.wait_ge(s["ptd"], at + 1)
                    if at % 4 == 0 and g >= 1:
                        pe.wait_ge(s["osb"], g)
                    blocks = nkeys(plan, g) // P
                    for i in range(2):
                        h = 2 * (at % 4) + i
                        for b in range(blocks):
                            tile = TILES - blocks + b
                            if plan["even"]:
                                c0 = GROUP_E * (g % 2) + QK_E + DH * (h // 4)
                                v = qkv[:, tile, c0:c0 + DH]
                            else:
                                v = o_v[:, tile, DH * (h + 8 * (g % 2)):DH * (h + 1 + 8 * (g % 2))]
                            ins = pe.matmul(ps[:, 6, DH * h:DH * (h + 1)], buf(pt, at % 2, i)[:, b * P:(b + 1) * P], v,
                                            start=(b == 0), stop=(b == blocks - 1))
                    if at % 4 == 3:
                        ins.then_inc(s["o"], 1)

                def turn_out(t, half):
                    pe.wait_ge(s["osb"], 2 * t + 2)
                    if 2 * t + half >= 1:
                        pe.wait_ge(s["otl"], 2 * t + half)
                    for k in range(4):
                        c0 = (4 * half + k) * P
                        ins = pe.transpose(ps[:, 7, k * P:(k + 1) * P], o_sb[:, c0:c0 + P], ident)
                    ins.then_inc(s["ot"], 1)

                scores(0)
                for at in range(pairs + 6):
                    if at + 1 < pairs:
                        scores(at + 1)
                    if at < pairs:
                        turn(at)
                    if 1 <= at <= pairs:
                        values(at - 1)
                    for half in range(2):
                        last = at - 3 - half
                        if last >= 0 and last % 8 == 7 and last < pairs:
                            if plan["even"]:
                                pe.wait_ge(mods[1]["taken"], EARLY_MOD + min(at, pairs - 1) // 4 + 1 if at % 4 >= 2 or at >= pairs else EARLY_MOD + at // 4)
                            turn_out(last // 8, half)
                    if plan["even"] and at < pairs and at % 4 == 0:
                        n = EARLY_MOD + at // 4
                        pe.wait_ge(mods[1]["taken"], n)
                        if at >= 12:
                            pe.wait_ge(s["otl"], 2 * ((at - 4) // 8))
                        mod_rows(M1_S, n, 7)
                    if plan["even"] and at < pairs and at % 4 == 1:
                        mod_turn(mods[1], EARLY_MOD + at // 4, 7)
                pe.wait_ge(s["otl"], plan["groups"])

            pe.wait_ge(vec_loaded, 16 * 12)
            pe.wait_ge(const_loaded, 16)
            pe.transpose(ps[:, 0, 0:96], vrow0[:], ident[0:96, 0:96]).then_inc(st["vt"], 1)
            pe.transpose(ps[:, 0, 96:176], vrow1[:], ident[0:80, 0:80]).then_inc(st["vt"], 1)
            pe.wait_ge(st["silu_c"], 1)
            pe.wait_ge(st["vec"], 2)
            m = mods[0]
            pe.wait_ge(m["bc_lo"], 1)
            for n in range(PER_MOD // 2 + 1):
                if n < PER_MOD // 2:
                    if n >= 2:
                        pe.wait_ge(m["row"], n - 1)
                    mod_rows(M0_S, n, n % 2)
                if n >= 1:
                    if n >= 3:
                        pe.wait_ge(m["taken"], n - 2)
                    mod_turn(m, n - 1, 2 + (n - 1) % 2)
            norm(norms[0], TILES, (2, 4), f_tmp)

            def banks_free0(n):
                if n >= 2:
                    pe.wait_ge(gemms[0]["act"], 2 * (n - 1))
                    pe.wait_ge(gemms[0]["dve"], 2 * (n - 1))

            project(WIN0_S, 3, range(TILES), lambda n, t: (n % 2) * 4 + t, banks_free0, norms[0]["lo"])
            m = mods[1]
            pe.wait_ge(m["bc_lo"], 1)
            for n in range(EARLY_MOD):
                mod_rows(M1_S, n, 0)
                if n >= 1:
                    pe.wait_ge(m["taken"], n)
                mod_turn(m, n, 7)
            pe.wait_ge(qk["ready"], TILES)
            for i in range(10):
                g, c = i // 5, i % 5
                if i >= 6:
                    pe.wait_ge(qk["dve"] if i % 2 else qk["act"], (i - 6) // 2 + 1)
                for t in range(TILES):
                    src = qkv[:, t, GROUP_E * g + P * c:GROUP_E * g + P * (c + 1)]
                    ins = pe.transpose(ps[:, 1 + i % 6, t * P:(t + 1) * P], src, ident)
                ins.then_inc(qk["t"], 1)
            pe.wait_ge(qk["act"], 5)
            pe.wait_ge(qk["dve"], 5)
            attention(attns[0], even_plan, qkv_p, qkv_pt)
            broadcast_gate(gates[0], 0, 0, (0, 1))
            pe.wait_ge(gates[0]["sb"], 2)
            project(WOUT0_S, 2, range(TILES), lambda n, t: 2 * t + n)
            for n, (first, stream) in enumerate(((FFA_S, 0), (FFB_S, 1))):
                norm(norms[1 + n], 2, (0, 2), f_tmp)
                broadcast_gate(gates[1 + n], 0, 1, (stream,))
                pe.wait_ge(gates[1 + n]["sb"], 1)
                pe.wait_ge(norms[1 + n]["lo"], 2)
                swiglu(ffns[n], first, 2, CHUNKS_E, f_h, f_hth, f_htl, 3)
            norm(norms[3], TILES, (0, 2), f_tmp)
            pe.wait_ge(norms[3]["lo"], TILES)
            for n in range(6):
                if n >= 2:
                    pe.wait_ge(gemms[1]["act"], 2 * (n - 1))
                    pe.wait_ge(gemms[1]["dve"], 2 * (n - 1))
                for half in range(2):
                    s = WIN1_S + 2 * n + half
                    use(s)
                    for b in range(4):
                        for kk in range(4):
                            k = 4 * half + kk
                            out = ps[:, (n % 2) * 4 + b, :]
                            if n < 4:
                                width = SEQ if n < 2 else N
                                ins = product(out[:, 0:width], both(s, kk * N + b * P, kk * N + (b + 1) * P),
                                              tokens(k, 0, width), k == 0, k == KD - 1)
                            else:
                                ins = product(out, tokens(k, b * P, (b + 1) * P), both(s, kk * N, (kk + 1) * N),
                                              k == 0, k == KD - 1)
                    ins.then_inc(slot_used, 1)
            pe.wait_ge(gemms[1]["act"], 12)
            pe.wait_ge(gemms[1]["dve"], 12)
            attention(attns[1], odd_plan, o_p, o_pt)
            broadcast_gate(gates[3], 1, 0, (0,))
            project(WOUT1_S, 2, range(LAT_TILES), lambda n, t: 2 * t + n)
            m = norms[4]
            norm(m, 2, (0, 0), m_tmp)
            pe.wait_ge(misc_loaded, 64)
            for i in range(2):
                pe.wait_ge(m["t1"], i + 1)
                for k in range(KD):
                    ins = pe.matmul(ps[:, 6, 8 * i:8 * i + 8], m_mod[:, i, k, :], w_router[:, k, :],
                                    start=(k == 0), stop=(k == KD - 1))
                ins.then_inc(router["logits"], 1)
                for k in range(KD):
                    ins = pe.transpose(ps[:, 2 + 2 * i + k // 4, (k % 4) * P:(k % 4 + 1) * P], m_mod[:, i, k, :], ident)
                ins.then_inc(router["back"], 1)
            broadcast_gate(gates[4], 1, 1, (0,), 0)
            pe.wait_ge(router["sel"], 2)
            tri = const[:, C_TRI:C_E8]
            sel = [items[:, 2 + t, 0:EXPERTS] for t in range(2)]
            pe.matmul(ps[:, 6, 16:24], tri, sel[0], start=True, stop=True)
            pe.matmul(ps[:, 6, 24:32], ones[:], sel[0], start=True, stop=False)
            pe.matmul(ps[:, 6, 24:32], tri, sel[1], start=False, stop=True)
            pe.matmul(ps[:, 6, 32:40], ones[:], sel[0], start=True, stop=False)
            pe.matmul(ps[:, 6, 32:40], ones[:], sel[1], start=False, stop=True).then_inc(router["rank"], 1)

            def gather(i):
                pe.wait_ge(pick_ready, i * 2 + 2)
                for part, src in enumerate((h_hi, h_lo)):
                    for k in range(KD):
                        for t in range(2):
                            ins = pe.matmul(ps[:, 4 + 2 * part + k // 4, (k % 4) * P:(k % 4 + 1) * P],
                                            src[:, t, k * P:(k + 1) * P], pick[:, t, :], start=(t == 0), stop=(t == 1))
                ins.then_inc(gathered, 1)

            pe.wait_ge(m["lo"], 2)
            gather(0)
            pe.wait_ge(gates[4]["sb"], 1)
            pe.wait_ge(route_ready, 1)
            n_items = pe.value_load(table[0:1, ITEM_COLS:ITEM_COLS + 1], min_val=EXPERTS, max_val=EXPERTS + 3)
            with pe.Fori(0, n_items) as i:
                pe.wait_ge(ht_hi, i + 1)
                pe.wait_ge(ht_lo, i + 1)
                pe.wait_ge(acc_added[0], i + 1)

                def turn_put():
                    pe.wait_ge(put_ready, i * 2 + 2)
                    for t in range(2):
                        ins = pe.transpose(ps[:, 4, t * P:(t + 1) * P], put[:, t, :], ident)
                    ins.then_inc(put_turned, 1)
                    pe.wait_ge(acc_added[1], i + 1)

                swiglu(ffns[2], MOE_S, 1, CHUNKS_O, m_h, m_hth, m_htl, 2, i * (ITEM_SLOTS // RAW), turn_put)
                pe.wait_ge(put_t_ready, i + 1)
                gather(i + 1)
                pe.wait_ge(y_copied, i + 1)
                for t in range(2):
                    for nh in range(2):
                        ins = pe.matmul(ps[:, 2 * t + nh, :], put_t[:, t, :], m_y[:, nh * N:(nh + 1) * N], start=True, stop=True)
                    ins.then_inc(scattered, 1)


_INS = ["x", "c", "ctx", "c_ctx", "e_w_mod", "e_b_mod", "e_g_pre_mix", "e_g_post_mix", "e_g_pre_ffn", "e_g_post_ffn",
        "e_w_in", "e_w_out", "e_g_q", "e_g_k", "e_sink", "e_w_gate", "e_w_up", "e_w_down", "o_w_mod", "o_b_mod",
        "o_g_pre_mix", "o_g_post_mix", "o_g_pre_ffn", "o_g_post_ffn", "o_w_in", "o_w_out", "o_rpb", "o_w_router",
        "o_w_gate", "o_w_up", "o_w_down"]


def kernel(**inputs):
    import concourse.bacc as _bacc
    from concourse.bass_utils import run_bass_kernel_spmd as _run

    nc = _bacc.Bacc("TRN2", target_bir_lowering=False, num_devices=1)
    arrays, args = {}, {}
    given = {name: np.ascontiguousarray(inputs[name]) for name in _INS}
    given["constants"] = shape_constants()
    for name, x in given.items():
        arrays[f"in_{name}"] = x
        args[name] = nc.dram_tensor(f"in_{name}", x.shape, mybir.dt.from_np(x.dtype), kind="ExternalInput").ap()
    args["out"] = nc.dram_tensor("out_0", (1, SEQ, D), F32, kind="ExternalOutput").ap()
    build(nc, args)
    r = _run(nc, [arrays], core_ids=[0])
    return r.results[0]["out_0"]
```

```python
from contextlib import ExitStack

import concourse.bass as bass
from concourse import mybir
import numpy as np

P = 128
D = 1024
KD = D // P
SEQ = 256
CTX = 256
TILES = (SEQ + CTX) // P
LAT_TILES = SEQ // P
GRID_W = 64
ROWS = SEQ // GRID_W
DH = 64
N_MOD = 6
D_FF = 2816
D_FFE = 3584
EXPERTS = 8
QKV_E = 1536
GROUP_E = QKV_E // 2
QK_E = 10 * DH
HEADS_O = 16
NA_ROWS = 8
NA_COLS = 16
RPB_W = 2 * NA_COLS - 1
RPB_R = 2 * NA_ROWS - 1
ROW_SHIFTS = 2 * ROWS - 1
EPS = 1e-6
SCALE = DH ** -0.5
NEG = -1e30
WINDOW = 128

COND = P // 4
MODS = 2 * N_MOD * D // 512
MIX_MODS = 2 * D // 512
QK_MODS = 4
N = 512
SLOT = 4 * N
RAW = 6
SPLIT = 3
FFC = 256
CHUNKS_E = D_FF // FFC
CHUNKS_O = D_FFE // FFC
ITEM_SLOTS = 3 * CHUNKS_O
ITEM_COLS = 12

EVEN_BANKS = [(0, 1, 4, 5), (2, 3, 6, 7)]
ODD_BANKS = [(0, 1, 2, 7), (0, 1, 2, 7), (3, 4, 5, 6), (0, 1, 2, 7), (3, 4, 5, 6), (0, 1, 2, 7)]

WIN0_S = 2 * MIX_MODS
WOUT0_S = 2 * MODS + 6
FFA_S = WOUT0_S + 4
FFB_S = FFA_S + 3 * CHUNKS_E
WIN1_S = FFB_S + 3 * CHUNKS_E
WOUT1_S = WIN1_S + 12
MOE_S = WOUT1_S + 4


ALU = mybir.AluOpType
ACT = mybir.ActivationFunctionType
F32 = mybir.dt.float32
F32R = mybir.dt.float32r
I32 = mybir.dt.int32
U32 = mybir.dt.uint32
AX_X = mybir.AxisListType.X

C_IDENT = 0
C_WIN = C_IDENT + P
C_ROPE = C_WIN + 2 * P
C_COL = C_ROPE + 4 * 32
C_IOTA = C_COL + GRID_W
C_TRI = C_IOTA + P
C_E8 = C_TRI + P
C_SEL = C_E8 + EXPERTS
C_ALL = C_SEL + 2


def shape_constants():
    out = np.zeros((P, C_ALL), np.float32)
    i = np.arange(P)
    out[:, C_IDENT:C_WIN] = np.eye(P)
    for t in range(2):
        dist = np.abs((t * P + i)[:, None] - ((1 - t) * P + i)[None, :])
        out[:, C_WIN + t * P:C_WIN + (t + 1) * P] = np.where(dist <= WINDOW, 0.0, NEG)
    half = DH // 2
    freqs = (np.float32(10000.0) ** (-np.arange(0, half, 2, dtype=np.float32) / np.float32(half))).astype(np.float32)
    for t in range(2):
        token = t * P + i
        row, col = (token // GRID_W).astype(np.float32), (token % GRID_W).astype(np.float32)
        ang = np.concatenate([row[:, None] * freqs, col[:, None] * freqs], axis=-1).astype(np.float32)
        out[:, C_ROPE + t * 64:C_ROPE + t * 64 + 32] = np.cos(ang)
        out[:, C_ROPE + t * 64 + 32:C_ROPE + t * 64 + 64] = np.sin(ang)
    qc, kc = (i % GRID_W)[:, None], np.arange(GRID_W)[None, :]
    first = np.clip(qc - NA_COLS // 2, 0, GRID_W - NA_COLS)
    out[:, C_COL:C_IOTA] = np.where((kc >= first) & (kc < first + NA_COLS), 0.0, NEG)
    out[:, C_IOTA:C_TRI] = i[None, :]
    out[:, C_TRI:C_E8] = i[:, None] < i[None, :]
    out[:, C_E8:C_SEL] = np.arange(EXPERTS)[None, :]
    for j in range(2):
        out[[COND * j, COND * (2 + j)], C_SEL + j] = 1.0
    return out


def mod_slot(c):
    return 2 * c if c < MIX_MODS else 2 * c + 6


class Chain:

    def __init__(self, eng, sem):
        self.eng, self.sem, self.n = eng, sem, 0

    def add(self, ins):
        ins.then_inc(self.sem, 1)
        self.n = self.n + 1

    def wait(self):
        self.eng.wait_ge(self.sem, self.n)


def build(nc, a):
    with ExitStack() as ctx:
        def sem(name):
            return ctx.enter_context(nc.semaphore(name))

        def sems(prefix, names):
            return {n: sem(f"{prefix}_{n}") for n in names.split()}

        def sb(name, shape, dt=F32, scope=ctx):
            return scope.enter_context(nc.sbuf_tensor(name, shape, dt))

        raw = sb("raw", [P, RAW, SLOT])
        whi = sb("whi", [P, SPLIT, SLOT], F32R)
        wlo = sb("wlo", [P, SPLIT, SLOT], F32R)
        rpb_sb = sb("rpb_sb", [HEADS_O * ROW_SHIFTS, P])
        x_lat = sb("x_lat", [P, LAT_TILES, D])
        hh = sb("hh", [P, KD, N], F32R)
        hl = sb("hl", [P, KD, N], F32R)
        o_sb = sb("o_sb", [P, D])
        const = sb("const", [P, C_ALL])
        vt = sb("vt", [P, 2, 80])
        silu_c = sb("silu_c", [P, KD, 2])
        mod = sb("mod", [P, 2, N_MOD * KD, 2])
        coef_a = sb("coef_a", [P, 2, 2, KD, 2])
        coef_g = sb("coef_g", [P, 2, 2, KD, 2])
        qk_gain = sb("qk_gain", [P, 2, DH])
        sink = sb("sink", [P, 8])
        neg_sink = sb("neg_sink", [P, 8])
        ones = sb("ones", [P, P])
        eps = sb("eps", [P, 1])
        ssq = sb("ssq", [P, 9])
        root = sb("root", [P, 8])
        rstd = sb("rstd", [P, 8])
        w_router = sb("w_router", [P, KD, EXPERTS])
        neg_max = sb("neg_max", [P, 2, 8])
        sink_arg = sb("sink_arg", [P, 2, 8])
        sink_exp = sb("sink_exp", [P, 2, 8])
        exp_sum = sb("exp_sum", [P, 2, 8])
        exp_inv = sb("exp_inv", [P, 2, 8])

        with ExitStack() as even:
            x_ctx = sb("x_ctx", [P, 2, D], F32, even)
            with ExitStack() as s:
                vrow0 = sb("vrow0", [96, P], F32, s)
                vrow1 = sb("vrow1", [80, P], F32, s)
            with ExitStack() as s:
                qkv = sb("qkv", [P, TILES, QKV_E], F32, s)
                qk_t = sb("qk_t", [P, 10, N], F32, s)
                mod_row = sb("mod_row", [P, 2, N], F32, s)
            with ExitStack() as s:
                f_gate = sb("f_gate", [P, 2, D], F32, s)
                f_tmp = sb("f_tmp", [P, 2, D], F32, s)
                f_mod = sb("f_mod", [P, 2, KD, P], F32, s)
                f_silu = sb("f_silu", [P, 2, FFC], F32, s)
                f_h = sb("f_h", [P, 2, FFC], F32, s)
                f_hth = sb("f_hth", [P, 2, 2, 2 * P], F32R, s)
                f_htl = sb("f_htl", [P, 2, 2, 2 * P], F32R, s)
        with ExitStack() as s:
            o_k = sb("o_k", [P, 8, N], F32, s)
            o_v = sb("o_v", [P, TILES, D], F32, s)
            o_q = sb("o_q", [P, 8, SEQ], F32, s)
            o_bias = sb("o_bias", [P, 4, SEQ], F32, s)
            o_p = sb("o_p", [P, 2, 2, N], F32, s)
            o_pt = sb("o_pt", [P, 2, 2, N], F32, s)
        with ExitStack() as s:
            m_gate = sb("m_gate", [P, 1, D], F32, s)
            m_tmp = sb("m_tmp", [P, 2, D], F32, s)
            m_mod = sb("m_mod", [P, 2, KD, P], F32, s)
            m_acc = sb("m_acc", [P, 2, D], F32, s)
            h_hi = sb("h_hi", [P, 2, D], F32R, s)
            h_lo = sb("h_lo", [P, 2, D], F32R, s)
            m_silu = sb("m_silu", [P, 1, FFC], F32, s)
            m_h = sb("m_h", [P, 1, FFC], F32, s)
            m_hth = sb("m_hth", [P, 2, 2, P], F32R, s)
            m_htl = sb("m_htl", [P, 2, 2, P], F32R, s)
            m_y = m_tmp[:, 0, :]
            pick = sb("pick", [P, 2, P], F32R, s)
            put = sb("put", [P, 2, P], F32, s)
            put_t = sb("put_t", [P, 2, P], F32, s)
            logits = sb("logits", [P, 2, EXPERTS], F32, s)
            top = sb("top", [P, 2, 8], F32, s)
            top_i = sb("top_i", [P, 2, 8], U32, s)
            top_f = sb("top_f", [P, 2, 8], F32, s)
            gw = sb("gw", [P, 2, 4], F32, s)
            hot = sb("hot", [P, 2, 2, EXPERTS], F32, s)
            items = sb("items", [P, 7, ITEM_COLS], F32, s)
            over = sb("over", [P, 4, 12], F32, s)
            over_hot = sb("over_hot", [P, 4, EXPERTS], F32, s)
            over_tmp = sb("over_tmp", [P, 7, EXPERTS], F32, s)
            table = sb("table", [1, 16], I32, s)

        ps = ctx.enter_context(nc.psum_tensor("ps", [P, 8, N], F32))
        bias_dram = nc.dram_tensor("bias_scratch", [HEADS_O * ROW_SHIFTS, GRID_W, P], F32, kind="Internal").ap()

        ident = const[:, C_IDENT:C_WIN]

        def x_tile(t):
            return x_lat[:, t, :] if t < LAT_TILES else x_ctx[:, t - LAT_TILES, :]

        def bank_pair(bank):
            return ps[:, bank:bank + 2, :].rearrange("p b n -> p (b n)")

        x_loaded, const_loaded, vec_loaded, misc_loaded = (sem(n) for n in
                                                           ("x_loaded", "const_loaded", "vec_loaded", "misc_loaded"))
        raw_landed = [sem(f"raw_landed{i}") for i in range(RAW)]
        hi_ready, lo_ready, slot_used = (sem(n) for n in ("hi_ready", "lo_ready", "slot_used"))
        mods = sems("mod", "bc_hi bc_lo row turned taken")
        act_chain, dve_chain = sem("act_chain"), sem("dve_chain")
        st = sems("set", "vt silu_c vec coef0 coef1 pool")
        norms = [sems(f"norm{i}", "root xn xt t1 hi lo") for i in range(5)]
        router = sems("router", "logits back exp ex sel rank")
        gates = [sems(f"gate{i}", "bc sb") for i in range(5)]
        resids = [sems(f"resid{i}", "root x") for i in range(5)]
        gemms = [sems(f"gemm{i}", "act dve") for i in range(2)]
        ffns = [sems(f"ffn{i}", "silu h t hi lo") for i in range(3)]
        attns = [sems(f"attn{i}", "s nm p t pta ptd o osb ot oth otl") for i in range(2)]
        qk = sems("qk", "sq pool ssq root ready t act dve")
        bias = sems("bias", "rows wrote pool")
        bias_landed = [sem(f"bias_landed{i}") for i in range(4)]
        route_ready, pick_ready, gathered, ht_hi, ht_lo = (sem(n) for n in
                                                           ("route_ready", "pick_ready", "gathered", "ht_hi", "ht_lo"))
        put_ready, put_turned, put_t_ready, y_copied, scattered = (
            sem(n) for n in ("put_ready", "put_turned", "put_t_ready", "y_copied", "scattered"))
        acc_added = [sem(f"acc_added{t}") for t in range(2)]
        out_stored, mixed = sem("out_stored"), sem("mixed")

        def used(s, turns=0):
            return slot_used, turns * RAW + s + 1

        even_plan = {"groups": 2 * TILES, "even": True}
        odd_plan = {"groups": 4, "even": False}
        qkv_p = [[qkv[:, b, i * GROUP_E:i * GROUP_E + N] for i in range(2)] for b in range(2)]
        qkv_pt = [[qkv[:, 2 + b, i * GROUP_E:i * GROUP_E + N] for i in range(2)] for b in range(2)]

        def qkv_parts(n, t):
            src = ps[:, EVEN_BANKS[n % 2][t], :]
            queries = [qkv[:, t, GROUP_E * g:GROUP_E * g + 8 * DH].rearrange("p (c a d) -> p a c d", a=2, d=DH)
                       for g in range(2)]
            if n == 0:
                return [(queries[0], src.rearrange("p (a c d) -> p a c d", a=2, d=DH))]
            if n == 1:
                return [(qkv[:, t, N:GROUP_E], src[:, 0:256]),
                        (queries[1][:, 0], src[:, 256:512].rearrange("p (c d) -> p c d", d=DH))]
            return [(queries[1][:, 1], src[:, 0:256].rearrange("p (c d) -> p c d", d=DH)),
                    (qkv[:, t, GROUP_E + 8 * DH:QKV_E], src[:, 256:512])]

        def nkeys(plan, g):
            return N if not plan["even"] or g // 2 < LAT_TILES else CTX

        def has_sink(plan, g):
            return plan["even"] and g % 2 == 1

        def buf(p, b, i):
            return p[b][i] if isinstance(p, list) else p[:, b, i, :]

        rot_a, rot_b = (qk_t[:, 3 * g:3 * g + 3, :].rearrange("p a b -> p (a b)")[:, 0:4 * 320].rearrange(
            "p (m h c) -> p m h c", m=4, c=32) for g in range(2))

        def rotate(eng, chain, t, g, rot):
            v = qkv[:, t, g * GROUP_E:g * GROUP_E + QK_E].rearrange("p (h c e) -> p h c e", h=10, e=2)
            cs = [const[:, C_ROPE + t * 64 + 32 * m:C_ROPE + t * 64 + 32 * (m + 1)].unsqueeze(1).to_broadcast([P, 10, 32])
                  for m in range(2)]
            for m, (e, w) in enumerate(((0, 0), (1, 1), (0, 1), (1, 0))):
                chain.add(eng.tensor_tensor(rot[:, m], v[:, :, :, e], cs[w], ALU.mult))
            chain.wait()
            chain.add(eng.tensor_tensor(v[:, :, :, 0], rot[:, 0], rot[:, 1], ALU.subtract))
            return eng.tensor_tensor(v[:, :, :, 1], rot[:, 2], rot[:, 3], ALU.add)

        def qk_ssq():
            return qk_t[:, 9, 0:40]

        def qk_root():
            return qk_t[:, 9, 64:104]

        def attention_mod(at):
            return MIX_MODS + QK_MODS + at // 2

        def turned_out(at, half, pairs):
            last = at - 3 - 2 * half
            return last // 8 if 0 <= last < pairs and last % 8 == 7 else None

        def attention_act(act, s, plan, p, pt, mod_copy, split_to, load_bias, gate):
            pairs = 4 * plan["groups"]
            for at in range(pairs + 6):
                if plan["even"] and 2 <= at <= pairs and at % 2 == 0:
                    mod_copy(attention_mod(at) - 1, 7)
                if at < pairs:
                    g, n = at // 4, nkeys(plan, at // 4)
                    act.wait_ge(s["nm"], at + 1)
                    if at >= 2:
                        act.wait_ge(s["t"], at - 1)
                    for i in range(2):
                        h = 2 * (at % 4) + i
                        ins = act.activation(buf(p, at % 2, i)[:, 0:n], ps[:, 2 * (at % 2) + i, 0:n], ACT.Exp,
                                             bias=neg_max[:, g % 2, h:h + 1], accum_out=exp_sum[:, g % 2, h:h + 1])
                    if has_sink(plan, g):
                        h = 2 * (at % 4)
                        ins = act.activation(sink_exp[:, g % 2, h:h + 2], sink_arg[:, g % 2, h:h + 2], ACT.Exp)
                    ins.then_inc(s["p"], 1)
                    if not plan["even"] and at + 2 < pairs:
                        load_bias(2 * at + 4)
                        load_bias(2 * at + 5)
                if 1 <= at <= pairs:
                    n = nkeys(plan, (at - 1) // 4)
                    act.wait_ge(s["t"], at)
                    act.activation(buf(pt, (at - 1) % 2, 0)[:, 0:n], ps[:, 4, 0:n], ACT.Copy).then_inc(s["pta"], 1)
                for half in range(2):
                    t = turned_out(at, half, pairs)
                    if t is not None:
                        act.wait_ge(s["ot"], 2 * t + half + 1)
                        act.activation(hh[:, 4 * half:4 * half + 4, t * P:(t + 1) * P],
                                       ps[:, 7, :].rearrange("p (k n) -> p k n", n=P), ACT.Copy).then_inc(s["oth"], 1)
                if at == pairs + 3:
                    gate()
                if plan["even"] and at < pairs:
                    split_to(mod_slot(MIX_MODS + QK_MODS) + at + 2)

        block = ctx.enter_context(nc.Block())

        @block.sync
        def _(sp):
            sp.dma_start(const[:], a["constants"]).then_inc(const_loaded, 16)
            for layer, rows in (("e", vrow0), ("o", vrow1)):
                sp.dma_start(rows[0:48, :], a[f"{layer}_b_mod"].rearrange("o (r p) -> (o r) p", p=P)).then_inc(vec_loaded, 16)
                for i, g in enumerate(("pre_mix", "post_mix", "pre_ffn", "post_ffn")):
                    sp.dma_start(rows[48 + 8 * i:56 + 8 * i, :],
                                 a[f"{layer}_g_{g}"].rearrange("o (r p) -> (o r) p", p=P)).then_inc(vec_loaded, 16)
            sp.dma_start(vrow0[80:88, :], a["c"].rearrange("o (r p) -> (o r) p", p=P)).then_inc(vec_loaded, 16)
            sp.dma_start(vrow0[88:96, :], a["c_ctx"].rearrange("(r p) -> r p", p=P)).then_inc(vec_loaded, 16)
            sp.dma_start(x_lat[:], a["x"].rearrange("o (t p) d -> p (o t) d", p=P)).then_inc(x_loaded, 16)
            sp.dma_start(x_ctx[:], a["ctx"].rearrange("o (t p) d -> p (o t) d", p=P)).then_inc(x_loaded, 16)

            def fill(s, pairs, turns=0):
                before = s - RAW
                if before >= 0:
                    sp.wait_ge(lo_ready, turns * RAW + before + 1)
                for dst, src in pairs:
                    sp.dma_start(dst, src).then_inc(raw_landed[s % RAW], 16)

            def fill_projection(s, w, n, half):
                dst = raw[:, s % RAW, :].rearrange("p (k n) -> p k n", n=N)
                src = w.rearrange("o (k p) n -> p (o k) n", p=P)[:, 4 * half:4 * half + 4, n * N:(n + 1) * N]
                fill(s, [(dst[:, 0:2], src[:, 0:2]), (dst[:, 2:4], src[:, 2:4])])

            def fill_all(first, w, chunks):
                for n in range(chunks):
                    for half in range(2):
                        fill_projection(first + 2 * n + half, w, n, half)

            def fill_mods(c0, c1):
                for c in range(c0, c1):
                    w, n = (a["e_w_mod"], c) if c < MODS // 2 else (a["o_w_mod"], c - MODS // 2)
                    for half in range(2):
                        fill_projection(mod_slot(c) + half, w, n, half)

            def swiglu_stream(first, chunks, wg, wu, wd, expert_k, expert_b, item_turns):
                def gu(s, kk, turns, j):
                    for half in range(2):
                        dst = raw[:, (s + half) % RAW, :].rearrange("p (k n) -> p k n", n=N)
                        k0 = bass.ds(expert_k + 4 * half, 4)
                        c0 = bass.ds(j * 2 * FFC + kk * FFC, FFC)
                        fill(s + half, [(dst[:, :, 0:FFC], wg[:, k0, c0]), (dst[:, :, FFC:N], wu[:, k0, c0])], turns)

                def down(s, kk, turns, j):
                    dst = raw[:, s % RAW, :].rearrange("p (b n) -> p b n", n=D)
                    b0 = expert_b + j * 4 + 2 * kk
                    fill(s, [(dst[:, b:b + 1], wd[:, bass.ds(b0 + b, 1)]) for b in range(2)], turns)

                gu(first, 0, item_turns, 0)

                def body(kk, turns, j):
                    gu(first + 3 * kk - 1, kk, turns, j)
                    down(first + 3 * kk + 1, kk - 1, turns, j)

                body(1, item_turns, 0)
                with sp.Fori(0, (chunks - 2) // 2) as j:
                    body(2, item_turns + j, j)
                    body(3, item_turns + j, j)
                if chunks % 2:
                    body(chunks - 1, item_turns, 0)
                down(first + 3 * chunks - 1, chunks - 1, item_turns, 0)

            fill_mods(0, MIX_MODS)
            fill_all(WIN0_S, a["e_w_in"], 3)
            fill_mods(MIX_MODS, MODS)
            fill_all(WOUT0_S, a["e_w_out"], 2)
            eg, eu = (a[n].rearrange("o (k p) f -> p (o k) f", p=P) for n in ("e_w_gate", "e_w_up"))
            ed = a["e_w_down"].rearrange("o (b p) n -> p (o b) n", p=P)
            for first in (FFA_S, FFB_S):
                swiglu_stream(first, CHUNKS_E, eg, eu, ed, 0, 0, 0)
            fill_all(WIN1_S, a["o_w_in"], 6)
            fill_all(WOUT1_S, a["o_w_out"], 2)

            og, ou = (a[n].rearrange("o e (k p) f -> p (o e k) f", p=P) for n in ("o_w_gate", "o_w_up"))
            od = a["o_w_down"].rearrange("o e (b p) n -> p (o e b) n", p=P)
            turns_per_item = ITEM_SLOTS // RAW
            with sp.Fori(0, EXPERTS - 1) as i:
                swiglu_stream(MOE_S, CHUNKS_O, og, ou, od, i * KD, i * (D_FFE // P), i * turns_per_item)
            sp.wait_ge(route_ready, 1)
            n_items = sp.value_load(table[0:1, ITEM_COLS:ITEM_COLS + 1], min_val=EXPERTS, max_val=EXPERTS + 3)
            with sp.Fori(EXPERTS - 1, n_items) as i:
                e = sp.value_load(table[0:1, bass.ds(i, 1)], min_val=0, max_val=EXPERTS - 1)
                swiglu_stream(MOE_S, CHUNKS_O, og, ou, od, e * KD, e * (D_FFE // P), i * turns_per_item)
            for ahead in range(2):
                dst = raw[:, (MOE_S + ahead) % RAW, :].rearrange("p (k n) -> p k n", n=N)
                fill(MOE_S + ahead, [(dst[:, 0:2], og[:, 0:2, 0:N]), (dst[:, 2:4], og[:, 2:4, 0:N])], n_items * turns_per_item)
            for t in range(LAT_TILES):
                sp.wait_ge(resids[4]["x"], t + 1)
                sp.dma_start(a["out"].rearrange("o (t p) d -> p (o t) d", p=P)[:, t, :], x_lat[:, t, :]).then_inc(out_stored, 16)
            sp.wait_ge(out_stored, 16 * LAT_TILES)

        @block.gpsimd
        def _(pool):
            chain = Chain(pool, sem("pool_chain"))
            pool.memset(ones[:], 1.0).then_inc(st["pool"], 1)
            pool.memset(eps[:], EPS).then_inc(st["pool"], 1)
            pool.memset(rpb_sb[:], 0.0).then_inc(st["pool"], 1)
            for i, name in enumerate(("e_g_q", "e_g_k")):
                pool.dma_start(qk_gain[:, i, :], bass.AP(a[name].tensor, 0, [[0, P], [1, DH]])).then_inc(misc_loaded, 16)
            pool.dma_start(sink[:], bass.AP(a["e_sink"].tensor, 0, [[0, P], [1, 8]])).then_inc(misc_loaded, 16)
            pool.dma_start(w_router[:], a["o_w_router"].rearrange("o (k p) e -> p (o k) e", p=P)).then_inc(misc_loaded, 16)
            pool.wait_ge(st["pool"], 3)
            for h in range(HEADS_O):
                r0 = NA_ROWS - ROWS
                pool.dma_start(rpb_sb[h * ROW_SHIFTS:(h + 1) * ROW_SHIFTS, GRID_W - NA_COLS:GRID_W - NA_COLS + RPB_W],
                               a["o_rpb"][0, h, r0:r0 + ROW_SHIFTS, :]).then_inc(bias["rows"], 16)
            pool.wait_ge(bias["rows"], 16 * HEADS_O)
            n_rows = HEADS_O * ROW_SHIFTS
            pool.dma_start(bass.AP(bias_dram.tensor, 0, [[GRID_W * P, n_rows], [P, GRID_W], [1, P]]),
                           bass.AP(rpb_sb, 0, [[P, n_rows], [0, GRID_W], [1, P]])).then_inc(bias["wrote"], 16)
            pool.wait_ge(bias["wrote"], 16)
            def mask_unit(u):
                pool.wait_ge(bias_landed[u % 4], 32 * (u // 4 + 1))
                v = o_bias[:, u % 4, :].rearrange("p (k c) -> p k c", c=GRID_W)
                m = bass.AP(const, C_COL, [[C_ALL, P], [0, ROWS], [1, GRID_W]])
                pool.tensor_tensor(v, v, m, ALU.add).then_inc(bias["pool"], 1)

            pool.wait_ge(const_loaded, 16)
            pool.wait_ge(gemms[0]["act"], 6)
            pool.wait_ge(gemms[0]["dve"], 6)
            pool.wait_ge(qk["ssq"], 1)
            for t in range(LAT_TILES):
                rotate(pool, chain, t, 1, rot_b).then_inc(qk["pool"], 1)
                pool.wait_ge(qk["pool"], t + 1)
            for u in range(2 * HEADS_O):
                mask_unit(u)

        @block.scalar
        def _(act):
            chain = Chain(act, act_chain)
            ahead = [0]

            def hi(s, turns=0):
                act.wait_ge(raw_landed[s % RAW], turns * 32 + 32 * (s // RAW + 1))
                if s >= SPLIT:
                    act.wait_ge(*used(s - SPLIT, turns))
                act.activation(whi[:, s % SPLIT, :], raw[:, s % RAW, :], ACT.Copy).then_inc(hi_ready, 1)

            def split_to(s):
                while ahead[0] <= s:
                    hi(ahead[0])
                    ahead[0] += 1

            def spread_conditioning():
                act.activation(hh[:, :, 3 * P:3 * P + 2 * COND].rearrange("p k (j n) -> p k j n", j=2),
                               silu_c[:].unsqueeze(3).to_broadcast([P, KD, 2, COND]), ACT.Copy).then_inc(mods["bc_hi"], 1)

            def mod_copy(c, bank):
                act.wait_ge(*used(mod_slot(c) + 1))
                if c >= 2:
                    act.wait_ge(mods["turned"], c - 1)
                act.activation(mod_row[:, c % 2, :], ps[:, bank, :], ACT.Copy).then_inc(mods["row"], 1)

            def rms(src, col, signal):
                chain.wait()
                chain.add(act.activation(o_sb[:], src, ACT.Square, accum_out=ssq[:, col:col + 1]))
                chain.wait()
                act.activation(root[:, col:col + 1], ssq[:, col:col + 1], ACT.Sqrt, scale=1.0 / D,
                               bias=eps[:, 0:1]).then_inc(signal, 1)

            def load_bias(u):
                t, h = u // HEADS_O, u % HEADS_O
                for r2 in range(2):
                    row = 2 * t + r2
                    src = bass.AP(bias_dram.tensor, (h * ROW_SHIFTS + ROWS - 1 - row) * GRID_W * P + GRID_W - 1,
                                  [[P - 1, GRID_W], [GRID_W * P, ROWS], [1, GRID_W]])
                    act.dma_start(o_bias[r2 * GRID_W:(r2 + 1) * GRID_W, u % 4, :].rearrange("p (k c) -> p k c", c=GRID_W),
                                  src).then_inc(bias_landed[u % 4], 16)

            def load_table(func):
                chain.wait()
                chain.add(act.activation(ssq[:, 8:9], eps[:], func))

            def norm_roots(m, tiles, i0=0, x_ready=None):
                for i, t in enumerate(tiles, i0):
                    if x_ready is not None:
                        act.wait_ge(x_ready[0], x_ready[1] + i - i0 + 1)
                    rms(x_tile(t), 4 + i, m["root"])

            def norm_hi(m, tiles, mod_tile, i0=0, dst=None):
                for i, t in enumerate(tiles, i0):
                    if dst is None:
                        act.wait_ge(m["t1"], i + 1)
                        act.activation(hh[:, :, t * P:(t + 1) * P], mod_tile[:, i % 2], ACT.Copy).then_inc(m["hi"], 1)
                    else:
                        act.wait_ge(router["back"], i + 1)
                        act.activation(dst[:, i, :], ps[:, 2 + 2 * i:4 + 2 * i, :].rearrange("p b n -> p (b n)"),
                                       ACT.Copy).then_inc(m["hi"], 1)

            def gate(g, dst, rows=(0,), banks=(6, 4)):
                for n, (j, bank) in enumerate(zip(rows, banks)):
                    act.wait_ge(g["bc"], n + 1)
                    act.activation(dst[:, j, :], bank_pair(bank), ACT.Copy).then_inc(g["sb"], 1)

            def resid_roots(r, n, y_ready, y_of, i0=0):
                for i in range(i0, n):
                    act.wait_ge(*y_ready(i))
                    rms(y_of(i), i, r["root"])

            def swiglu(f, first, m_tiles, silu, hth):
                def silu_chunk(kk, turns):
                    act.wait_ge(*used(first + (3 * kk if kk else 1), turns))
                    act.activation(silu[:], ps[:, 0:m_tiles, 0:FFC], ACT.Silu).then_inc(f["silu"], 1)

                def turned(kk, turns):
                    act.wait_ge(f["t"], turns * 2 + kk + 1)
                    cols = 2 * m_tiles * P
                    act.activation(hth[:, kk % 2].rearrange("p b n -> p (b n)"), ps[:, m_tiles, 0:cols],
                                   ACT.Copy).then_inc(f["hi"], 1)

                def body(kk, turns, before_silu=None, after_silu=None):
                    if kk:
                        hi(first + 3 * kk + 1, turns)
                    hi(first + 3 * kk + 2, turns)
                    if before_silu is not None:
                        before_silu()
                    silu_chunk(kk, turns)
                    if after_silu is not None:
                        after_silu()
                    hi(first + 3 * kk + 3, turns)
                    turned(kk, turns)
                return body

            def swiglu_all(f, first, m_tiles, chunks, silu, hth, item_turns, before_silu=None, after_silu=None,
                           after_first=None, after_second=None):
                body = swiglu(f, first, m_tiles, silu, hth)
                body(0, item_turns, before_silu, after_silu)
                if after_first is not None:
                    after_first()
                body(1, item_turns)
                if after_second is not None:
                    after_second()
                with act.Fori(0, (chunks - 2) // 2) as j:
                    body(2, item_turns + j)
                    body(3, item_turns + j)
                if chunks % 2:
                    body(chunks - 1, item_turns)
                hi(first + 3 * chunks + 1, item_turns)

            act.wait_ge(st["vt"], 2)
            act.activation(silu_c[:], ps[:, 0, 80:96].rearrange("p (j k) -> p k j", j=2), ACT.Silu).then_inc(st["silu_c"], 1)
            act.wait_ge(st["silu_c"], 1)
            spread_conditioning()
            act.wait_ge(x_loaded, 32)
            act.wait_ge(st["pool"], 3)
            norm_roots(norms[0], range(TILES))
            for c in range(MIX_MODS):
                split_to(mod_slot(c) + 3)
                mod_copy(c, c % 2)
                split_to(mod_slot(c) + 4)
            norm_hi(norms[0], range(TILES), f_mod)
            for n in range(3):
                split_to(WIN0_S + 2 * n + 3)
                for t in range(2):
                    act.wait_ge(*used(WIN0_S + 2 * n + 1))
                    for dst, src in qkv_parts(n, t):
                        ins = act.activation(dst, src, ACT.Copy)
                    ins.then_inc(gemms[0]["act"], 1)
                split_to(WIN0_S + 2 * n + 4)
            spread_conditioning()
            act.wait_ge(gemms[0]["dve"], 6)
            act.wait_ge(gemms[0]["act"], 6)
            for t in range(TILES):
                act.activation(qk_t[:, 2 * t:2 * t + 2, :].rearrange("p a b -> p (a b)")[:, 0:QK_E], qkv[:, t, 0:QK_E],
                               ACT.Square).then_inc(qk["sq"], 1)
            split_to(mod_slot(MIX_MODS) + 3)
            act.wait_ge(qk["ssq"], 1)
            act.activation(qk_root(), qk_ssq(), ACT.Sqrt, scale=1.0 / DH, bias=eps[:, 0:1]).then_inc(qk["root"], 1)
            for c in range(MIX_MODS, MIX_MODS + QK_MODS):
                split_to(mod_slot(c) + 3)
                mod_copy(c, 7 * (c % 2))
                split_to(mod_slot(c) + 4)
            load_table(ACT.Exp)
            for i in range(0, 10, 2):
                act.wait_ge(qk["t"], i + 1)
                act.activation(qk_t[:, i, :], ps[:, 1 + i % 6, :], ACT.Copy,
                               scale=SCALE if i % 5 < 4 else 1.0).then_inc(qk["act"], 1)
            attention_act(act, attns[0], even_plan, qkv_p, qkv_pt, mod_copy, split_to, load_bias,
                          lambda: gate(gates[0], f_gate, (0, 1), (2, 0)))
            load_table(ACT.Sqrt)
            split_to(WOUT0_S + 5)
            def mixed_roots(i0, i1):
                resid_roots(resids[0], i1, lambda i: (mixed, i + 1) if i < TILES - 1 else used(WOUT0_S + 3),
                            lambda i: bank_pair(2 * i), i0)

            mixed_roots(0, LAT_TILES)
            norm_roots(norms[1], (0, 1), x_ready=(resids[0]["x"], 0))
            mixed_roots(LAT_TILES, TILES)
            norm_hi(norms[1], (0, 1), f_mod)

            def ffn_gates():
                gate(gates[1], f_gate, (0,), (6,))
                gate(gates[2], f_gate, (1,), (4,))

            swiglu_all(ffns[0], FFA_S, 2, CHUNKS_E, f_silu, f_hth, 0,
                       lambda: norm_roots(norms[2], (2, 3), x_ready=(resids[0]["x"], 2)), ffn_gates,
                       lambda: norm_hi(norms[2], (2, 3), f_mod))
            resid_roots(resids[1], 2, lambda i: used(FFB_S - 1), lambda i: bank_pair(3 + 2 * i))
            swiglu_all(ffns[1], FFB_S, 2, CHUNKS_E, f_silu, f_hth, 0,
                       lambda: norm_roots(norms[3], (0, 1), x_ready=(resids[1]["x"], 0)), None,
                       lambda: norm_hi(norms[3], (0, 1), f_mod))
            ahead[0] = WIN1_S + 2
            resid_roots(resids[2], 2, lambda i: used(WIN1_S - 1), lambda i: bank_pair(3 + 2 * i))
            split_to(WIN1_S + 2)
            norm_roots(norms[3], (2, 3), 2, (resids[2]["x"], 0))
            load_table(ACT.Exp)
            for n in range(6):
                split_to(WIN1_S + 2 * n + 3)
                for b in range(2):
                    act.wait_ge(*used(WIN1_S + 2 * n + 1))
                    src = ps[:, ODD_BANKS[n][b], :]
                    if n < 2:
                        ins = act.activation(o_q[:, 4 * n + b, :], src[:, 0:SEQ], ACT.Copy, scale=SCALE)
                    elif n < 4:
                        ins = act.activation(o_k[:, 4 * (n - 2) + b, :], src, ACT.Copy)
                    else:
                        ins = act.activation(o_v[:, b, (n - 4) * N:(n - 3) * N], src, ACT.Copy)
                    ins.then_inc(gemms[1]["act"], 1)
                if n == 0:
                    norm_hi(norms[3], (2, 3), f_mod, 2)
                if n == 3:
                    act.wait_ge(bias["wrote"], 16)
                    act.wait_ge(norms[3]["lo"], TILES)
                    for u in range(4):
                        load_bias(u)
                split_to(WIN1_S + 2 * n + 4)
            attention_act(act, attns[1], odd_plan, o_p, o_pt, mod_copy, split_to, load_bias,
                          lambda: gate(gates[3], m_gate, (0,), (2,)))
            load_table(ACT.Sqrt)
            split_to(WOUT1_S + 5)
            resid_roots(resids[3], 2, lambda i: (mixed, TILES + i) if i < LAT_TILES - 1 else used(WOUT1_S + 3), lambda i: bank_pair(2 * i))
            norm_roots(norms[4], (0, 1), x_ready=(resids[3]["x"], 0))
            load_table(ACT.Exp)
            act.wait_ge(router["exp"], 1)
            act.activation(gw[:, :, 1:2], gw[:, :, 0:1], ACT.Exp).then_inc(router["ex"], 1)
            norm_hi(norms[4], (0, 1), m_mod, dst=h_hi)

            def ht(i):
                act.wait_ge(gathered, i + 1)
                act.activation(hh[:, :, 0:P], ps[:, 4:6, :].rearrange("p b (k n) -> p (b k) n", n=P), ACT.Copy).then_inc(ht_hi, 1)

            ht(0)
            gate(gates[4], m_gate, (0,), (0,))
            act.wait_ge(acc_added[0], 1)
            act.activation(m_y, m_acc[:, 0, :], ACT.Copy).then_inc(y_copied, 1)
            act.activation(put_t[:].rearrange("p t n -> p (t n)"), m_acc[:, 0, 0:2 * P], ACT.Copy).then_inc(put_t_ready, 1)
            load_table(ACT.Silu)
            act.wait_ge(route_ready, 1)
            n_items = act.value_load(table[0:1, ITEM_COLS:ITEM_COLS + 1], min_val=EXPERTS, max_val=EXPERTS + 3)
            with act.Fori(0, n_items) as i:
                def put_turn():
                    act.wait_ge(put_turned, i + 1)
                    act.activation(put_t[:].rearrange("p t n -> p (t n)"), ps[:, 4, 0:2 * P], ACT.Copy).then_inc(put_t_ready, 1)
                swiglu_all(ffns[2], MOE_S, 1, CHUNKS_O, m_silu, m_hth, i * (ITEM_SLOTS // RAW), after_second=put_turn)
                ht(i + 1)
                act.wait_ge(*used(MOE_S + ITEM_SLOTS - 1, i * (ITEM_SLOTS // RAW)))
                act.activation(m_y, ps[:, 2:4, :].rearrange("p b n -> p (b n)"), ACT.Copy).then_inc(y_copied, 1)
            load_table(ACT.Sqrt)
            resid_roots(resids[4], 2, lambda i: (acc_added[i], n_items + 2), lambda i: m_acc[:, i, :])

        @block.vector
        def _(dve):
            chain = Chain(dve, dve_chain)
            ahead = [0]

            def lo(s, turns=0):
                dve.wait_ge(hi_ready, turns * RAW + s + 1)
                dve.tensor_tensor(wlo[:, s % SPLIT, :], raw[:, s % RAW, :], whi[:, s % SPLIT, :].bitcast(F32),
                                  ALU.subtract).then_inc(lo_ready, 1)

            def split_to(s):
                while ahead[0] <= s:
                    lo(ahead[0])
                    ahead[0] += 1

            def spread_conditioning(count):
                dve.wait_ge(mods["bc_hi"], count)
                v = hh[:, :, 3 * P:4 * P].rearrange("p k (part j n) -> p k part j n", part=2, j=2)
                for j in range(2):
                    ins = dve.tensor_tensor(v[:, :, 1, j], silu_c[:, :, j].unsqueeze(2).to_broadcast([P, KD, COND]),
                                            v[:, :, 0, j].bitcast(F32), ALU.subtract)
                ins.then_inc(mods["bc_lo"], 1)

            def mod_take(c, bank):
                layer, n, m = c // (MODS // 2), c % (MODS // 2), mods
                dve.wait_ge(m["turned"], c + 1)
                src = ps[:, bank, 0:8].rearrange("p (b j) -> p b j", j=2)
                dve.tensor_tensor(mod[:, layer, 4 * n:4 * n + 4, :], src,
                                  vt[:, layer, 4 * n:4 * n + 4].unsqueeze(2).to_broadcast([P, 4, 2]), ALU.add).then_inc(m["taken"], 1)

            def coefficients(layer, i, norm=True, gate=True):
                ready = st[f"coef{layer}"]
                if norm:
                    pre = vt[:, layer, 48 + 16 * i:56 + 16 * i].unsqueeze(2).to_broadcast([P, KD, 2])
                    dve.scalar_tensor_tensor(coef_a[:, layer, i], mod[:, layer, 8 * (1 + 3 * i):8 * (2 + 3 * i)], 1.0, pre,
                                             ALU.add, ALU.mult).then_inc(ready, 1)
                if gate:
                    post = vt[:, layer, 56 + 16 * i:64 + 16 * i].unsqueeze(2).to_broadcast([P, KD, 2])
                    dve.tensor_tensor(coef_g[:, layer, i], mod[:, layer, 8 * (2 + 3 * i):8 * (3 + 3 * i)], post,
                                      ALU.mult).then_inc(ready, 1)

            def norm_parts(m, tiles, layer, which, xn, mod_tile, banks, i0=0, dst=None):
                def scale(i):
                    dve.wait_ge(m["root"], i + 1)
                    chain.add(dve.reciprocal(rstd[:, 4 + i:5 + i], root[:, 4 + i:5 + i]))
                    chain.wait()
                    if i >= 2:
                        dve.wait_ge(m["xt"], i - 1)
                    dve.tensor_scalar(xn[:, i % 2, :], x_tile(tiles[i - i0]), rstd[:, 4 + i:5 + i], None,
                                      ALU.mult).then_inc(m["xn"], 1)

                def modulate(i):
                    j = 0 if tiles[i - i0] < LAT_TILES else 1
                    dve.wait_ge(m["xt"], i + 1)
                    if i >= 2 and dst is None:
                        dve.wait_ge(m["hi"], i - 1)
                        dve.wait_ge(m["lo"], i - 1)
                    for k in range(KD):
                        ins = dve.tensor_scalar(mod_tile[:, i % 2, k, :],
                                                ps[:, banks[i % len(banks)] + k // 4, (k % 4) * P:(k % 4 + 1) * P],
                                                coef_a[:, layer, which, k, j:j + 1], mod[:, layer, 24 * which + k, j:j + 1],
                                                ALU.mult, ALU.add)
                    ins.then_inc(m["t1"], 1)

                def split(i):
                    t = tiles[i - i0]
                    dve.wait_ge(m["hi"], i + 1)
                    if dst is None:
                        dve.tensor_tensor(hl[:, :, t * P:(t + 1) * P], mod_tile[:, i % 2],
                                          hh[:, :, t * P:(t + 1) * P].bitcast(F32), ALU.subtract).then_inc(m["lo"], 1)
                    else:
                        dve.tensor_tensor(dst[1][:, i, :], bank_pair(2 + 2 * i),
                                          dst[0][:, i, :].bitcast(F32), ALU.subtract).then_inc(m["lo"], 1)
                return scale, modulate, split

            def norm_ffn(m, tiles, layer, which, i0=0):
                scale, modulate, split = norm_parts(m, tiles, layer, which, f_tmp, f_mod, (3, 5), i0)

                def scales():
                    for i in range(i0, i0 + 2):
                        scale(i)

                def modulates():
                    for i in range(i0, i0 + 2):
                        modulate(i)
                    for i in range(i0, i0 + 2):
                        split(i)
                return scales, modulates

            def resid(r, tiles, g, y_of, gate_tile, tmp, i0=0):
                for i, t in enumerate(tiles, i0):
                    dve.wait_ge(r["root"], i + 1)
                    chain.add(dve.reciprocal(rstd[:, i:i + 1], root[:, i:i + 1]))
                    chain.wait()
                    j = 0 if t < LAT_TILES else 1
                    dve.wait_ge(*g[j])
                    chain.add(dve.scalar_tensor_tensor(tmp[:, i % 2, :], y_of(i), rstd[:, i:i + 1], gate_tile[:, j, :],
                                                       ALU.mult, ALU.mult))
                    chain.wait()
                    dve.tensor_tensor(x_tile(t), x_tile(t), tmp[:, i % 2, :], ALU.add).then_inc(r["x"], 1)

            def swiglu_body(f, first, m_tiles, silu, h, hth, htl):
                def body(kk, turns, between=None):
                    if kk:
                        lo(first + 3 * kk + 1, turns)
                    lo(first + 3 * kk + 2, turns)
                    dve.wait_ge(f["silu"], turns * 2 + kk + 1)
                    dve.tensor_tensor(h[:], silu[:], ps[:, 0:m_tiles, FFC:N], ALU.mult).then_inc(f["h"], 1)
                    if between is not None:
                        between()
                    lo(first + 3 * kk + 3, turns)
                    dve.wait_ge(f["hi"], turns * 2 + kk + 1)
                    cols = 2 * m_tiles * P
                    dve.tensor_tensor(htl[:, kk % 2].rearrange("p b n -> p (b n)"), ps[:, m_tiles, 0:cols],
                                      hth[:, kk % 2].rearrange("p b n -> p (b n)").bitcast(F32),
                                      ALU.subtract).then_inc(f["lo"], 1)
                return body

            def swiglu_all(f, first, m_tiles, chunks, silu, h, hth, htl, item_turns, after_h=None, after_first=None):
                body = swiglu_body(f, first, m_tiles, silu, h, hth, htl)
                body(0, item_turns, after_h)
                if after_first is not None:
                    after_first()
                body(1, item_turns)
                with dve.Fori(0, (chunks - 2) // 2) as j:
                    body(2, item_turns + j)
                    body(3, item_turns + j)
                if chunks % 2:
                    body(chunks - 1, item_turns)
                lo(first + 3 * chunks + 1, item_turns)

            def attention(s, plan, p, pt):
                pairs = 4 * plan["groups"]
                for at in range(pairs + 6):
                    if at < pairs:
                        g, n = at // 4, nkeys(plan, at // 4)
                        h = 2 * (at % 4)
                        nm = neg_max[:, g % 2, h:h + 2]
                        dve.wait_ge(s["s"], at + 1)
                        if not plan["even"]:
                            dve.wait_ge(bias["pool"], 2 * at + 2)
                            local = ps[:, 2 * (at % 2):2 * (at % 2) + 2, 0:SEQ]
                            chain.add(dve.tensor_tensor(local, local, o_bias[:, 2 * (at % 2):2 * (at % 2) + 2, :], ALU.add))
                            chain.wait()
                        ins = dve.tensor_reduce(nm, ps[:, 2 * (at % 2):2 * (at % 2) + 2, 0:n], AX_X, ALU.max, negate=True)
                        if has_sink(plan, g):
                            chain.add(ins)
                            chain.wait()
                            chain.add(dve.tensor_tensor(nm, nm, neg_sink[:, h:h + 2], ALU.min))
                            chain.wait()
                            ins = dve.tensor_tensor(sink_arg[:, g % 2, h:h + 2], nm, sink[:, h:h + 2], ALU.add)
                        ins.then_inc(s["nm"], 1)
                    if plan["even"] and 2 <= at <= pairs and at % 2 == 0:
                        mod_take(attention_mod(at) - 1, 7)
                    if 1 <= at <= pairs:
                        n = nkeys(plan, (at - 1) // 4)
                        dve.wait_ge(s["t"], at)
                        dve.tensor_copy(buf(pt, (at - 1) % 2, 1)[:, 0:n], ps[:, 5, 0:n]).then_inc(s["ptd"], 1)
                    last = at - 2
                    if last >= 0 and last % 4 == 3 and last < pairs:
                        g = last // 4
                        dve.wait_ge(s["p"], last + 1)
                        total = exp_sum[:, g % 2, :]
                        if has_sink(plan, g):
                            chain.add(dve.tensor_tensor(total, total, sink_exp[:, g % 2, :], ALU.add))
                            chain.wait()
                        chain.add(dve.reciprocal(exp_inv[:, g % 2, :], total))
                        dve.wait_ge(s["o"], g + 1)
                        if g % 2 == 0 and g >= 2:
                            dve.wait_ge(s["ot"], g)
                        chain.wait()
                        dve.tensor_tensor(o_sb[:, (g % 2) * N:(g % 2 + 1) * N].rearrange("p (h d) -> p h d", d=DH),
                                          ps[:, 6, :].rearrange("p (h d) -> p h d", d=DH),
                                          exp_inv[:, g % 2, :].unsqueeze(2).to_broadcast([P, 8, DH]),
                                          ALU.mult).then_inc(s["osb"], 1)
                    for half in range(2):
                        t = turned_out(at, half, pairs)
                        if t is not None:
                            dve.wait_ge(s["oth"], 2 * t + half + 1)
                            dve.tensor_tensor(hl[:, 4 * half:4 * half + 4, t * P:(t + 1) * P],
                                              ps[:, 7, :].rearrange("p (k n) -> p k n", n=P),
                                              hh[:, 4 * half:4 * half + 4, t * P:(t + 1) * P].bitcast(F32),
                                              ALU.subtract).then_inc(s["otl"], 1)
                    if plan["even"] and at < pairs:
                        split_to(mod_slot(MIX_MODS + QK_MODS) + at + 1)
                    if plan["even"] and attention_mod(at) == MODS // 2 + 1 and at % 2 == 1:
                        dve.wait_ge(mods["taken"], MODS // 2)
                        coefficients(0, 0, norm=False)
                        coefficients(0, 1)

            dve.wait_ge(st["silu_c"], 1)
            dve.tensor_copy(vt[:, 0, :], ps[:, 0, 0:80]).then_inc(st["vec"], 1)
            dve.tensor_copy(vt[:, 1, :], ps[:, 0, 96:176]).then_inc(st["vec"], 1)
            dve.wait_ge(st["vec"], 2)
            spread_conditioning(1)
            scale, modulate, split = norm_parts(norms[0], range(TILES), 0, 0, f_tmp, f_mod, (2, 4, 6, 2))
            for i in range(TILES):
                scale(i)
            for c in range(MIX_MODS):
                split_to(mod_slot(c) + 3)
                if c:
                    mod_take(c - 1, (c - 1) % 2)
                split_to(mod_slot(c) + 4)
            mod_take(MIX_MODS - 1, (MIX_MODS - 1) % 2)
            dve.wait_ge(mods["taken"], MIX_MODS)
            coefficients(0, 0, gate=False)
            dve.wait_ge(const_loaded, 16)
            dve.wait_ge(st["coef0"], 1)
            for i in range(TILES):
                modulate(i)
                split(i)
            dve.wait_ge(misc_loaded, 64)
            chain.add(dve.tensor_scalar(neg_sink[:], sink[:], -1.0, None, ALU.mult))
            for n in range(3):
                split_to(WIN0_S + 2 * n + 3)
                for t in range(2, 4):
                    dve.wait_ge(*used(WIN0_S + 2 * n + 1))
                    for dst, src in qkv_parts(n, t):
                        ins = dve.tensor_copy(dst, src)
                    ins.then_inc(gemms[0]["dve"], 1)
                split_to(WIN0_S + 2 * n + 4)
            spread_conditioning(2)
            dve.wait_ge(gemms[0]["act"], 6)
            dve.wait_ge(gemms[0]["dve"], 6)
            for t in range(TILES):
                dve.wait_ge(qk["sq"], t + 1)
                sq = qk_t[:, 2 * t:2 * t + 2, :].rearrange("p a b -> p (a b)")[:, 0:QK_E]
                ins = dve.tensor_reduce(qk_ssq()[:, 10 * t:10 * t + 10], sq.rearrange("p (h d) -> p h d", d=DH), AX_X, ALU.add)
            ins.then_inc(qk["ssq"], 1)
            dve.wait_ge(qk["root"], 1)
            qk_inv = qk_t[:, 9, 128:168]
            chain.add(dve.reciprocal(qk_inv, qk_root()))
            for t in range(TILES):
                if t < TILES - 1:
                    split_to(mod_slot(MIX_MODS + t) + 3)
                v = qkv[:, t, 0:QK_E].rearrange("p (h d) -> p h d", d=DH)
                chain.wait()
                chain.add(dve.tensor_tensor(v, v, qk_inv[:, 10 * t:10 * t + 10].unsqueeze(2).to_broadcast([P, 10, DH]), ALU.mult))
                chain.wait()
                for i, (h0, h1) in enumerate(((0, 8), (8, 10))):
                    gain = qk_gain[:, i, :].unsqueeze(1).to_broadcast([P, h1 - h0, DH])
                    ins = dve.tensor_tensor(v[:, h0:h1], v[:, h0:h1], gain, ALU.mult)
                    if i == 0 or t < LAT_TILES:
                        chain.add(ins)
                    else:
                        ins.then_inc(qk["ready"], 1)
                chain.wait()
                if t < LAT_TILES:
                    rotate(dve, chain, t, 0, rot_a).then_inc(qk["ready"], 1)
                c = MIX_MODS + t
                mod_take(c, 7 * (c % 2))
                split_to(mod_slot(c) + 4)
            for i in range(1, 10, 2):
                dve.wait_ge(qk["t"], i + 1)
                dve.tensor_scalar(qk_t[:, i, :], ps[:, 1 + i % 6, :], SCALE if i % 5 < 4 else 1.0, None,
                                  ALU.mult).then_inc(qk["dve"], 1)
            attention(attns[0], even_plan, qkv_p, qkv_pt)
            dve.wait_ge(mods["taken"], MODS)
            coefficients(1, 0)
            coefficients(1, 1)
            split_to(WOUT0_S + 5)
            resid(resids[0], (0, 1), ((gates[0]["sb"], 1),), lambda i: bank_pair(2 * i), f_gate, f_tmp)
            dve.wait_ge(st["coef0"], 4)
            scale, modulate, split = norm_parts(norms[1], (0, 1), 0, 1, f_tmp, f_mod, (0, 2))
            scale(0)
            scale(1)
            for i in range(2):
                modulate(i)
                split(i)
            resid(resids[0], (2, 3), (None, (gates[0]["sb"], 2)), lambda i: bank_pair(2 * i), f_gate, f_tmp, 2)
            swiglu_all(ffns[0], FFA_S, 2, CHUNKS_E, f_silu, f_h, f_hth, f_htl, 0, *norm_ffn(norms[2], (2, 3), 0, 1))
            resid(resids[1], (0, 1), ((gates[1]["sb"], 1),), lambda i: bank_pair(3 + 2 * i), f_gate, f_tmp)
            dve.wait_ge(st["coef1"], 4)
            swiglu_all(ffns[1], FFB_S, 2, CHUNKS_E, f_silu, f_h, f_hth, f_htl, 0, *norm_ffn(norms[3], (0, 1), 1, 0))
            ahead[0] = WIN1_S + 2
            resid(resids[2], (2, 3), (None, (gates[2]["sb"], 1)), lambda i: bank_pair(3 + 2 * i), f_gate, f_tmp)
            split_to(WIN1_S + 2)
            scales, modulates = norm_ffn(norms[3], (2, 3), 1, 0, 2)
            scales()
            for n in range(6):
                split_to(WIN1_S + 2 * n + 3)
                for b in range(2, 4):
                    dve.wait_ge(*used(WIN1_S + 2 * n + 1))
                    src = ps[:, ODD_BANKS[n][b], :]
                    if n < 2:
                        ins = dve.tensor_scalar(o_q[:, 4 * n + b, :], src[:, 0:SEQ], SCALE, None, ALU.mult)
                    elif n < 4:
                        ins = dve.tensor_copy(o_k[:, 4 * (n - 2) + b, :], src)
                    else:
                        ins = dve.tensor_copy(o_v[:, b, (n - 4) * N:(n - 3) * N], src)
                    ins.then_inc(gemms[1]["dve"], 1)
                if n == 0:
                    modulates()
                split_to(WIN1_S + 2 * n + 4)
            attention(attns[1], odd_plan, o_p, o_pt)
            split_to(WOUT1_S + 5)
            resid(resids[3], (0, 1), ((gates[3]["sb"], 1),), lambda i: bank_pair(2 * i), m_gate, m_tmp)
            scale, modulate, split = norm_parts(norms[4], (0, 1), 1, 1, m_tmp, m_mod, (0, 4), dst=(h_hi, h_lo))
            scale(0)
            scale(1)
            modulate(0)
            modulate(1)

            e8 = const[:, C_E8:C_SEL]
            dve.wait_ge(router["logits"], 2)
            chain.add(dve.tensor_copy(logits[:], ps[:, 6, 0:16].rearrange("p (t e) -> p t e", e=EXPERTS)))
            chain.wait()
            for t in range(2):
                chain.add(dve.max(top[:, t, :], logits[:, t, :]))
            chain.wait()
            for t in range(2):
                chain.add(dve.max_index(top_i[:, t, :], top[:, t, :], logits[:, t, :]))
            dve.tensor_tensor(gw[:, :, 0:1], top[:, :, 1:2], top[:, :, 0:1], ALU.subtract).then_inc(router["exp"], 1)
            chain.wait()
            chain.add(dve.tensor_copy(top_f[:], top_i[:]))
            dve.wait_ge(router["ex"], 1)
            chain.add(dve.tensor_scalar(gw[:, :, 2:3], gw[:, :, 1:2], 1.0, None, ALU.add))
            chain.wait()
            chain.add(dve.reciprocal(gw[:, :, 2:3], gw[:, :, 2:3]))
            chain.wait()
            chain.add(dve.tensor_tensor(gw[:, :, 3:4], gw[:, :, 1:2], gw[:, :, 2:3], ALU.mult))
            for t in range(2):
                chain.add(dve.tensor_scalar(hot[:, t, 0, :], e8, top_f[:, t, 0:1], None, ALU.is_equal))
                chain.wait()
                dve.scalar_tensor_tensor(items[:, 2 + t, 0:EXPERTS], e8, top_f[:, t, 1:2], hot[:, t, 0, :], ALU.is_equal,
                                         ALU.add).then_inc(router["sel"], 1)
                chain.add(dve.tensor_scalar(hot[:, t, 1, :], e8, top_f[:, t, 1:2], gw[:, t, 3:4], ALU.is_equal, ALU.mult))
                chain.wait()
                chain.add(dve.scalar_tensor_tensor(items[:, 4 + t, 0:EXPERTS], hot[:, t, 0, :], gw[:, t, 2:3], hot[:, t, 1, :],
                                                   ALU.mult, ALU.add))
            split(0)
            split(1)
            chain.add(dve.memset(over[:], 0.0))
            dve.wait_ge(router["rank"], 1)
            chain.add(dve.tensor_copy(items[:, 0:2, 0:EXPERTS], ps[:, 6, 16:32].rearrange("p (t e) -> p t e", e=EXPERTS)))
            iota = const[:, C_IOTA:C_TRI]

            def make_pick(i):
                for t in range(2):
                    ins = dve.tensor_scalar(pick[:, t, :], iota, items[:, t, bass.ds(i, 1)], items[:, 2 + t, bass.ds(i, 1)],
                                            ALU.is_equal, ALU.mult)
                    ins.then_inc(pick_ready, 1)

            def ht(i):
                dve.wait_ge(ht_hi, i + 1)
                dve.tensor_copy(hl[:, :, 0:P], ps[:, 6:8, :].rearrange("p b (k n) -> p (b k) n", n=P)).then_inc(ht_lo, 1)

            chain.wait()
            chain.add(dve.tensor_scalar(over[:, 0, 4:12], ps[:, 6, 32:40], float(P), None, ALU.is_gt))
            chain.wait()
            make_pick(0)
            for t in range(2):
                dve.memset(m_acc[:, t, :], 0.0).then_inc(acc_added[t], 1)
            chain.add(dve.tensor_copy(items[:, 6, 0:EXPERTS], e8))
            chain.wait()
            for step in range(3):
                chain.wait()
                d = 1 << step
                chain.add(dve.tensor_tensor(over[:, step + 1, 4:12], over[:, step, 4:12], over[:, step, 4 - d:12 - d], ALU.add))
            for j in range(4):
                chain.wait()
                chain.add(dve.scalar_tensor_tensor(over_hot[:, j, :], over[:, 3, 4:12], float(j + 1), over[:, 0, 4:12],
                                                   ALU.is_equal, ALU.mult))
                chain.wait()
                chain.add(dve.tensor_tensor(over_tmp[:], items[:, :, 0:EXPERTS],
                                            over_hot[:, j, :].unsqueeze(1).to_broadcast([P, 7, EXPERTS]), ALU.mult))
                chain.wait()
                chain.add(dve.tensor_reduce(items[:, :, EXPERTS + j], over_tmp[:], AX_X, ALU.add))
            chain.wait()
            chain.add(dve.tensor_scalar(items[:, 0:2, EXPERTS:ITEM_COLS], items[:, 0:2, EXPERTS:ITEM_COLS], float(P), None,
                                        ALU.subtract))
            chain.add(dve.tensor_copy(table[0:1, 0:ITEM_COLS], items[0:1, 6, :]))
            dve.tensor_scalar(table[0:1, ITEM_COLS:ITEM_COLS + 1], over[0:1, 3, 11:12], float(EXPERTS), None,
                              ALU.add).then_inc(route_ready, 1)
            dve.wait_ge(gathered, 1)
            ht(0)
            chain.wait()
            dve.wait_ge(route_ready, 1)
            n_items = dve.value_load(table[0:1, ITEM_COLS:ITEM_COLS + 1], min_val=EXPERTS, max_val=EXPERTS + 3)

            def add_scattered(i):
                for t in range(2):
                    dve.wait_ge(scattered, i * 2 + t + 1)
                    dve.wait_ge(acc_added[t], i + 1)
                    dve.tensor_tensor(m_acc[:, t, :], m_acc[:, t, :], ps[:, 4 + 2 * t:6 + 2 * t, :].rearrange("p b n -> p (b n)"),
                                      ALU.add).then_inc(acc_added[t], 1)

            with dve.Fori(0, n_items) as i:
                def in_head():
                    add_scattered(i)
                    for t in range(2):
                        dve.tensor_scalar(put[:, t, :], iota, items[:, t, bass.ds(i, 1)], items[:, 4 + t, bass.ds(i, 1)],
                                          ALU.is_equal, ALU.mult).then_inc(put_ready, 1)
                    make_pick(i + 1)
                swiglu_all(ffns[2], MOE_S, 1, CHUNKS_O, m_silu, m_h, m_hth, m_htl, i * (ITEM_SLOTS // RAW), after_first=in_head)
                ht(i + 1)
            add_scattered(n_items)
            resid(resids[4], (0, 1), ((gates[4]["sb"], 1),), lambda i: m_acc[:, i, :], m_gate, m_tmp)

        @block.tensor
        def _(pe):
            def use(s, turns=0):
                pe.wait_ge(lo_ready, turns * RAW + s + 1)

            def product(out, lhs, rhs, start, stop):
                (lh, ll), (rh, rl) = lhs, rhs
                pe.matmul(out, lh, rh, start=start, stop=False)
                pe.matmul(out, ll, rh, start=False, stop=False)
                return pe.matmul(out, lh, rl, start=False, stop=stop)

            def both(s, a0, a1):
                q = s % SPLIT
                return whi[:, q, a0:a1], wlo[:, q, a0:a1]

            def tokens(k, a0, a1):
                return hh[:, k, a0:a1], hl[:, k, a0:a1]

            def mod_rows(c, bank, halves=(0, 1)):
                for half in halves:
                    s = mod_slot(c) + half
                    use(s)
                    for kk in range(4):
                        k = 4 * half + kk
                        high, low = both(s, kk * N, (kk + 1) * N)
                        pe.matmul(ps[:, bank, :], hh[:, k, 3 * P:4 * P], high, start=(k == 0), stop=False)
                        ins = pe.matmul(ps[:, bank, :], hh[:, k, 3 * P:4 * P], low, start=False, stop=(k == KD - 1))
                    ins.then_inc(slot_used, 1)

            def mod_turn(c, bank):
                pe.wait_ge(mods["row"], c + 1)
                for b in range(4):
                    ins = pe.matmul(ps[:, bank, 2 * b:2 * b + 2], mod_row[:, c % 2, b * P:(b + 1) * P],
                                    const[:, C_SEL:C_SEL + 2], start=True, stop=True)
                ins.then_inc(mods["turned"], 1)

            def mod_blocks(c0, c1, banks):
                for c in range(c0, c1 + 1):
                    if c < c1:
                        if c >= c0 + 2:
                            pe.wait_ge(mods["taken"], c - 1)
                        mod_rows(c, banks[c % 2])
                    if c > c0:
                        mod_turn(c - 1, banks[(c - 1) % 2])

            def norm(m, n, banks, xn, i0=0):
                for i in range(i0, i0 + n):
                    pe.wait_ge(m["xn"], i + 1)
                    before = [b for b in range(i) if banks[b % len(banks)] == banks[i % len(banks)]]
                    if before:
                        pe.wait_ge(m["t1"], before[-1] + 1)
                    for k in range(KD):
                        ins = pe.transpose(ps[:, banks[i % len(banks)] + k // 4, (k % 4) * P:(k % 4 + 1) * P],
                                           xn[:, i % 2, k * P:(k + 1) * P], ident)
                    ins.then_inc(m["xt"], 1)

            def broadcast_gate(g, layer, which, streams, bank=6):
                for n, j in enumerate(streams):
                    for k in range(KD):
                        ins = pe.matmul(ps[:, bank - 2 * n + k // 4, (k % 4) * P:(k % 4 + 1) * P],
                                        coef_g[:, layer, which, k, j:j + 1].to_broadcast([P, P]), ident,
                                        start=True, stop=True)
                    ins.then_inc(g["bc"], 1)

            def project(first, chunks, tiles, bank_of, before=None, tile_ready=None, tile_done=None):
                for n in range(chunks):
                    if before is not None:
                        before(n)
                    s = first + 2 * n

                    def tile(t, half):
                        for kk in range(4):
                            k = 4 * half + kk
                            ins = product(ps[:, bank_of(n, t), :], tokens(k, t * P, (t + 1) * P),
                                          both(s + half, kk * N, (kk + 1) * N), k == 0, k == KD - 1)
                        if t == tiles[-1]:
                            ins.then_inc(slot_used, 1)
                        elif tile_done is not None and n == chunks - 1 and half == 1:
                            ins.then_inc(tile_done, 1)

                    if tile_ready is not None and n == 0:
                        use(s + 1)
                        for t in tiles:
                            pe.wait_ge(tile_ready, t + 1)
                            tile(t, 0)
                            tile(t, 1)
                    else:
                        for half in range(2):
                            use(s + half)
                            for t in tiles:
                                tile(t, half)

            def swiglu(f, first, m_tiles, chunks, h, hth, htl, y_bank, item_turns=0, after_first=None, after_second=None,
                       before_last=None, tok0=0, after_turn=None, y_free=None, tile_ready=None):
                def gate_up(kk, turns):
                    s = first + (3 * kk - 1 if kk else 0)

                    def tile(m, half):
                        for k4 in range(4):
                            k = 4 * half + k4
                            ins = product(ps[:, m, :], tokens(k, tok0 + m * P, tok0 + (m + 1) * P),
                                          both(s + half, k4 * N, (k4 + 1) * N), k == 0, k == KD - 1)
                        if m == m_tiles - 1:
                            ins.then_inc(slot_used, 1)

                    if tile_ready is not None and kk == 0:
                        use(s + 1, turns)
                        for m in range(m_tiles):
                            pe.wait_ge(tile_ready, m + 1)
                            tile(m, 0)
                            tile(m, 1)
                    else:
                        for half in range(2):
                            use(s + half, turns)
                            for m in range(m_tiles):
                                tile(m, half)

                def turn(kk, turns):
                    pe.wait_ge(f["h"], turns * 2 + kk + 1)
                    for b in range(2):
                        for m in range(m_tiles):
                            c0 = (b * m_tiles + m) * P
                            ins = pe.transpose(ps[:, m_tiles, c0:c0 + P], h[:, m, b * P:(b + 1) * P], ident)
                    ins.then_inc(f["t"], 1)

                def down(kk, s, turns, start=False, stop=False):
                    use(s, turns)
                    pe.wait_ge(f["hi"], turns * 2 + kk + 1)
                    pe.wait_ge(f["lo"], turns * 2 + kk + 1)
                    for m in range(m_tiles):
                        for nh in range(2):
                            for b in range(2):
                                ins = product(ps[:, y_bank + 2 * m + nh, :],
                                              (hth[:, kk % 2, b, m * P:(m + 1) * P], htl[:, kk % 2, b, m * P:(m + 1) * P]),
                                              both(s, b * D + nh * N, b * D + (nh + 1) * N),
                                              start and b == 0, stop and b == 1)
                    ins.then_inc(slot_used, 1)

                def body(kk, turns):
                    gate_up(kk, turns)
                    if kk == 1 and y_free is not None:
                        pe.wait_ge(*y_free)
                    down(kk - 1, first + 3 * kk + 1, turns, start=(kk == 1))
                    turn(kk, turns)

                gate_up(0, item_turns)
                if after_first is not None:
                    after_first()
                turn(0, item_turns)
                if after_turn is not None:
                    after_turn()
                body(1, item_turns)
                if after_second is not None:
                    after_second()
                with pe.Fori(0, (chunks - 2) // 2) as j:
                    body(2, item_turns + j)
                    body(3, item_turns + j)
                if chunks % 2:
                    body(chunks - 1, item_turns)
                if before_last is not None:
                    before_last()
                down(chunks - 1, first + 3 * chunks - 1, item_turns, stop=True)

            def attention(s, plan, p, pt, gates_of_mix):
                pairs = 4 * plan["groups"]

                def scores(at):
                    g = at // 4
                    if at >= 2:
                        pe.wait_ge(s["p"], at - 1)
                    for i in range(2):
                        h = 2 * (at % 4) + i
                        out = ps[:, 2 * (at % 2) + i, 0:nkeys(plan, g)]
                        t = g // 2
                        if plan["even"]:
                            half, col, key0 = h // 4, 5 * (g % 2), 0 if t < LAT_TILES else SEQ
                            rows = slice(DH * half, DH * (half + 1))
                            masked = g % 2 == 1 and t < LAT_TILES
                            ins = pe.matmul(out, qk_t[rows, col + h % 4, t * P:(t + 1) * P], qk_t[rows, col + 4, key0:N],
                                            start=True, stop=not masked)
                            if masked:
                                c0 = (1 - t) * P
                                ins = pe.matmul(out[:, c0:c0 + P], ident, const[:, C_WIN + t * P:C_WIN + (t + 1) * P],
                                                start=False, stop=True)
                        else:
                            h += 8 * (g % 2)
                            rows = slice(DH * (h % 2), DH * (h % 2 + 1))
                            ins = pe.matmul(out, o_q[rows, h // 2, t * P:(t + 1) * P], o_k[rows, h // 2, :], start=True, stop=True)
                    ins.then_inc(s["s"], 1)

                def turn(at):
                    pe.wait_ge(s["p"], at + 1)
                    if at >= 1:
                        pe.wait_ge(s["pta"], at)
                        pe.wait_ge(s["ptd"], at)
                    for i in range(2):
                        for b in range(nkeys(plan, at // 4) // P):
                            ins = pe.transpose(ps[:, 4 + i, b * P:(b + 1) * P], buf(p, at % 2, i)[:, b * P:(b + 1) * P], ident)
                    ins.then_inc(s["t"], 1)

                def values(at):
                    g = at // 4
                    pe.wait_ge(s["pta"], at + 1)
                    pe.wait_ge(s["ptd"], at + 1)
                    if at % 4 == 0 and g >= 1:
                        pe.wait_ge(s["osb"], g)
                    blocks = nkeys(plan, g) // P
                    for i in range(2):
                        h = 2 * (at % 4) + i
                        for b in range(blocks):
                            tile = TILES - blocks + b
                            if plan["even"]:
                                c0 = GROUP_E * (g % 2) + QK_E + DH * (h // 4)
                                v = qkv[:, tile, c0:c0 + DH]
                            else:
                                v = o_v[:, tile, DH * (h + 8 * (g % 2)):DH * (h + 1 + 8 * (g % 2))]
                            ins = pe.matmul(ps[:, 6, DH * h:DH * (h + 1)], buf(pt, at % 2, i)[:, b * P:(b + 1) * P], v,
                                            start=(b == 0), stop=(b == blocks - 1))
                    if at % 4 == 3:
                        ins.then_inc(s["o"], 1)

                def turn_out(t, half):
                    pe.wait_ge(s["osb"], 2 * t + 2)
                    if 2 * t + half >= 1:
                        pe.wait_ge(s["otl"], 2 * t + half)
                    for k in range(4):
                        c0 = (4 * half + k) * P
                        ins = pe.transpose(ps[:, 7, k * P:(k + 1) * P], o_sb[:, c0:c0 + P], ident)
                    ins.then_inc(s["ot"], 1)

                scores(0)
                outs = 0
                for at in range(pairs + 6):
                    if at + 1 < pairs:
                        scores(at + 1)
                    if plan["even"] and 2 <= at <= pairs and at % 2 == 0:
                        mod_turn(attention_mod(at) - 1, 7)
                    if 1 <= at <= pairs:
                        turn(at - 1)
                    for half in range(2):
                        t = turned_out(at, half, pairs)
                        if t is not None:
                            if plan["even"]:
                                pe.wait_ge(mods["taken"], min(attention_mod(at), MODS))
                            turn_out(t, half)
                            outs += 1
                    if 2 <= at <= pairs + 1:
                        values(at - 2)
                    if at == pairs + 2:
                        pe.wait_ge(s["p"], pairs)
                        gates_of_mix()
                    if plan["even"] and at < pairs:
                        if at % 2 == 0:
                            pe.wait_ge(mods["taken"], attention_mod(at))
                            if outs:
                                pe.wait_ge(s["otl"], outs)
                        mod_rows(attention_mod(at), 7, (at % 2,))
                pe.wait_ge(s["otl"], plan["groups"])

            pe.wait_ge(vec_loaded, 16 * 12)
            pe.wait_ge(const_loaded, 16)
            pe.transpose(ps[:, 0, 0:96], vrow0[:], ident[0:96, 0:96]).then_inc(st["vt"], 1)
            pe.transpose(ps[:, 0, 96:176], vrow1[:], ident[0:80, 0:80]).then_inc(st["vt"], 1)
            pe.wait_ge(st["silu_c"], 1)
            pe.wait_ge(st["vec"], 2)
            norm0_banks = (2, 4, 6, 2)
            norm(norms[0], 3, norm0_banks, f_tmp)
            pe.wait_ge(mods["bc_lo"], 1)
            mod_blocks(0, MIX_MODS, (0, 1))
            norm(norms[0], 1, norm0_banks, f_tmp, 3)

            def banks_free0(n):
                if n >= 2:
                    pe.wait_ge(gemms[0]["act"], 2 * (n - 1))
                    pe.wait_ge(gemms[0]["dve"], 2 * (n - 1))

            project(WIN0_S, 3, range(TILES), lambda n, t: EVEN_BANKS[n % 2][t], banks_free0, norms[0]["lo"])
            pe.wait_ge(mods["bc_lo"], 2)
            mod_blocks(MIX_MODS, MIX_MODS + QK_MODS, (0, 7))
            pe.wait_ge(qk["ready"], TILES)
            pe.wait_ge(qk["pool"], LAT_TILES)
            for i in range(10):
                g, c = i // 5, i % 5
                if i >= 6:
                    pe.wait_ge(qk["dve"] if i % 2 else qk["act"], (i - 6) // 2 + 1)
                for t in range(TILES):
                    src = qkv[:, t, GROUP_E * g + P * c:GROUP_E * g + P * (c + 1)]
                    ins = pe.transpose(ps[:, 1 + i % 6, t * P:(t + 1) * P], src, ident)
                ins.then_inc(qk["t"], 1)
            pe.wait_ge(qk["act"], 5)
            pe.wait_ge(qk["dve"], 5)

            def mix_gates():
                pe.wait_ge(st["coef0"], 4)
                broadcast_gate(gates[0], 0, 0, (0, 1), 2)

            attention(attns[0], even_plan, qkv_p, qkv_pt, mix_gates)
            pe.wait_ge(gates[0]["sb"], 2)
            project(WOUT0_S, 2, range(TILES), lambda n, t: 2 * t + n, tile_done=mixed)
            norm(norms[1], 2, (0, 2), f_tmp)

            def ffn_gates():
                pe.wait_ge(resids[0]["x"], TILES)
                broadcast_gate(gates[1], 0, 1, (0,))
                broadcast_gate(gates[2], 0, 1, (1,), 4)

            def norm_context():
                pe.wait_ge(gates[1]["sb"], 1)
                pe.wait_ge(gates[2]["sb"], 1)
                norm(norms[2], 2, (3, 5), f_tmp)

            swiglu(ffns[0], FFA_S, 2, CHUNKS_E, f_h, f_hth, f_htl, 3, after_first=ffn_gates, after_turn=norm_context,
                   y_free=(norms[2]["t1"], 2), tile_ready=norms[1]["lo"])
            swiglu(ffns[1], FFB_S, 2, CHUNKS_E, f_h, f_hth, f_htl, 3, tok0=SEQ, tile_ready=norms[2]["lo"],
                   after_turn=lambda: norm(norms[3], 2, (3, 5), f_tmp), y_free=(norms[3]["t1"], 2))
            pe.wait_ge(norms[3]["lo"], 2)
            for n in range(6):
                if n == 1:
                    norm(norms[3], 2, (3, 5), f_tmp, 2)
                if n == 2:
                    pe.wait_ge(norms[3]["lo"], TILES)
                before = [m for m in range(n) if ODD_BANKS[m] == ODD_BANKS[n]]
                if before:
                    pe.wait_ge(gemms[1]["act"], 2 * (before[-1] + 1))
                    pe.wait_ge(gemms[1]["dve"], 2 * (before[-1] + 1))
                for half in range(2):
                    s = WIN1_S + 2 * n + half
                    use(s)
                    for b in range(4):
                        for kk in range(4):
                            k = 4 * half + kk
                            out = ps[:, ODD_BANKS[n][b], :]
                            if n < 4:
                                width = SEQ if n < 2 else N
                                ins = product(out[:, 0:width], both(s, kk * N + b * P, kk * N + (b + 1) * P),
                                              tokens(k, 0, width), k == 0, k == KD - 1)
                            else:
                                ins = product(out, tokens(k, b * P, (b + 1) * P), both(s, kk * N, (kk + 1) * N),
                                              k == 0, k == KD - 1)
                    ins.then_inc(slot_used, 1)
            pe.wait_ge(gemms[1]["act"], 12)
            pe.wait_ge(gemms[1]["dve"], 12)
            attention(attns[1], odd_plan, o_p, o_pt, lambda: broadcast_gate(gates[3], 1, 0, (0,), 2))
            pe.wait_ge(gates[3]["sb"], 1)
            project(WOUT1_S, 2, range(LAT_TILES), lambda n, t: 2 * t + n, tile_done=mixed)
            m = norms[4]
            norm(m, 2, (0, 4), m_tmp)
            pe.wait_ge(misc_loaded, 64)
            for i in range(2):
                pe.wait_ge(m["t1"], i + 1)
                for k in range(KD):
                    ins = pe.matmul(ps[:, 6, 8 * i:8 * i + 8], m_mod[:, i, k, :], w_router[:, k, :],
                                    start=(k == 0), stop=(k == KD - 1))
                ins.then_inc(router["logits"], 1)
            for i in range(2):
                for k in range(KD):
                    ins = pe.transpose(ps[:, 2 + 2 * i + k // 4, (k % 4) * P:(k % 4 + 1) * P], m_mod[:, i, k, :], ident)
                ins.then_inc(router["back"], 1)
            pe.wait_ge(router["sel"], 2)
            tri = const[:, C_TRI:C_E8]
            sel = [items[:, 2 + t, 0:EXPERTS] for t in range(2)]
            pe.matmul(ps[:, 6, 16:24], tri, sel[0], start=True, stop=True)
            pe.matmul(ps[:, 6, 24:32], ones[:], sel[0], start=True, stop=False)
            pe.matmul(ps[:, 6, 24:32], tri, sel[1], start=False, stop=True)
            pe.matmul(ps[:, 6, 32:40], ones[:], sel[0], start=True, stop=False)
            pe.matmul(ps[:, 6, 32:40], ones[:], sel[1], start=False, stop=True).then_inc(router["rank"], 1)

            def gather(i):
                pe.wait_ge(pick_ready, i * 2 + 2)
                for part, src in enumerate((h_hi, h_lo)):
                    for k in range(KD):
                        for t in range(2):
                            ins = pe.matmul(ps[:, 4 + 2 * part + k // 4, (k % 4) * P:(k % 4 + 1) * P],
                                            src[:, t, k * P:(k + 1) * P], pick[:, t, :], start=(t == 0), stop=(t == 1))
                ins.then_inc(gathered, 1)

            pe.wait_ge(m["lo"], 2)
            gather(0)
            broadcast_gate(gates[4], 1, 1, (0,), 0)
            pe.wait_ge(gates[4]["sb"], 1)
            pe.wait_ge(route_ready, 1)
            n_items = pe.value_load(table[0:1, ITEM_COLS:ITEM_COLS + 1], min_val=EXPERTS, max_val=EXPERTS + 3)

            def scatter(i):
                pe.wait_ge(y_copied, i + 1)
                pe.wait_ge(put_t_ready, i + 1)
                for t in range(2):
                    for nh in range(2):
                        ins = pe.matmul(ps[:, 4 + 2 * t + nh, :], put_t[:, t, :], m_y[:, nh * N:(nh + 1) * N], start=True, stop=True)
                    ins.then_inc(scattered, 1)

            with pe.Fori(0, n_items) as i:
                pe.wait_ge(ht_hi, i + 1)
                pe.wait_ge(ht_lo, i + 1)

                def turn_put():
                    pe.wait_ge(put_ready, i * 2 + 2)
                    pe.wait_ge(acc_added[0], i + 2)
                    for t in range(2):
                        ins = pe.transpose(ps[:, 4, t * P:(t + 1) * P], put[:, t, :], ident)
                    ins.then_inc(put_turned, 1)

                def gather_next():
                    pe.wait_ge(acc_added[1], i + 2)
                    pe.wait_ge(put_t_ready, i + 2)
                    gather(i + 1)

                swiglu(ffns[2], MOE_S, 1, CHUNKS_O, m_h, m_hth, m_htl, 2, i * (ITEM_SLOTS // RAW),
                       lambda: scatter(i), turn_put, gather_next)
            pe.wait_ge(ht_hi, n_items + 1)
            pe.wait_ge(ht_lo, n_items + 1)
            scatter(n_items)


_INS = ["x", "c", "ctx", "c_ctx", "e_w_mod", "e_b_mod", "e_g_pre_mix", "e_g_post_mix", "e_g_pre_ffn", "e_g_post_ffn",
        "e_w_in", "e_w_out", "e_g_q", "e_g_k", "e_sink", "e_w_gate", "e_w_up", "e_w_down", "o_w_mod", "o_b_mod",
        "o_g_pre_mix", "o_g_post_mix", "o_g_pre_ffn", "o_g_post_ffn", "o_w_in", "o_w_out", "o_rpb", "o_w_router",
        "o_w_gate", "o_w_up", "o_w_down"]


def kernel(**inputs):
    import concourse.bacc as _bacc
    from concourse.bass_utils import run_bass_kernel_spmd as _run

    nc = _bacc.Bacc("TRN2", target_bir_lowering=False, num_devices=1)
    arrays, args = {}, {}
    given = {name: np.ascontiguousarray(inputs[name]) for name in _INS}
    given["constants"] = shape_constants()
    for name, x in given.items():
        arrays[f"in_{name}"] = x
        args[name] = nc.dram_tensor(f"in_{name}", x.shape, mybir.dt.from_np(x.dtype), kind="ExternalInput").ap()
    args["out"] = nc.dram_tensor("out_0", (1, SEQ, D), F32, kind="ExternalOutput").ap()
    build(nc, args)
    r = _run(nc, [arrays], core_ids=[0])
    return r.results[0]["out_0"]
```
